# Optimizing a Trainium2 kernel written in Bass

```python
import math
import jax, jax.numpy as jnp
from jax import lax
import numpy as np

D_MODEL = 1024
BATCH = 1
SEQ = 128
DEPTH = 2
DEC_BATCH = 1
DEC_SEQ = 512
PAST_LEN = 128

GRID_W = 64
Q_BLOCK = 128
EPS = 1e-6
ROPE_THETA = 10000.0
N_MLA = (DEPTH + 1) // 2
N_GQA = DEPTH // 2
MLA_HEADS = 16
MLA_NOPE = 64
MLA_ROPE = 32
MLA_V = 64
Q_LORA = 384
KV_LORA = 256
KV_DIM = KV_LORA + MLA_ROPE
MLA_SCALE = 1.0 / math.sqrt(MLA_NOPE + MLA_ROPE)
GQA_HEADS = 16
GQA_KV_HEADS = 4
GQA_GROUP = GQA_HEADS // GQA_KV_HEADS
GQA_HEAD_DIM = 64
GQA_SCALE = 1.0 / math.sqrt(GQA_HEAD_DIM)
N_GROUPS = 4
EXPERTS_PER_GROUP = 4
N_EXPERTS = N_GROUPS * EXPERTS_PER_GROUP
TOP_K = 2
EXPERT_FF = 256

kernel_name = "hybrid_mla_gqa_hmoe_diffusion_step"

def rms_norm(x, g):
    xf = x.astype(jnp.float32)
    y = xf * lax.rsqrt(jnp.mean(xf * xf, axis=-1, keepdims=True) + EPS)
    return (y * g.astype(jnp.float32)).astype(x.dtype)

def modulate(h, shift, scale):
    return h * (1 + scale[:, None, :]) + shift[:, None, :]

def axial_rope_tables(n_tokens, rot_dim, dtype):
    rows = n_tokens // GRID_W
    t = jnp.arange(rows * GRID_W)
    row = (t // GRID_W).astype(jnp.float32)
    col = (t % GRID_W).astype(jnp.float32)
    axis_dim = rot_dim // 2
    inv = jnp.power(ROPE_THETA, -jnp.arange(0, axis_dim, 2, dtype=jnp.float32) / axis_dim)
    ang = jnp.concatenate([row[:, None] * inv, col[:, None] * inv], axis=-1)
    return jnp.cos(ang).astype(dtype), jnp.sin(ang).astype(dtype)

def apply_rope(x, cos, sin):
    xp = x.reshape(x.shape[:-1] + (x.shape[-1] // 2, 2))
    x0, x1 = xp[..., 0], xp[..., 1]
    c = cos[None, :, None, :]
    s = sin[None, :, None, :]
    return jnp.stack([x0 * c - x1 * s, x0 * s + x1 * c], axis=-1).reshape(x.shape)

def block_attention(q, k, v, scale):
    B, Tq = q.shape[:2]
    nb = Tq // Q_BLOCK
    qb = q.reshape((B, nb, Q_BLOCK) + q.shape[2:]).swapaxes(0, 1)

    def one_block(qblk):
        s = jnp.einsum('bqhgd,bkhd->bhgqk', qblk, k).astype(jnp.float32) * scale
        p = jax.nn.softmax(s, axis=-1).astype(v.dtype)
        return jnp.einsum('bhgqk,bkhe->bqhge', p, v)

    out = lax.map(one_block, qb)
    return out.swapaxes(0, 1).reshape((B, Tq) + out.shape[3:])

def mla_project(h, w_dq, g_q, w_uq, w_dkv, g_kv):
    B, T, _ = h.shape
    q = (rms_norm(h @ w_dq, g_q) @ w_uq).reshape(B, T, MLA_HEADS, MLA_NOPE + MLA_ROPE)
    kv = h @ w_dkv
    c_kv = rms_norm(kv[..., :KV_LORA], g_kv)
    return q[..., :MLA_NOPE], q[..., MLA_NOPE:], c_kv, kv[..., KV_LORA:]

def mla_attend(q_nope, q_pe, keys, w_uk, w_uv, w_o):
    B, T = q_nope.shape[:2]
    q_lat = jnp.einsum('bthn,chn->bthc', q_nope, w_uk)
    q = jnp.concatenate([q_lat, q_pe], axis=-1)[:, :, None]
    k = keys[:, :, None, :]
    v = keys[:, :, None, :KV_LORA]
    o = block_attention(q, k, v, MLA_SCALE)[:, :, 0]
    o = jnp.einsum('bthc,chv->bthv', o, w_uv).reshape(B, T, MLA_HEADS * MLA_V)
    return o @ w_o

def gqa_project(h, w_qkv, g_q, g_k):
    B, T, _ = h.shape
    qkv = h @ w_qkv
    nq = GQA_HEADS * GQA_HEAD_DIM
    nk = GQA_KV_HEADS * GQA_HEAD_DIM
    q = rms_norm(qkv[..., :nq].reshape(B, T, GQA_HEADS, GQA_HEAD_DIM), g_q)
    k = rms_norm(qkv[..., nq:nq + nk].reshape(B, T, GQA_KV_HEADS, GQA_HEAD_DIM), g_k)
    v = qkv[..., nq + nk:].reshape(B, T, GQA_KV_HEADS, GQA_HEAD_DIM)
    return q, k, v

def gqa_attend(q, k, v, w_o):
    B, T = q.shape[:2]
    qg = q.reshape(B, T, GQA_KV_HEADS, GQA_GROUP, GQA_HEAD_DIM)
    o = block_attention(qg, k, v, GQA_SCALE).reshape(B, T, GQA_HEADS * GQA_HEAD_DIM)
    return o @ w_o

def hier_moe(h, w_group, b_group, w_exp, b_exp, w_gate, w_up, w_down):
    B, T, D = h.shape
    xt = h.reshape(B * T, D)
    N = xt.shape[0]
    g_prob = jax.nn.softmax((xt @ w_group).astype(jnp.float32) + b_group.astype(jnp.float32), axis=-1)
    g_w, g_idx = lax.top_k(g_prob, 1)
    e_logits = ((xt @ w_exp).astype(jnp.float32) + b_exp.astype(jnp.float32)).reshape(N, N_GROUPS, EXPERTS_PER_GROUP)
    idx = jnp.broadcast_to(g_idx[:, :, None], (N, 1, EXPERTS_PER_GROUP))
    e_in = jnp.take_along_axis(e_logits, idx, axis=1)[:, 0]
    e_val, e_idx = lax.top_k(e_in, TOP_K)
    e_w = jax.nn.softmax(e_val, axis=-1) * g_w
    expert_id = g_idx * EXPERTS_PER_GROUP + e_idx
    combine = jnp.sum(jax.nn.one_hot(expert_id, N_EXPERTS, dtype=jnp.float32) * e_w[..., None], axis=1)
    hid = jax.nn.silu(jnp.einsum('nd,edf->nef', xt, w_gate)) * jnp.einsum('nd,edf->nef', xt, w_up)
    hid = hid * combine[:, :, None].astype(hid.dtype)
    out = jnp.einsum('nef,efd->nd', hid, w_down)
    return out.reshape(B, T, D)

def setup_inputs(seed: int = 0) -> dict:
    key = jax.random.key(seed)
    ks = iter(jax.random.split(key, 40))
    f32 = jnp.float32
    D = D_MODEL

    def nrm(shape, scale):
        return scale * jax.random.normal(next(ks), shape, f32)

    def gain(shape):
        return 1.0 + 0.05 * jax.random.normal(next(ks), shape, f32)

    return {
        "x_prompt": nrm((BATCH, SEQ, D), 1.0),
        "x_sample": nrm((DEC_BATCH, DEC_SEQ, D), 1.0),
        "cache_mla": nrm((DEC_BATCH, N_MLA, PAST_LEN, KV_DIM), 1.0),
        "cache_gqa": nrm((DEC_BATCH, N_GQA, PAST_LEN, 2, GQA_KV_HEADS, GQA_HEAD_DIM), 1.0),
        "c": nrm((DEC_BATCH, D), 1.0),
        "c_ctx": nrm((D,), 1.0),
        "ada_w": nrm((DEPTH, D, 6 * D), 0.5 * D ** -0.5),
        "ada_b": nrm((DEPTH, 6 * D), 0.01),
        "norm_mix": gain((DEPTH, D)),
        "norm_ffn": gain((DEPTH, D)),
        "mla_w_dq": nrm((N_MLA, D, Q_LORA), D ** -0.5),
        "mla_q_norm": gain((N_MLA, Q_LORA)),
        "mla_w_uq": nrm((N_MLA, Q_LORA, MLA_HEADS * (MLA_NOPE + MLA_ROPE)), Q_LORA ** -0.5),
        "mla_w_dkv": nrm((N_MLA, D, KV_DIM), D ** -0.5),
        "mla_kv_norm": gain((N_MLA, KV_LORA)),
        "mla_w_uk": nrm((N_MLA, KV_LORA, MLA_HEADS, MLA_NOPE), KV_LORA ** -0.5),
        "mla_w_uv": nrm((N_MLA, KV_LORA, MLA_HEADS, MLA_V), KV_LORA ** -0.5),
        "mla_w_o": nrm((N_MLA, MLA_HEADS * MLA_V, D), (MLA_HEADS * MLA_V) ** -0.5),
        "gqa_w_qkv": nrm((N_GQA, D, (GQA_HEADS + 2 * GQA_KV_HEADS) * GQA_HEAD_DIM), D ** -0.5),
        "gqa_q_norm": gain((N_GQA, GQA_HEAD_DIM)),
        "gqa_k_norm": gain((N_GQA, GQA_HEAD_DIM)),
        "gqa_w_o": nrm((N_GQA, GQA_HEADS * GQA_HEAD_DIM, D), (GQA_HEADS * GQA_HEAD_DIM) ** -0.5),
        "moe_w_group": nrm((DEPTH, D, N_GROUPS), D ** -0.5),
        "moe_b_group": nrm((DEPTH, N_GROUPS), 0.01),
        "moe_w_expert": nrm((DEPTH, D, N_EXPERTS), D ** -0.5),
        "moe_b_expert": nrm((DEPTH, N_EXPERTS), 0.01),
        "moe_w_gate": nrm((DEPTH, N_EXPERTS, D, EXPERT_FF), D ** -0.5),
        "moe_w_up": nrm((DEPTH, N_EXPERTS, D, EXPERT_FF), D ** -0.5),
        "moe_w_down": nrm((DEPTH, N_EXPERTS, EXPERT_FF, D), EXPERT_FF ** -0.5),
        "final_norm": gain((D,)),
    }

def reference(x_prompt, x_sample, cache_mla, cache_gqa, c, c_ctx,
              ada_w, ada_b, norm_mix, norm_ffn,
              mla_w_dq, mla_q_norm, mla_w_uq, mla_w_dkv, mla_kv_norm, mla_w_uk, mla_w_uv, mla_w_o,
              gqa_w_qkv, gqa_q_norm, gqa_k_norm, gqa_w_o,
              moe_w_group, moe_b_group, moe_w_expert, moe_b_expert, moe_w_gate, moe_w_up, moe_w_down,
              final_norm):
    n_lat = x_sample.shape[1]
    cos_mla, sin_mla = axial_rope_tables(n_lat, MLA_ROPE, x_sample.dtype)
    cos_gqa, sin_gqa = axial_rope_tables(n_lat, GQA_HEAD_DIM, x_sample.dtype)

    xp, xs = x_prompt, x_sample
    mla_states, gqa_states = [], []
    for l in range(DEPTH):
        j = l // 2
        mod_p = (jax.nn.silu(c_ctx) @ ada_w[l] + ada_b[l])[None]
        mod_s = jax.nn.silu(c) @ ada_w[l] + ada_b[l]
        sh_a_p, sc_a_p, gt_a_p, sh_m_p, sc_m_p, gt_m_p = jnp.split(mod_p, 6, axis=-1)
        sh_a_s, sc_a_s, gt_a_s, sh_m_s, sc_m_s, gt_m_s = jnp.split(mod_s, 6, axis=-1)

        hp = modulate(rms_norm(xp, norm_mix[l]), sh_a_p, sc_a_p)
        hs = modulate(rms_norm(xs, norm_mix[l]), sh_a_s, sc_a_s)
        if l % 2 == 0:
            prm = (mla_w_dq[j], mla_q_norm[j], mla_w_uq[j], mla_w_dkv[j], mla_kv_norm[j])
            qn_p, qpe_p, ckv_p, kpe_p = mla_project(hp, *prm)
            keys_p = jnp.concatenate([ckv_p, kpe_p], axis=-1)
            mix_p = mla_attend(qn_p, qpe_p, keys_p, mla_w_uk[j], mla_w_uv[j], mla_w_o[j])
            mla_states.append(keys_p)
            qn_s, qpe_s, ckv_s, kpe_s = mla_project(hs, *prm)
            qpe_s = apply_rope(qpe_s, cos_mla, sin_mla)
            kpe_s = apply_rope(kpe_s[:, :, None], cos_mla, sin_mla)[:, :, 0]
            keys_s = jnp.concatenate([cache_mla[:, j], jnp.concatenate([ckv_s, kpe_s], axis=-1)], axis=1)
            mix_s = mla_attend(qn_s, qpe_s, keys_s, mla_w_uk[j], mla_w_uv[j], mla_w_o[j])
        else:
            q_p, k_p, v_p = gqa_project(hp, gqa_w_qkv[j], gqa_q_norm[j], gqa_k_norm[j])
            mix_p = gqa_attend(q_p, k_p, v_p, gqa_w_o[j])
            gqa_states.append(jnp.stack([k_p, v_p], axis=2))
            q_s, k_s, v_s = gqa_project(hs, gqa_w_qkv[j], gqa_q_norm[j], gqa_k_norm[j])
            q_s = apply_rope(q_s, cos_gqa, sin_gqa)
            k_s = apply_rope(k_s, cos_gqa, sin_gqa)
            k_all = jnp.concatenate([cache_gqa[:, j, :, 0], k_s], axis=1)
            v_all = jnp.concatenate([cache_gqa[:, j, :, 1], v_s], axis=1)
            mix_s = gqa_attend(q_s, k_all, v_all, gqa_w_o[j])
        xp = xp + gt_a_p[:, None, :] * mix_p
        xs = xs + gt_a_s[:, None, :] * mix_s

        moe_prm = (moe_w_group[l], moe_b_group[l], moe_w_expert[l], moe_b_expert[l],
                   moe_w_gate[l], moe_w_up[l], moe_w_down[l])
        hp = modulate(rms_norm(xp, norm_ffn[l]), sh_m_p, sc_m_p)
        hs = modulate(rms_norm(xs, norm_ffn[l]), sh_m_s, sc_m_s)
        xp = xp + gt_m_p[:, None, :] * hier_moe(hp, *moe_prm)
        xs = xs + gt_m_s[:, None, :] * hier_moe(hs, *moe_prm)

    y_prompt = rms_norm(xp, final_norm)
    y_sample = rms_norm(xs, final_norm)
    new_mla = jnp.stack(mla_states, axis=1)
    new_gqa = jnp.stack(gqa_states, axis=1)
    return (y_prompt, y_sample, new_mla, new_gqa)


_drawn_inputs = setup_inputs


def setup_inputs(seed=0):
    import zlib

    import numpy as np

    out = dict(_drawn_inputs(seed))
    spreads = {}
    factors = {'cache_mla': 4.451,
     'cache_gqa': 5.08,
     'ada_b': 3.662,
     'mla_q_norm': 8.0,
     'gqa_q_norm': 8.0,
     'moe_b_group': 5.744,
     'moe_b_expert': 8.0}
    for name, (base, spread) in spreads.items():
        noise = np.random.default_rng([zlib.crc32(name.encode()), seed]).standard_normal(out[name].shape)
        drawn = base * np.exp(spread * noise) if base else spread * noise
        out[name] = __import__('jax').numpy.asarray(drawn.astype(out[name].dtype))
    for name, factor in factors.items():
        out[name] = (out[name] * factor).astype(out[name].dtype)
    return out
```

```python
from contextlib import ExitStack

import numpy as np
import concourse.bass as bass
from concourse import mybir

F32 = mybir.dt.float32
I32 = mybir.dt.int32
ALU = mybir.AluOpType
ACT = mybir.ActivationFunctionType
AX = mybir.AxisListType
ds = bass.ds

P = 128
D = 1024
KD = D // P
NTILE = 5
LAT = NTILE - 1
NKEYT = 6
KEYS = NKEYT * P
LKEYS = 5 * P
EPS = 1e-6
HEADS = 16
NOPE, ROPE, VD = 64, 32, 64
QD = NOPE + ROPE
QL, KVL = 384, 256
KV = KVL + ROPE
KVH, HD = 4, 64
NG, EPG = 4, 4
NE = NG * EPG
NR = NG + NE
FF = 256
TOK = NTILE * P
PAIRS = 2 * TOK
SLOT_TILES = (PAIRS - NE) // P + NE
GRID_W = 64
BANK = 512
SLOT = 4096
NSLOT = 4
ADA_ITEMS = 12
NQ, NK = HEADS * HD, KVH * HD
SCALE = (QD ** -0.5, HD ** -0.5)
ROUNDS = (SLOT_TILES - 2) // 2
LOOPED = 2 * ROUNDS
MASKED = -3.0e38

C_ID, C_ONE, C_TRI, C_CM = 0, P, 2 * P, 3 * P
C_SM = C_CM + LAT * ROPE
C_CG = C_SM + LAT * ROPE
C_SG = C_CG + LAT * HD
C_R4 = C_SG + LAT * HD
C_TI = C_R4 + NG
C_END = C_TI + SLOT_TILES

VA_ADA, VA_MIX, VA_FFN = 0, 96, 112
VB_COND, VB_QN, VB_END = 0, 16, 19


def bmid(ap, n):
    return ap.unsqueeze(1).broadcast_to([ap.shape[0], n, ap.shape[1]])


def blast(ap, n):
    return ap.unsqueeze(2).broadcast_to([ap.shape[0], ap.shape[1], n])


def split(ap, a):
    return ap.rearrange("p (a b) -> p a b", a=a)


A_HEADS = HEADS * KEYS + NKEYT * D + 3 * TOK
ARENA = A_HEADS + 5632 + QL

R_SH = 0
R_EX = R_SH + NTILE * (NG + 1)
R_W = R_EX + NTILE * (NG + 1)
R_FREE = R_W + 2 * NTILE
R_M = R_FREE + NTILE * (NG + NE + NG + NE + 2 * EPG + 4 + NG + 2 * EPG + 2 * NE)

MATRICES = (("dq", "dkv", "uk", "uv", "uq0", "uq1", "wo0", "wo1"), ("qkv0", "qkv1", "qkv2", "gwo0", "gwo1"))


def program(nc, ctx, A, O):
    def sb(name, cols, dt=F32):
        return ctx.enter_context(nc.sbuf_tensor(name, [P, cols], dt))

    def split_rows(ap):
        return ap.rearrange("p (a b) -> p a b", b=P)

    sems = {}

    def S(name, layer=None):
        key = name if layer is None else f"{name}_{layer}"
        if key not in sems:
            sems[key] = ctx.enter_context(nc.semaphore(key))
        return sems[key]

    const = sb("const", C_END)
    X = sb("X", NTILE * D)
    veca, vecb = sb("veca", P), sb("vecb", P)
    cola, colb = sb("cola", P), sb("colb", VB_END)
    cond = sb("cond", 2 * KD)
    modc = sb("modc", 2 * 96)
    modt = sb("modt", P)
    gate_rows = sb("gate_rows", 2 * D)
    zeros = sb("zeros", P)
    kvn_row, qkn_row = sb("kvn_row", KVL), sb("qkn_row", 2 * HD)
    rbias, rw = sb("rbias", 2 * NR), sb("rw", KD * NR)
    ring = sb("ring", NSLOT * SLOT)
    ssq, rstd, st = sb("ssq", NTILE), sb("rstd", NTILE), sb("st", 2 * NTILE)
    hst, hsum, hinv = sb("hst", HEADS), sb("hsum", HEADS), sb("hinv", HEADS)
    pst = sb("pst", 3 * (HEADS + KVH))
    arena = sb("arena", ARENA)
    expert, slot_i = sb("expert", SLOT_TILES, I32), sb("slot_i", 2 * NTILE, I32)
    ps = ctx.enter_context(nc.psum_tensor("ps", [P, 8 * BANK], F32))

    hs = nc.dram_tensor("slot_rows", (SLOT_TILES * P, D), F32).ap()
    ys = nc.dram_tensor("slot_out", (SLOT_TILES * P, D), F32).ap()
    modrow = [nc.dram_tensor(f"mod_rows{l}", (2, 6, D), F32).ap() for l in range(2)]

    ident, ones, tri = const[:, C_ID:C_ID + P], const[:, C_ONE:C_ONE + P], const[:, C_TRI:C_TRI + P]

    def bank(b, n=BANK, at=0):
        return ps[:, b * BANK + at:b * BANK + at + n]

    def ar(at, n):
        return arena[:, at:at + n]

    def xt(t):
        return X[:, ds(t * D, D)]

    m_kT, m_V, m_qlT = ar(0, HEADS * KEYS), ar(HEADS * KEYS, NKEYT * D), ar(A_HEADS - 3 * TOK, 3 * TOK)
    qT, Pb, PT = ar(A_HEADS, HEADS * P), ar(A_HEADS + 2048, 2 * LKEYS), ar(A_HEADS + 3328, 2 * LKEYS)
    o_tok, oT, qls = ar(A_HEADS + 4608, D), Pb[:, 0:D], ar(A_HEADS + 5632, QL)
    q_tok, q_cos, q_sin = ar(A_HEADS + 2048, HEADS * QD), ar(A_HEADS + 3584, 512), ar(A_HEADS + 4096, 512)
    m_ckvT, m_krT = ar(A_HEADS, 2 * KEYS), ar(A_HEADS + 2 * KEYS, KEYS)
    m_ql, m_key = ar(4 * D, 2 * QL), ar(5 * D, NKEYT * KV)
    m_junk, m_rope = ar(7 * D, D), ar(8 * D, 2 * ROPE)
    g_kT, g_V, g_qT = ar(0, KVH * KEYS), ar(3072, NKEYT * NK), ar(4608, 8 * TOK)
    g_qk, g_cache = ar(13824, 2 * (NQ + NK)), ar(18944, NK)
    g_a, g_b, g_junk = ar(16384, NQ + NK), ar(17664, NQ + NK), ar(19200, D)
    e_row, e_h, e_hT = ar(0, 4 * D), ar(4 * D, NTILE * D), ar(9 * D, 2 * D)
    e_junk, e_r = ar(11 * D, D), ar(12 * D, 1600)
    e_xs, e_xsT = ar(14000, 2 * D), ar(16048, 2 * D)
    e_sil, e_hid, e_hidT, e_y = ar(18096, 2 * FF), ar(18608, 2 * FF), ar(19120, 2 * FF), ar(19632, 2 * D)
    e_g = ar(4 * D, 4 * D)
    xn = [lambda t, o=o: ar(o + (t % 2) * D, D) for o in (0, 9728)]
    hT = [lambda t, o=o: ar(o + (2 + t % 2) * D, D) for o in (0, 9728)]

    def pbuf(h, n):
        return Pb[:, (h % 2) * LKEYS:(h % 2) * LKEYS + n]

    def ptbuf(h, n):
        return PT[:, (h % 2) * LKEYS:(h % 2) * LKEYS + n]

    def spair(h, n):
        return ps[:, (h % 2) * 2 * BANK:(h % 2) * 2 * BANK + n]

    place, uses, order = {}, [0] * NSLOT, []

    def item(name):
        s = len(order) % NSLOT
        uses[s] += 1
        place[name] = (s, 32 * uses[s], len(order))
        order.append(name)

    def use_of(n):
        kind, l, t = order[n]
        if kind in ("gu", "dn"):
            return S("gu_done" if kind == "gu" else "y_done", l), t + 1
        return S("ring_used"), sum(x[0] not in ("gu", "dn") for x in order[:n + 1])

    for l in range(2):
        for n in range(ADA_ITEMS):
            item(("ada", l, n))
        for n in MATRICES[l]:
            item((n, l, 0))
        for n in range(-len(order) % NSLOT):
            item(("pad", l, n))
        item(("gu", l, 0))
        for t in range(SLOT_TILES):
            if t + 1 < SLOT_TILES:
                item(("gu", l, t + 1))
            item(("dn", l, t))
        for n in range(-len(order) % NSLOT):
            item(("pad", 2 + l, n))

    def slot_of(name, cols):
        s = place[name][0]
        return ring[:, s * SLOT:s * SLOT + cols]

    def wait_landed(pe, name, more=0):
        s, v, _ = place[name]
        pe.wait_ge(S(f"ring_landed{s}"), more + v)

    def tiles_before(l, it):
        return it + NTILE * l

    def meet(eng, n):
        eng.drain().then_inc(S("phase_over"), 1)
        eng.wait_ge(S("phase_over"), 4 * (n + 1))

    rows_of = {"dq": A["mla_w_dq"][0], "dkv": A["mla_w_dkv"][0], "uk": A["mla_w_uk"], "uv": A["mla_w_uv"],
               "uq": A["mla_w_uq"][0], "wo": A["mla_w_o"][0], "qkv": A["gqa_w_qkv"][0], "gwo": A["gqa_w_o"][0]}
    cols_of = {"dq": (QL, 0), "dkv": (KV, 0), "uk": (D, 0), "uv": (D, 0), "uq0": (768, 0), "uq1": (768, 768)}
    for n in (*MATRICES[0], *MATRICES[1]):
        cols_of.setdefault(n, (BANK, BANK * int(n[-1]) if n[-1].isdigit() else 0))

    inputs = [(const[:], A["const"]), (veca[:], A["vec_a"]), (vecb[0:VB_END, :], A["vec_b"]),
              (X[:, 0:D], A["x_prompt"][0]), (split(X[:, D:], LAT), A["x_sample"][0].rearrange("(t p) n -> p t n", p=P)),
              (m_key[:, 0:KV], A["cache_mla"][0, 0]),
              (kvn_row[:], A["mla_kv_norm"][0:1, :].broadcast_to([P, KVL])),
              (qkn_row[:, 0:HD], A["gqa_q_norm"][0:1, :].broadcast_to([P, HD])),
              (qkn_row[:, HD:2 * HD], A["gqa_k_norm"][0:1, :].broadcast_to([P, HD]))]
    for l in range(2):
        inputs.append((rbias[:, l * NR:l * NR + NG], A["moe_b_group"][l:l + 1, :].broadcast_to([P, NG])))
        inputs.append((rbias[:, l * NR + NG:(l + 1) * NR], A["moe_b_expert"][l:l + 1, :].broadcast_to([P, NE])))

    block = ctx.enter_context(nc.Block())

    @block.sync
    def _(sp):
        def free(n):
            if n >= NSLOT:
                sp.wait_ge(*use_of(n - NSLOT))

        def load(name, src, cols, off):
            s, _, n = place[name]
            free(n)
            kk = src.shape[0] // P
            w = split(ring[:, s * SLOT:s * SLOT + kk * cols], kk)
            src = src.rearrange("(k p) n -> p k n", p=P)
            ha = (kk + 1) // 2
            sp.dma_start(w[:, 0:ha], src[:, 0:ha, off:off + cols]).then_inc(S(f"ring_landed{s}"), 16)
            sp.dma_start(w[:, ha:kk], src[:, ha:kk, off:off + cols]).then_inc(S(f"ring_landed{s}"), 16)

        def load_gu(l, t, e):
            s = place[("gu", l, t)][0]
            w = split(ring[:, s * SLOT:(s + 1) * SLOT], KD)
            for m, name in enumerate(("moe_w_gate", "moe_w_up")):
                src = A[name][l][ds(e, 1)].rearrange("e (k p) n -> p (e k) n", p=P)
                sp.dma_start(w[:, :, m * FF:(m + 1) * FF], src).then_inc(S(f"ring_landed{s}"), 16)

        def load_dn(l, t, e):
            s = place[("dn", l, t)][0]
            w = split(ring[:, s * SLOT:s * SLOT + 2 * D], 2)
            src = A["moe_w_down"][l][ds(e, 1)].rearrange("e (k p) n -> p (e k) n", p=P)
            for k in range(2):
                sp.dma_start(w[:, k:k + 1], src[:, k:k + 1]).then_inc(S(f"ring_landed{s}"), 16)

        def load_rows(l, t, u, used=None):
            if used is not None:
                sp.wait_ge(S("xs_used", l), used)
            sp.dma_start(e_xs[:, (u % 2) * D:(u % 2 + 1) * D], hs[ds(t * P, P), :]).then_inc(S(f"xs_landed{u % 2}", l), 16)

        def expert_of(t):
            return sp.value_load(expert[0:1, ds(t, 1)], min_val=0, max_val=NE - 1)

        def pads(l):
            for name in order:
                if name[0] == "pad" and name[1] == l:
                    s, _, n = place[name]
                    free(n)
                    sp.nop().then_inc(S(f"ring_landed{s}"), 32)

        for l in range(2):
            for n in range(ADA_ITEMS):
                load(("ada", l, n), A["ada_w"][l], BANK, n * BANK)
            for n in MATRICES[l]:
                load((n, l, 0), rows_of[n.rstrip("012")], *cols_of[n])
            pads(l)
            sp.wait_ge(S("routed", l), 1)
            sp.wait_ge(S("rows_scattered", l), 16 * 2 * NTILE)
            load_rows(l, 0, 0)
            load_rows(l, 1, 1)
            load_gu(l, 0, expert_of(0))

            def turn(t, u):
                e, e_next = expert_of(t), expert_of(t + 1)
                if u:
                    sp.wait_ge(S("gu_done", l), t)
                load_gu(l, u + 1, e_next)
                if u + 2 < SLOT_TILES:
                    load_rows(l, t + 2, u, t + 1)
                if u >= 2:
                    sp.wait_ge(S("y_done", l), t - 1)
                load_dn(l, u, e)

            for t in range(2):
                turn(t, t)
            with sp.Fori(1, ROUNDS) as i:
                for u in range(2):
                    turn(i * 2 + u, u + 2)
            for t in range(LOOPED, SLOT_TILES - 1):
                turn(t, t)
            e = expert_of(SLOT_TILES - 1)
            sp.wait_ge(S("y_done", l), SLOT_TILES - 2)
            load_dn(l, SLOT_TILES - 1, e)
            pads(2 + l)
        for t in range(NTILE):
            sp.wait_ge(S("y_ready"), t + 1)
            dst = O[0][0] if t == 0 else O[1][0, (t - 1) * P:t * P, :]
            sp.dma_start(dst, e_h[:, t * D:(t + 1) * D]).then_inc(S("results_stored"), 16)
        sp.wait_ge(S("results_stored"), 16 * NTILE)

    @block.gpsimd
    def _(pool):
        pool.memset(zeros[:], 0.0).then_inc(S("zero_made"), 1)
        pool.wait_ge(S("zero_made"), 1)
        pool.wait_ge(S("ada_done", 0), 1)
        for t in range(SLOT_TILES):
            pool.dma_start(split_rows(hs[t * P:(t + 1) * P, :]), bmid(zeros[:], KD)).then_inc(S("table_zeroed"), 16)
        pool.wait_ge(S("table_zeroed"), 16 * SLOT_TILES)
        pool.wait_ge(S("turned_out", 0), NKEYT)
        pool.wait_ge(S("state_stored", 0), 16)
        nc.gpsimd.tensor_copy(split(m_kT[64:96, :], HEADS), bmid(m_krT[64:96, :], HEADS)).then_inc(S("rope_keys"), 1)
        for l in range(2):
            meet(pool, 2 * l)
            pool.wait_ge(S("routed", l), 1)
            for t in range(NTILE):
                for c in range(2):
                    pool.indirect_dma_start(
                        hs, bass.IndirectOffsetOnAxis(ap=slot_i[:, 2 * t + c:2 * t + c + 1], axis=0),
                        e_h[:, t * D:(t + 1) * D], None).then_inc(S("rows_scattered", l), 16)
            pool.wait_ge(S("rows_scattered", l), 16 * 2 * NTILE)
            pool.wait_ge(S("y_stored0", l), 16 * ((SLOT_TILES + 1) // 2 + 1))
            pool.wait_ge(S("y_stored1", l), 16 * (SLOT_TILES // 2 + 1))
            for t in range(NTILE):
                if t >= 2:
                    pool.wait_ge(S("combined", l), t - 1)
                for c in range(2):
                    pool.indirect_dma_start(
                        e_g[:, (2 * (t % 2) + c) * D:(2 * (t % 2) + c + 1) * D], None, ys,
                        bass.IndirectOffsetOnAxis(ap=slot_i[:, 2 * t + c:2 * t + c + 1], axis=0))\
                        .then_inc(S(f"gathered{t % 2}", l), 16)
            meet(pool, 2 * l + 1)

    @block.scalar
    def _(act):
        for dst, src in inputs:
            act.dma_start(dst, src).then_inc(S("inputs"), 16)
        act.wait_ge(S("cols_ready"), 1)
        act.activation(cond[:], colb[:, VB_COND:VB_COND + 2 * KD], ACT.Silu).then_inc(S("cond_ready"), 1)

        def squares(name, junk):
            for t in range(NTILE):
                act.activation(junk, xt(t), ACT.Square, accum_out=ssq[:, t:t + 1]).then_inc(S(f"{name}_squared"), 1)
                act.drain()
            act.wait_ge(S(f"{name}_mean"), 1)
            act.activation(st[:, NTILE:], st[:, 0:NTILE], ACT.Sqrt).then_inc(S(f"{name}_root"), 1)

        def mod_store(l):
            act.wait_ge(S("mod_turned_out", l), 1)
            act.dma_start(modrow[l].rearrange("v c (k p) -> (v c k) p", p=P), modt[0:96, :]).then_inc(S("mod_stored", l), 16)
            act.wait_ge(S("mod_stored", l), 16)
            for v in range(2):
                act.dma_start(gate_rows[:, v * D:(v + 1) * D], modrow[l][v, 2:3, :].broadcast_to([P, D]))\
                    .then_inc(S("gates_a", l), 16)

        def heads(l, it, keys):
            past = tiles_before(l, it)
            for h in range(HEADS):
                act.wait_ge(S("max_ready"), past * HEADS + h + 1)
                if h >= 2:
                    act.wait_ge(S("p_turned"), past * HEADS + h - 1)
                act.activation(pbuf(h, keys), spair(h, keys), ACT.Exp, bias=hst[:, h:h + 1],
                               accum_out=hsum[:, h:h + 1]).then_inc(S("exp_ready"), 1)
            act.wait_ge(S("o_turned"), past + 1)
            act.activation(oT[:, BANK:D], bank(5), ACT.Copy).then_inc(S("oT_ready"), 1)

        def experts(l):
            for v in range(2):
                act.dma_start(gate_rows[:, v * D:(v + 1) * D], modrow[l][v, 5:6, :].broadcast_to([P, D]))\
                    .then_inc(S("rows_e", l), 16)
                for n, c in ((0, 4), (1, 3)):
                    act.dma_start(e_row[:, (2 * v + n) * D:(2 * v + n + 1) * D], modrow[l][v, c:c + 1, :].broadcast_to([P, D]))\
                        .then_inc(S("rows_e", l), 16)
            act.dma_start(split(rw[:], KD)[:, :, 0:NG], A["moe_w_group"][l].rearrange("(k p) n -> p k n", p=P))\
                .then_inc(S("router_landed", l), 16)
            act.dma_start(split(rw[:], KD)[:, :, NG:NR], A["moe_w_expert"][l].rearrange("(k p) n -> p k n", p=P))\
                .then_inc(S("router_landed", l), 16)
            squares(f"ffn{l}", e_junk)
            for t in range(NTILE):
                act.wait_ge(S("h_turned", l), t + 1)
                if t >= 2:
                    act.wait_ge(S("logits", l), t - 1)
                act.activation(e_hT[:, (t % 2) * D:(t % 2 + 1) * D], ps[:, 0:D], ACT.Copy).then_inc(S("hT_out", l), 1)
            act.wait_ge(S("shifted", l), 1)
            act.activation(r_ex, r_sh, ACT.Exp).then_inc(S("r_exp", l), 1)

            def sil(t, u):
                act.wait_ge(S("gu_done", l), t + 1)
                act.activation(e_sil[:, (u % 2) * FF:(u % 2 + 1) * FF], bank(2 + u % 2, FF), ACT.Silu).then_inc(S("sil_ready", l), 1)

            def y_out(t, u, r):
                act.wait_ge(S("y_done", l), t + 1)
                act.wait_ge(S(f"y_stored{u % 2}", l), r * 16 + 16)
                y = e_y[:, (u % 2) * D:(u % 2 + 1) * D]
                act.activation(y, ps[:, 6 * BANK:8 * BANK], ACT.Copy).then_inc(S("y_out", l), 1)
                act.wait_ge(S("y_out", l), t + 2)
                act.dma_start(ys[ds(t * P, P), :], y).then_inc(S(f"y_stored{u % 2}", l), 16)

            act.drain().then_inc(S("y_out", l), 1)
            for b in range(2):
                act.drain().then_inc(S(f"y_stored{b}", l), 16)
            sil(0, 0)
            with act.Fori(0, ROUNDS) as i:
                for u in range(2):
                    sil(i * 2 + (u + 1), u + 1)
                    y_out(i * 2 + u, u, i)
            for t in range(LOOPED, SLOT_TILES):
                if t + 1 < SLOT_TILES:
                    sil(t + 1, t + 1)
                y_out(t, t, t // 2)

        r_sh, r_ex = e_r[:, R_SH:R_SH + NTILE * (NG + 1)], e_r[:, R_EX:R_EX + NTILE * (NG + 1)]

        act.wait_ge(S("inputs"), 16 * len(inputs))
        squares("mix0", m_junk)

        def turned_m(t):
            j = t if t > 0 else 5 if t == 0 else 0
            act.wait_ge(S("turned", 0), t + 2)
            if t >= 0:
                for m in range(3):
                    act.activation(m_qlT[:, m * TOK + t * P:m * TOK + (t + 1) * P], bank(4, P, m * P), ACT.Identity,
                                   scale=colb[:, VB_QN + m:VB_QN + m + 1])
            act.activation(split(m_ckvT, 2)[:, :, j * P:(j + 1) * P], split(bank(5, 2 * P), 2), ACT.Copy)
            act.activation(m_krT[64:96, j * P:(j + 1) * P], ps[0:ROPE, 5 * BANK + 2 * P:5 * BANK + 3 * P], ACT.Copy)\
                .then_inc(S("turned_out", 0), 1)

        turned_m(-1)
        for t in range(NTILE):
            act.wait_ge(S("projected", 0), t + 1)
            act.activation(m_junk[:, 0:QL], bank(2, QL), ACT.Square, accum_out=pst[:, 0:1])
            act.activation(m_junk[:, QL:QL + KVL], bank(3, KVL), ACT.Square, accum_out=pst[:, 1:2]).then_inc(S("proj_squared", 0), 1)
            act.wait_ge(S("proj_mean", 0), t + 1)
            act.activation(pst[:, 4:6], pst[:, 2:4], ACT.Sqrt).then_inc(S("proj_root", 0), 1)
            if t == 0:
                act.wait_ge(S("proj_out", 0), 1)
                act.dma_start(O[2][0, 0], m_key[:, 5 * KV:6 * KV]).then_inc(S("state_stored", 0), 16)
            else:
                turned_m(t - 1)
        turned_m(NTILE - 1)
        mod_store(0)
        act.wait_ge(S("state_stored", 0), 16)
        for m in range(HEADS // 2):
            act.wait_ge(S("k_made"), m + 1)
            act.activation(m_kT[0:64, 2 * m * KEYS:(2 * m + 1) * KEYS], spair(m, KEYS)[0:64], ACT.Copy).then_inc(S("k_even"), 1)
        for j in range(0, NKEYT, 2):
            act.wait_ge(S("v_made"), j + 1)
            act.activation(m_V[:, j * D:(j + 1) * D], ps[:, 4 * BANK:6 * BANK], ACT.Copy).then_inc(S("v_even"), 1)
        act.wait_ge(S("rope_keys"), 1)

        def m_tile(it, keys):
            act.activation(split(qls, 3), split(m_qlT, 3)[:, :, ds(it * P, P)], ACT.Copy).then_inc(S("ql_ready"), 1)
            act.wait_ge(S("q_made"), it + 1)
            act.activation(split(q_tok, 4), split(ps[:, 0:4 * BANK], 4)[:, :, 0:4 * QD], ACT.Copy, scale=SCALE[0])\
                .then_inc(S("q_out"), 1)
            act.wait_ge(S("q_turned"), it + 1)
            act.activation(qT[0:QD, 0:D], ps[0:QD, 0:D], ACT.Copy).then_inc(S("q_ready", 0), 1)
            heads(0, it, keys)

        m_tile(0, P)
        with act.Fori(0, LAT) as i:
            m_tile(i + 1, LKEYS)
        meet(act, 0)
        experts(0)
        meet(act, 1)

        act.dma_start(g_V[:, 0:NK], A["cache_gqa"][0, 0, :, 1].rearrange("t h d -> t (h d)")).then_inc(S("cache_landed"), 16)
        act.dma_start(g_cache, A["cache_gqa"][0, 0, :, 0].rearrange("t h d -> t (h d)")).then_inc(S("cache_landed"), 16)
        mod_store(1)
        squares("mix1", g_junk)

        def turned_g(t):
            j = t if t > 0 else 5 if t == 0 else 0
            act.wait_ge(S("turned", 1), t + 2)
            if t >= 0:
                act.activation(split(g_qT, 8)[:, :, t * P:(t + 1) * P], split(ps[:, 5 * BANK:7 * BANK], 8), ACT.Copy,
                               scale=SCALE[1])
            for half in range(2):
                last = act.activation(split(g_kT[half * HD:(half + 1) * HD, :], KVH)[:, :, j * P:(j + 1) * P],
                                      split(bank(7)[0:HD, :], KVH), ACT.Copy)
            last.then_inc(S("turned_out", 1), 1)

        turned_g(-1)
        for t in range(NTILE):
            act.wait_ge(S("projected", 1), t + 1)
            if t >= 2:
                act.wait_ge(S("turned", 1), t)
            act.activation(g_qk[:, (t % 2) * (NQ + NK):(t % 2 + 1) * (NQ + NK)], ps[:, 2 * BANK:2 * BANK + NQ + NK], ACT.Copy)
            j = t if t > 0 else 5
            act.activation(g_V[:, j * NK:(j + 1) * NK], bank(4, NK, NK), ACT.Copy).then_inc(S("proj_out", 1), 1)
            act.wait_ge(S("proj_mean", 1), t + 1)
            act.activation(pst[:, 40:60], pst[:, 20:40], ACT.Sqrt).then_inc(S("proj_root", 1), 1)
            if t == 0:
                act.wait_ge(S("qk_ready"), 1)
                act.dma_start(O[3][0, 0, :, 0].rearrange("t h d -> t (h d)"), g_qk[:, NQ:NQ + NK]).then_inc(S("state_stored", 1), 16)
                act.wait_ge(S("proj_out", 1), 1)
                act.dma_start(O[3][0, 0, :, 1].rearrange("t h d -> t (h d)"), g_V[:, 5 * NK:6 * NK]).then_inc(S("state_stored", 1), 16)
            else:
                turned_g(t - 1)
                if t == 1:
                    act.wait_ge(S("state_stored", 1), 32)
        turned_g(NTILE - 1)

        def g_tile(it, keys):
            act.wait_ge(S("turned_out", 1), NKEYT)
            act.activation(split(qT[:, 0:D], 8), split(g_qT, 8)[:, :, ds(it * P, P)], ACT.Copy).then_inc(S("q_ready", 1), 1)
            heads(1, it, keys)

        g_tile(0, P)
        with act.Fori(0, LAT) as i:
            g_tile(i + 1, LKEYS)
        meet(act, 2)
        experts(1)
        meet(act, 3)
        act.dma_start(e_row[:, 0:D], A["final_norm"].unsqueeze(0).broadcast_to([P, D])).then_inc(S("final_landed"), 16)
        squares("end", e_junk)

    @block.vector
    def _(dve):
        def settle():
            dve.drain()

        dve.wait_ge(S("cols_turned"), 1)
        nc.vector.tensor_copy(cola[:], bank(7, P))
        nc.vector.tensor_copy(colb[:], bank(7, VB_END, P)).then_inc(S("cols_ready"), 1)

        def modulation(l):
            mc = modc[:, 96 * l:96 * (l + 1)]
            settle()
            dve.wait_ge(S("ada_done", l), 1)
            nc.vector.tensor_tensor(split(mc, 2), bank(7, 96).rearrange("p (m v) -> p v m", v=2),
                                    bmid(cola[:, VA_ADA + 48 * l:VA_ADA + 48 * (l + 1)], 2), ALU.add)
            settle()
            for c, g in ((1, VA_MIX), (4, VA_FFN)):
                part = mc.rearrange("p (v c k) -> p v c k", v=2, c=6)[:, :, c]
                last = nc.vector.scalar_tensor_tensor(part, part, 1.0, bmid(cola[:, g + KD * l:g + KD * (l + 1)], 2),
                                                      ALU.add, ALU.mult)
            last.then_inc(S("mod_ready", l), 1)
            dve.wait_ge(S("mod_turned", l), 1)
            if l:
                dve.wait_ge(S("mod_stored", 0), 16)
            nc.vector.tensor_copy(modt[0:96, :], ps[0:96, 6 * BANK:6 * BANK + P]).then_inc(S("mod_turned_out", l), 1)
            settle()

        def row_stats(name):
            dve.wait_ge(S(f"{name}_squared"), NTILE)
            nc.vector.tensor_scalar(st[:, 0:NTILE], ssq[:], 1.0 / D, EPS, ALU.mult, ALU.add).then_inc(S(f"{name}_mean"), 1)
            dve.wait_ge(S(f"{name}_root"), 1)
            nc.vector.reciprocal(rstd[:], st[:, NTILE:])
            settle()

        def norm(l, t):
            if t >= 2:
                dve.wait_ge(S("n_turned", l), t - 1)
            nc.vector.tensor_scalar(xn[l](t), xt(t), rstd[:, t:t + 1], None, ALU.mult).then_inc(S("xn_ready", l), 1)

        def mod_cols(l, t):
            v = 0 if t == 0 else 1
            dve.wait_ge(S("n_turned", l), t + 1)
            if t >= 2:
                dve.wait_ge(S("projected", l), t - 1)
            for k in range(KD):
                at = 96 * l + 48 * v + k
                last = nc.vector.tensor_scalar(hT[l](t)[:, k * P:(k + 1) * P], ps[:, k * P:(k + 1) * P],
                                               modc[:, at + 8:at + 9], modc[:, at:at + 1], ALU.mult, ALU.add)
            last.then_inc(S("hT_ready", l), 1)

        def rope(out0, out1, cs, sn):
            nc.vector.tensor_tensor(out0, cs[..., 0], sn[..., 1], ALU.subtract)
            return nc.vector.tensor_tensor(out1, sn[..., 0], cs[..., 1], ALU.add)

        def heads(l, it, keys):
            past = tiles_before(l, it)
            for h in range(HEADS + 2):
                if h < HEADS:
                    dve.wait_ge(S("scored"), past * HEADS + h + 1)
                    nc.vector.tensor_reduce(hst[:, h:h + 1], spair(h, keys), AX.X, ALU.max, negate=True)\
                        .then_inc(S("max_ready"), 1)
                if h >= 2:
                    j = h - 2
                    dve.wait_ge(S("p_turned"), past * HEADS + j + 1)
                    if j >= 2:
                        dve.wait_ge(S("pv_done"), past * HEADS + j - 1)
                    nc.vector.tensor_copy(ptbuf(j, keys), ps[:, 4 * BANK:4 * BANK + keys]).then_inc(S("pt_ready"), 1)
                if h in (11, HEADS + 1):
                    o = 0 if h == 11 else 8
                    dve.wait_ge(S("pv_done"), past * HEADS + o + 8)
                    nc.vector.reciprocal(hinv[:, o:o + 8], hsum[:, o:o + 8])
                    settle()
                    nc.vector.tensor_tensor(split(o_tok[:, o * 64:(o + 8) * 64], 8), split(bank(6 + o // 8), 8),
                                            blast(hinv[:, o:o + 8], 64), ALU.mult).then_inc(S("o_ready"), 1)
            dve.wait_ge(S("o_turned"), past + 1)
            nc.vector.tensor_copy(oT[:, 0:BANK], bank(4)).then_inc(S("oT_ready"), 1)
            v = 0 if isinstance(it, int) else 1
            dve.wait_ge(S("mixed"), past + 1)
            nc.vector.tensor_tensor(o_tok, ps[:, 6 * BANK:8 * BANK], gate_rows[:, v * D:(v + 1) * D], ALU.mult)\
                .then_inc(S("mix_out"), 1)
            settle()
            nc.vector.tensor_tensor(xt(it), xt(it), o_tok, ALU.add)
            settle()

        dve.wait_ge(S("inputs"), 16 * len(inputs))
        row_stats("mix0")
        modulation(0)

        def post_m(t):
            dve.wait_ge(S("proj_squared", 0), t + 1)
            nc.vector.tensor_scalar(pst[:, 2:3], pst[:, 0:1], 1.0 / QL, EPS, ALU.mult, ALU.add)
            nc.vector.tensor_scalar(pst[:, 3:4], pst[:, 1:2], 1.0 / KVL, EPS, ALU.mult, ALU.add).then_inc(S("proj_mean", 0), 1)
            dve.wait_ge(S("proj_root", 0), t + 1)
            nc.vector.reciprocal(pst[:, 6:8], pst[:, 4:6])
            settle()
            if t >= 2:
                dve.wait_ge(S("turned", 0), t)
            j = t if t > 0 else 5
            key = m_key[:, j * KV:(j + 1) * KV]
            nc.vector.tensor_scalar(m_ql[:, (t % 2) * QL:(t % 2 + 1) * QL], bank(2, QL), pst[:, 6:7], None, ALU.mult)
            nc.vector.scalar_tensor_tensor(key[:, 0:KVL], bank(3, KVL), pst[:, 7:8], kvn_row[:], ALU.mult, ALU.mult)
            pe_ = bank(3, ROPE, KVL)
            if t == 0:
                nc.vector.tensor_copy(key[:, KVL:KV], pe_).then_inc(S("proj_out", 0), 1)
            else:
                cs, sn = m_rope[:, 0:ROPE], m_rope[:, ROPE:2 * ROPE]
                at = (t - 1) * ROPE
                nc.vector.tensor_tensor(cs, pe_, const[:, C_CM + at:C_CM + at + ROPE], ALU.mult)
                nc.vector.tensor_tensor(sn, pe_, const[:, C_SM + at:C_SM + at + ROPE], ALU.mult)
                settle()
                out = split(key[:, KVL:KV], ROPE // 2)
                rope(out[..., 0], out[..., 1], split(cs, ROPE // 2), split(sn, ROPE // 2)).then_inc(S("proj_out", 0), 1)
            settle()

        def post_g(t):
            W = NQ + NK
            qk = g_qk[:, (t % 2) * W:(t % 2 + 1) * W]
            heads_ = HEADS + KVH
            dve.wait_ge(S("proj_out", 1), t + 1)
            nc.vector.tensor_tensor(g_a, qk, qk, ALU.mult)
            settle()
            nc.vector.tensor_reduce(pst[:, 0:20], split(g_a, heads_), AX.X, ALU.add)
            settle()
            nc.vector.tensor_scalar(pst[:, 20:40], pst[:, 0:20], 1.0 / HD, EPS, ALU.mult, ALU.add).then_inc(S("proj_mean", 1), 1)
            dve.wait_ge(S("proj_root", 1), t + 1)
            nc.vector.reciprocal(pst[:, 0:20], pst[:, 40:60])
            settle()
            nc.vector.tensor_tensor(split(qk, heads_), split(qk, heads_), blast(pst[:, 0:20], HD), ALU.mult)
            settle()
            nc.vector.tensor_tensor(split(qk[:, 0:NQ], HEADS), split(qk[:, 0:NQ], HEADS), bmid(qkn_row[:, 0:HD], HEADS), ALU.mult)
            last = nc.vector.tensor_tensor(split(qk[:, NQ:W], KVH), split(qk[:, NQ:W], KVH), bmid(qkn_row[:, HD:2 * HD], KVH),
                                           ALU.mult)
            if t > 0:
                at = (t - 1) * HD
                settle()
                nc.vector.tensor_tensor(split(g_a, heads_), split(qk, heads_), bmid(const[:, C_CG + at:C_CG + at + HD], heads_), ALU.mult)
                nc.vector.tensor_tensor(split(g_b, heads_), split(qk, heads_), bmid(const[:, C_SG + at:C_SG + at + HD], heads_), ALU.mult)
                settle()
                out = split(qk, W // 2)
                last = rope(out[..., 0], out[..., 1], split(g_a, W // 2), split(g_b, W // 2))
            last.then_inc(S("qk_ready"), 1)
            settle()

        def projection(l, post):
            norm(l, 0)
            norm(l, 1)
            mod_cols(l, 0)
            for t in range(NTILE):
                if t + 2 < NTILE:
                    norm(l, t + 2)
                if t + 1 < NTILE:
                    mod_cols(l, t + 1)
                post(t)

        projection(0, post_m)
        dve.wait_ge(S("state_stored", 0), 16)
        for m in range(HEADS // 2):
            dve.wait_ge(S("k_made"), m + 1)
            nc.vector.tensor_copy(m_kT[0:64, (2 * m + 1) * KEYS:(2 * m + 2) * KEYS], spair(m, KEYS)[64:128]).then_inc(S("k_odd"), 1)
        for j in range(1, NKEYT, 2):
            dve.wait_ge(S("v_made"), j + 1)
            nc.vector.tensor_copy(m_V[:, j * D:(j + 1) * D], ps[:, 6 * BANK:8 * BANK]).then_inc(S("v_odd"), 1)
        dve.wait_ge(S("gates_a", 0), 32)
        dve.wait_ge(S("rope_keys"), 1)

        def m_tile(it, keys):
            if keys > P:
                dve.wait_ge(S("q_out"), it + 1)
                pe_ = split(q_tok, HEADS)[:, :, NOPE:QD]
                cos = const[:, ds(it * ROPE + (C_CM - ROPE), ROPE)]
                sin = const[:, ds(it * ROPE + (C_SM - ROPE), ROPE)]
                nc.vector.tensor_tensor(split(q_cos, HEADS), pe_, bmid(cos, HEADS), ALU.mult)
                nc.vector.tensor_tensor(split(q_sin, HEADS), pe_, bmid(sin, HEADS), ALU.mult)
                settle()
                out = pe_.rearrange("p h (r two) -> p h r two", two=2)
                cs = q_cos.rearrange("p (h r two) -> p h r two", h=HEADS, two=2)
                sn = q_sin.rearrange("p (h r two) -> p h r two", h=HEADS, two=2)
                rope(out[..., 0], out[..., 1], cs, sn).then_inc(S("q_roped"), 1)
            dve.wait_ge(S("q_turned"), it + 1)
            nc.vector.tensor_copy(qT[0:QD, D:2 * D], ps[0:QD, D:2 * D]).then_inc(S("q_ready", 0), 1)
            heads(0, it, keys)

        m_tile(0, P)
        with dve.Fori(0, LAT) as i:
            m_tile(i + 1, LKEYS)
        meet(dve, 0)

        def routing(l):
            r4 = const[:, C_R4:C_R4 + NG]
            n = [R_FREE]

            def new(cols):
                n[0] += cols
                return e_r[:, n[0] - cols:n[0]]

            def op(ins):
                settle()
                return ins

            T5 = NTILE
            lg, le = new(T5 * NG), new(T5 * NE)
            sc4, t80, ein, e2 = new(T5 * NG), new(T5 * NE), new(T5 * EPG), new(T5 * EPG)
            gm, m1, m2, mx = new(T5), new(T5), new(T5), new(T5)
            og, o1, o2 = new(T5 * NG), new(T5 * EPG), new(T5 * EPG)
            M1, M2, M = new(T5 * NE), new(T5 * NE), new(T5 * NE)
            den, gw = new(T5), new(T5)
            cnt, nt, cs, c2 = new(NE), new(NE), new(NE), new(NE)
            te, te1 = new(SLOT_TILES * NE), new(SLOT_TILES)
            slots = new(2 * T5)
            assert n[0] <= 1600, n[0]
            sh, ex = e_r[:, R_SH:R_SH + T5 * (NG + 1)], e_r[:, R_EX:R_EX + T5 * (NG + 1)]
            dve.wait_ge(S("logits", l), T5)
            lo = split(bank(2, T5 * 32), T5)
            nc.vector.tensor_tensor(split(lg, T5), lo[:, :, 0:NG], bmid(rbias[:, l * NR:l * NR + NG], T5), ALU.add)
            op(nc.vector.tensor_tensor(split(le, T5), lo[:, :, NG:NR], bmid(rbias[:, l * NR + NG:(l + 1) * NR], T5), ALU.add))

            def first_max(oh, v, m):
                op(nc.vector.tensor_reduce(m, split(v, T5), AX.X, ALU.max))
                op(nc.vector.tensor_tensor(split(sc4, T5), split(v, T5), blast(m, NG), ALU.is_equal))
                op(nc.vector.tensor_tensor(split(sc4, T5), split(sc4, T5), bmid(r4, T5), ALU.mult))
                op(nc.vector.tensor_reduce(mx, split(sc4, T5), AX.X, ALU.max))
                op(nc.vector.tensor_tensor(split(oh, T5), split(sc4, T5), blast(mx, NG), ALU.is_equal))

            first_max(og, lg, gm)
            nc.vector.tensor_tensor(split(sh[:, 0:T5 * NG], T5), split(lg, T5), blast(gm, NG), ALU.subtract)
            op(nc.vector.tensor_tensor(t80.rearrange("p (x j) -> p x j", j=EPG), le.rearrange("p (x j) -> p x j", j=EPG),
                                       blast(og, EPG), ALU.mult))
            op(nc.vector.tensor_reduce(split(ein, T5), t80.rearrange("p (t g j) -> p t j g", t=T5, g=NG), AX.X, ALU.add))
            first_max(o1, ein, m1)
            op(nc.vector.scalar_tensor_tensor(e2, o1, MASKED, ein, ALU.mult, ALU.add))
            first_max(o2, e2, m2)
            nc.vector.tensor_tensor(sh[:, T5 * NG:], m2, m1, ALU.subtract).then_inc(S("shifted", l), 1)
            for oh, m in ((o1, M1), (o2, M2)):
                for g in range(NG):
                    nc.vector.tensor_tensor(m.rearrange("p (t g j) -> p t g j", t=T5, g=NG)[:, :, g], split(oh, T5),
                                            blast(split(og, T5)[:, :, g], EPG), ALU.mult)
            settle()
            nc.vector.tensor_tensor(M, M1, M2, ALU.add).then_inc(S("picked", l), 1)
            dve.wait_ge(S("r_exp", l), 1)
            op(nc.vector.tensor_reduce(den, split(ex[:, 0:T5 * NG], T5), AX.X, ALU.add))
            op(nc.vector.scalar_tensor_tensor(den, ex[:, T5 * NG:], 1.0, den, ALU.add, ALU.mult))
            op(nc.vector.reciprocal(w_pair[:, 0:T5], den))
            op(nc.vector.tensor_tensor(w_pair[:, T5:], w_pair[:, 0:T5], ex[:, T5 * NG:], ALU.mult))
            dve.wait_ge(S("ranked", l), 1)
            rank = bank(3, T5 * NE)
            op(nc.vector.tensor_copy(cnt, bank(3, NE, T5 * NE)))
            op(nc.vector.tensor_scalar(nt, cnt, 0.0, None, ALU.is_gt))
            for k in range(1, NTILE):
                op(nc.vector.scalar_tensor_tensor(nt, cnt, float(k * P), nt, ALU.is_gt, ALU.add))
            src = nt
            for k, dst in ((1, cs), (2, c2), (4, cs), (8, c2)):
                nc.vector.tensor_copy(dst[:, 0:k], src[:, 0:k])
                op(nc.vector.tensor_tensor(dst[:, k:NE], src[:, k:NE], src[:, 0:NE - k], ALU.add))
                src = dst
            nc.vector.tensor_tensor(split(te, SLOT_TILES), blast(const[:, C_TI:C_TI + SLOT_TILES], NE), bmid(c2, SLOT_TILES),
                                    ALU.is_ge)
            op(nc.vector.tensor_tensor(cs, c2, nt, ALU.subtract))
            nc.vector.tensor_reduce(te1, split(te, SLOT_TILES), AX.X, ALU.add)
            op(nc.vector.tensor_scalar(cs, cs, float(P), None, ALU.mult))
            op(nc.vector.tensor_tensor(split(t80, T5), split(rank, T5), bmid(cs, T5), ALU.add))
            op(nc.vector.tensor_tensor(M1, M1, t80, ALU.mult))
            nc.vector.tensor_tensor(M2, M2, t80, ALU.mult)
            sl = slots.rearrange("p (t c) -> p c t", c=2)
            settle()
            nc.vector.tensor_reduce(sl[:, 0], split(M1, T5), AX.X, ALU.add)
            nc.vector.tensor_reduce(sl[:, 1], split(M2, T5), AX.X, ALU.add)
            op(nc.vector.tensor_scalar(te1, te1, float(NE - 1), None, ALU.min))
            nc.vector.tensor_copy(slot_i[:], slots)
            nc.vector.tensor_copy(expert[:], te1).then_inc(S("routed", l), 1)

        w_pair = e_r[:, R_W:R_W + 2 * NTILE]

        def experts(l):
            row_stats(f"ffn{l}")
            dve.wait_ge(S("rows_e", l), 16 * 6)
            for t in range(NTILE):
                v = 0 if t == 0 else 1
                h = e_h[:, t * D:(t + 1) * D]
                nc.vector.scalar_tensor_tensor(h, xt(t), rstd[:, t:t + 1], e_row[:, 2 * v * D:(2 * v + 1) * D], ALU.mult, ALU.mult)
                settle()
                nc.vector.tensor_tensor(h, h, e_row[:, (2 * v + 1) * D:(2 * v + 2) * D], ALU.add).then_inc(S("h_ready", l), 1)
            routing(l)

            def xsT(t, u):
                dve.wait_ge(S("xs_used", l), t + 1)
                nc.vector.tensor_copy(e_xsT[:, (u % 2) * D:(u % 2 + 1) * D], ps[:, 0:D]).then_inc(S("xsT_ready", l), 1)

            def hid(t, u):
                dve.wait_ge(S("sil_ready", l), t + 1)
                c = slice((u % 2) * FF, (u % 2 + 1) * FF)
                nc.vector.tensor_tensor(e_hid[:, c], bank(2 + u % 2, FF, FF), e_sil[:, c], ALU.mult).then_inc(S("hid_ready", l), 1)

            def hidT(t, u):
                dve.wait_ge(S("hid_turned", l), t + 1)
                nc.vector.tensor_copy(e_hidT[:, (u % 2) * FF:(u % 2 + 1) * FF], bank(4, FF)).then_inc(S("hidT_ready", l), 1)

            xsT(0, 0)
            hid(0, 0)
            xsT(1, 1)
            with dve.Fori(0, ROUNDS) as i:
                for u in range(2):
                    hidT(i * 2 + u, u)
                    xsT(i * 2 + (u + 2), u)
                    hid(i * 2 + (u + 1), u + 1)
            for t in range(LOOPED, SLOT_TILES):
                hidT(t, t)
                if t + 2 < SLOT_TILES:
                    xsT(t + 2, t)
                if t + 1 < SLOT_TILES:
                    hid(t + 1, t + 1)
            for t in range(NTILE):
                dve.wait_ge(S(f"gathered{t % 2}", l), 32 * (t // 2 + 1))
                a, b = (e_g[:, (2 * (t % 2) + c) * D:(2 * (t % 2) + c + 1) * D] for c in range(2))
                v = 0 if t == 0 else 1
                nc.vector.tensor_scalar(a, a, w_pair[:, t:t + 1], None, ALU.mult)
                settle()
                nc.vector.scalar_tensor_tensor(a, b, w_pair[:, NTILE + t:NTILE + t + 1], a, ALU.mult, ALU.add)
                settle()
                nc.vector.tensor_tensor(a, a, gate_rows[:, v * D:(v + 1) * D], ALU.mult)
                settle()
                nc.vector.tensor_tensor(xt(t), xt(t), a, ALU.add).then_inc(S("combined", l), 1)

        experts(0)
        meet(dve, 1)
        modulation(1)
        row_stats("mix1")
        projection(1, post_g)
        dve.wait_ge(S("gates_a", 1), 32)
        heads(1, 0, P)
        with dve.Fori(0, LAT) as i:
            heads(1, i + 1, LKEYS)
        meet(dve, 2)
        experts(1)
        meet(dve, 3)
        row_stats("end")
        dve.wait_ge(S("final_landed"), 16)
        for t in range(NTILE):
            nc.vector.scalar_tensor_tensor(e_h[:, t * D:(t + 1) * D], xt(t), rstd[:, t:t + 1], e_row[:, 0:D], ALU.mult, ALU.mult)\
                .then_inc(S("y_ready"), 1)

    @block.tensor
    def _(pe):
        mm = nc.tensor.matmul

        def turn(out, in_, rows=P):
            return nc.tensor.transpose(out, in_, ident[0:rows, 0:rows])

        pe.wait_ge(S("inputs"), 16 * len(inputs))
        turn(bank(7, P), veca[:])
        turn(bank(7, VB_END, P), vecb[0:VB_END, :], VB_END).then_inc(S("cols_turned"), 1)

        def ada(l):
            pe.wait_ge(S("cond_ready"), 1)
            c = cond[:].rearrange("p (v k) -> p k v", v=2)
            with pe.Fori(0, ADA_ITEMS // NSLOT) as i:
                for u in range(NSLOT):
                    w = split(slot_of(("ada", l, u), SLOT), KD)
                    wait_landed(pe, ("ada", l, u), i * 32)
                    for m in range(4):
                        out = ps[:, ds(i * 32 + (7 * BANK + 8 * u + 2 * m), 2)]
                        for k in range(KD):
                            last = mm(out, w[:, k, m * P:(m + 1) * P], c[:, k], start=k == 0, stop=k == KD - 1)
                    last.then_inc(S("ring_used"), 1)
            pe.drain().then_inc(S("ada_done", l), 1)
            pe.wait_ge(S("mod_ready", l), 1)
            turn(ps[0:96, 6 * BANK:6 * BANK + P], modc[:, 96 * l:96 * (l + 1)]).then_inc(S("mod_turned", l), 1)

        def turn_tile(l, t):
            pe.wait_ge(S("xn_ready", l), t + 1)
            if t:
                pe.wait_ge(S("hT_ready", l), t)
            for k in range(KD):
                last = turn(ps[:, k * P:(k + 1) * P], xn[l](t)[:, k * P:(k + 1) * P])
            last.then_inc(S("n_turned", l), 1)

        def project(l, t, parts, out_sem):
            pe.wait_ge(S("hT_ready", l), t + 1)
            if t:
                pe.wait_ge(out_sem, t)
            for b, (name, cols) in enumerate(parts):
                if t == 0:
                    wait_landed(pe, (name, l, 0))
                w = split(slot_of((name, l, 0), KD * cols), KD)
                for k in range(KD):
                    last = mm(bank(2 + b, cols), hT[l](t)[:, k * P:(k + 1) * P], w[:, k], start=k == 0, stop=k == KD - 1)
            last.then_inc(S("projected", l), 1)

        def heads(l, it, keys, score_of, v_of):
            past = tiles_before(l, it)
            g = past * HEADS
            first = 5 if keys == P else 0
            for n in range(HEADS + 3):
                if n < HEADS:
                    if n >= 2:
                        pe.wait_ge(S("exp_ready"), g + n - 1)
                    q, k = score_of(n)
                    for c in range(0, keys, BANK):
                        w = min(BANK, keys - c)
                        last = mm(spair(n, LKEYS)[:, c:c + w], q, k[:, first * P + c:first * P + c + w], start=True, stop=True)
                    last.then_inc(S("scored"), 1)
                if 0 <= n - 2 < HEADS:
                    h = n - 2
                    pe.wait_ge(S("exp_ready"), g + h + 1)
                    if h:
                        pe.wait_ge(S("pt_ready"), g + h)
                    for j in range(keys // P):
                        last = turn(ps[:, 4 * BANK + j * P:4 * BANK + (j + 1) * P], pbuf(h, keys)[:, j * P:(j + 1) * P])
                    last.then_inc(S("p_turned"), 1)
                if n >= 3:
                    h = n - 3
                    pe.wait_ge(S("pt_ready"), g + h + 1)
                    if h == 0 and not (isinstance(past, int) and past == 0):
                        pe.wait_ge(S("mix_out"), past)
                    for j in range(keys // P):
                        last = mm(bank(6 + h // 8, 64, 64 * (h % 8)), ptbuf(h, keys)[:, j * P:(j + 1) * P], v_of(h, first + j),
                                  start=j == 0, stop=j == keys // P - 1)
                    last.then_inc(S("pv_done"), 1)
            pe.wait_ge(S("o_ready"), past * 2 + 2)
            for k in range(KD):
                last = turn(ps[:, 4 * BANK + k * P:4 * BANK + (k + 1) * P], o_tok[:, k * P:(k + 1) * P])
            last.then_inc(S("o_turned"), 1)
            pe.wait_ge(S("oT_ready"), past * 2 + 2)
            for n in range(2):
                name = (MATRICES[l][-2 + n], l, 0)
                w = split(slot_of(name, SLOT), KD)
                if isinstance(it, int):
                    wait_landed(pe, name)
                for k in range(KD):
                    last = mm(bank(6 + n), oT[:, k * P:(k + 1) * P], w[:, k], start=k == 0, stop=k == KD - 1)
            last.then_inc(S("mixed"), 1)

        def used(n):
            pe.drain().then_inc(S("ring_used"), n)

        ada(0)

        def turn_keys_m(t):
            j = t if t > 0 else 5 if t == 0 else 0
            if t >= 0:
                pe.wait_ge(S("proj_out", 0), t + 1)
                pe.wait_ge(S("turned_out", 0), t + 1)
                for m in range(3):
                    turn(bank(4, P, m * P), m_ql[:, (t % 2) * QL + m * P:(t % 2) * QL + (m + 1) * P])
            key = m_key[:, j * KV:(j + 1) * KV]
            for m in range(2):
                turn(bank(5, P, m * P), key[:, m * P:(m + 1) * P])
            turn(ps[0:ROPE, 5 * BANK + 2 * P:5 * BANK + 3 * P], key[:, KVL:KV]).then_inc(S("turned", 0), 1)

        def turn_keys_g(t):
            W = NQ + NK
            if t >= 0:
                pe.wait_ge(S("qk_ready"), t + 1)
                pe.wait_ge(S("turned_out", 1), t + 1)
                for m in range(8):
                    turn(ps[:, 5 * BANK + m * P:5 * BANK + (m + 1) * P], g_qk[:, (t % 2) * W + m * P:(t % 2) * W + (m + 1) * P])
                k = g_qk[:, (t % 2) * W + NQ:(t % 2 + 1) * W]
            else:
                pe.wait_ge(S("cache_landed"), 32)
                k = g_cache
            for h in range(KVH):
                last = turn(ps[0:HD, 7 * BANK + h * P:7 * BANK + (h + 1) * P], k[:, h * HD:(h + 1) * HD])
            last.then_inc(S("turned", 1), 1)

        def projection(l, parts, turn_keys, out_sem):
            turn_tile(l, 0)
            turn_keys(-1)
            for t in range(NTILE):
                if t + 1 < NTILE:
                    turn_tile(l, t + 1)
                project(l, t, parts, out_sem)
                if t == NTILE - 1:
                    used(len(parts))
                if t:
                    turn_keys(t - 1)
            turn_keys(NTILE - 1)

        projection(0, (("dq", QL), ("dkv", KV)), turn_keys_m, S("proj_out", 0))
        wait_landed(pe, ("uk", 0, 0))
        pe.wait_ge(S("turned_out", 0), NKEYT)
        w = split(slot_of(("uk", 0, 0), 2 * D), 2)
        for m in range(HEADS // 2):
            if m >= 2:
                pe.wait_ge(S("k_even"), m - 1)
                pe.wait_ge(S("k_odd"), m - 1)
            for c, n in ((0, BANK), (BANK, KEYS - BANK)):
                for k in range(2):
                    last = mm(spair(m, KEYS)[:, c:c + n], w[:, k, m * P:(m + 1) * P], m_ckvT[:, k * KEYS + c:k * KEYS + c + n],
                              start=k == 0, stop=k == 1)
            last.then_inc(S("k_made"), 1)
        used(1)
        wait_landed(pe, ("uv", 0, 0))
        pe.wait_ge(S("mod_turned_out", 0), 1)
        w = split(slot_of(("uv", 0, 0), 2 * D), 2)
        for j in range(NKEYT):
            if j >= 2:
                pe.wait_ge(S("v_odd" if j % 2 else "v_even"), j // 2)
            for n in range(2):
                for k in range(2):
                    last = mm(bank(4 + 2 * (j % 2) + n), m_ckvT[:, k * KEYS + j * P:k * KEYS + (j + 1) * P],
                              w[:, k, n * BANK:(n + 1) * BANK], start=k == 0, stop=k == 1)
            last.then_inc(S("v_made"), 1)
        used(1)
        pe.wait_ge(S("k_even"), HEADS // 2)
        pe.wait_ge(S("k_odd"), HEADS // 2)
        pe.wait_ge(S("v_even"), NKEYT // 2)
        pe.wait_ge(S("v_odd"), NKEYT // 2)
        pe.wait_ge(S("rope_keys"), 1)
        for n in range(2):
            wait_landed(pe, (f"uq{n}", 0, 0))

        def m_tile(it, keys):
            pe.wait_ge(S("ql_ready"), it + 1)
            for b in range(4):
                w = split(slot_of((f"uq{b // 2}", 0, 0), 3 * 768), 3)
                for k in range(3):
                    last = mm(bank(b, 4 * QD), qls[:, k * P:(k + 1) * P], w[:, k, (b % 2) * 4 * QD:(b % 2 + 1) * 4 * QD],
                              start=k == 0, stop=k == 2)
            last.then_inc(S("q_made"), 1)
            pe.wait_ge(S("q_out"), it + 1)
            if keys > P:
                pe.wait_ge(S("q_roped"), it)
            for h in range(HEADS):
                last = turn(ps[0:QD, h * P:(h + 1) * P], q_tok[:, h * QD:(h + 1) * QD])
            last.then_inc(S("q_turned"), 1)
            pe.wait_ge(S("q_ready", 0), it * 2 + 2)
            heads(0, it, keys, lambda h: (qT[0:QD, h * P:(h + 1) * P], m_kT[0:QD, h * KEYS:(h + 1) * KEYS]),
                  lambda h, j: m_V[:, j * D + h * VD:j * D + (h + 1) * VD])

        m_tile(0, P)
        with pe.Fori(0, LAT) as i:
            m_tile(i + 1, LKEYS)
        used(4)
        meet(pe, 0)

        def experts(l):
            def turn_h(t):
                pe.wait_ge(S("h_ready", l), t + 1)
                if t:
                    pe.wait_ge(S("hT_out", l), t)
                for k in range(KD):
                    last = turn(ps[:, k * P:(k + 1) * P], e_h[:, t * D + k * P:t * D + (k + 1) * P])
                last.then_inc(S("h_turned", l), 1)

            turn_h(0)
            pe.wait_ge(S("router_landed", l), 32)
            for t in range(NTILE):
                if t + 1 < NTILE:
                    turn_h(t + 1)
                pe.wait_ge(S("hT_out", l), t + 1)
                for k in range(KD):
                    last = mm(bank(2, NR, t * 32), e_hT[:, (t % 2) * D + k * P:(t % 2) * D + (k + 1) * P], rw[:, k * NR:(k + 1) * NR],
                              start=k == 0, stop=k == KD - 1)
                last.then_inc(S("logits", l), 1)
            pe.wait_ge(S("picked", l), 1)
            M = e_r[:, R_M:R_M + NTILE * NE]
            for t in range(NTILE):
                for s in range(t + 1):
                    mm(bank(3, NE, t * NE), tri if s == t else ones, M[:, s * NE:(s + 1) * NE], start=s == 0, stop=s == t)
            for s in range(NTILE):
                last = mm(bank(3, NE, NTILE * NE), ones, M[:, s * NE:(s + 1) * NE], start=s == 0, stop=s == NTILE - 1)
            last.then_inc(S("ranked", l), 1)
            pe.wait_ge(S("routed", l), 1)

            def turn_rows(t, u, r):
                pe.wait_ge(S(f"xs_landed{u % 2}", l), r * 16 + 16)
                for k in range(KD):
                    last = turn(ps[:, k * P:(k + 1) * P], e_xs[:, (u % 2) * D + k * P:(u % 2) * D + (k + 1) * P])
                last.then_inc(S("xs_used", l), 1)

            def gate_up(t, u, more=0):
                pe.wait_ge(S("xsT_ready", l), t + 1)
                wait_landed(pe, ("gu", l, u), more)
                w = split(slot_of(("gu", l, u), SLOT), KD)
                for k in range(KD):
                    last = mm(bank(2 + u % 2), e_xsT[:, (u % 2) * D + k * P:(u % 2) * D + (k + 1) * P], w[:, k],
                              start=k == 0, stop=k == KD - 1)
                last.then_inc(S("gu_done", l), 1)

            def turn_hid(t, u):
                pe.wait_ge(S("hid_ready", l), t + 1)
                for k in range(2):
                    last = turn(bank(4, P, k * P), e_hid[:, (u % 2) * FF + k * P:(u % 2) * FF + (k + 1) * P])
                last.then_inc(S("hid_turned", l), 1)

            def down(t, u, more=0):
                pe.wait_ge(S("hidT_ready", l), t + 1)
                pe.wait_ge(S("y_out", l), t + 1)
                wait_landed(pe, ("dn", l, u), more)
                w = split(slot_of(("dn", l, u), 2 * D), 2)
                for n in range(2):
                    for k in range(2):
                        last = mm(bank(6 + n), e_hidT[:, (u % 2) * FF + k * P:(u % 2) * FF + (k + 1) * P],
                                  w[:, k, n * BANK:(n + 1) * BANK], start=k == 0, stop=k == 1)
                last.then_inc(S("y_done", l), 1)

            turn_rows(0, 0, 0)
            gate_up(0, 0)
            turn_rows(1, 1, 0)
            with pe.Fori(0, ROUNDS) as i:
                for u in range(2):
                    turn_hid(i * 2 + u, u)
                    gate_up(i * 2 + (u + 1), u + 1, i * 32)
                    turn_rows(i * 2 + (u + 2), u, i + 1)
                    down(i * 2 + u, u, i * 32)
            for t in range(LOOPED, SLOT_TILES):
                turn_hid(t, t)
                if t + 1 < SLOT_TILES:
                    gate_up(t + 1, t + 1)
                if t + 2 < SLOT_TILES:
                    turn_rows(t + 2, t, t // 2 + 1)
                down(t, t)

        def pads(l):
            n = sum(x[0] == "pad" and x[1] == l for x in order)
            if n:
                used(n)

        pads(0)
        experts(0)
        pads(2)
        meet(pe, 1)
        ada(1)
        projection(1, (("qkv0", BANK), ("qkv1", BANK), ("qkv2", BANK)), turn_keys_g, S("qk_ready"))
        pe.wait_ge(S("turned_out", 1), NKEYT)

        def g_tile(it, keys):
            pe.wait_ge(S("q_ready", 1), it + 1)

            def score_of(h):
                half = slice(64 * (h % 2), 64 * (h % 2) + 64)
                return qT[half, (h // 2) * P:(h // 2 + 1) * P], g_kT[half, (h // 4) * KEYS:(h // 4 + 1) * KEYS]

            heads(1, it, keys, score_of, lambda h, j: g_V[:, j * NK + (h // 4) * HD:j * NK + (h // 4 + 1) * HD])

        g_tile(0, P)
        with pe.Fori(0, LAT) as i:
            g_tile(i + 1, LKEYS)
        used(2)
        meet(pe, 2)
        pads(1)
        experts(1)
        pads(3)
        meet(pe, 3)


def constants():
    c = np.zeros((P, C_END), np.float32)
    c[:, C_ID:C_ID + P] = np.eye(P)
    c[:, C_ONE:C_ONE + P] = 1.0
    c[:, C_TRI:C_TRI + P] = np.triu(np.ones((P, P)), 1)
    t = np.arange(LAT * P)
    row, col = (t // GRID_W).astype(np.float32), (t % GRID_W).astype(np.float32)
    for dim, at_c, at_s in ((ROPE, C_CM, C_SM), (HD, C_CG, C_SG)):
        axis = dim // 2
        inv = np.power(np.float32(10000.0), -np.arange(0, axis, 2, dtype=np.float32) / np.float32(axis)).astype(np.float32)
        ang = np.concatenate([row[:, None] * inv, col[:, None] * inv], axis=1)
        for f, at in ((np.cos, at_c), (np.sin, at_s)):
            v = np.repeat(f(ang).astype(np.float32), 2, axis=1).reshape(LAT, P, dim)
            c[:, at:at + LAT * dim] = v.transpose(1, 0, 2).reshape(P, LAT * dim)
    c[:, C_R4:C_R4 + NG] = NG - np.arange(NG)
    c[:, C_TI:C_TI + SLOT_TILES] = np.arange(SLOT_TILES)
    return c


def kernel(**inputs):
    import concourse.bacc as bacc
    from concourse.bass_utils import run_bass_kernel_spmd

    a = {n: np.ascontiguousarray(np.asarray(x)) for n, x in inputs.items()}
    small = ("c", "c_ctx", "ada_b", "norm_mix", "norm_ffn", "mla_q_norm")
    lay = {n: x for n, x in a.items() if n not in small}
    lay["vec_a"] = np.concatenate([a["ada_b"].reshape(-1, P), a["norm_mix"].reshape(-1, P), a["norm_ffn"].reshape(-1, P)])
    lay["vec_b"] = np.concatenate([a["c_ctx"].reshape(-1, P), a["c"].reshape(-1, P), a["mla_q_norm"].reshape(-1, P)])
    lay["mla_w_uk"] = a["mla_w_uk"].reshape(KVL, HEADS * NOPE)
    lay["mla_w_uv"] = a["mla_w_uv"].reshape(KVL, HEADS * VD)
    lay["const"] = constants()
    nc = bacc.Bacc("TRN2", target_bir_lowering=False, num_devices=1)
    A = {n: nc.dram_tensor(f"in_{n}", x.shape, mybir.dt.from_np(x.dtype), kind="ExternalInput").ap() for n, x in lay.items()}
    shapes = ((1, P, D), (1, LAT * P, D), (1, 1, P, KV), (1, 1, P, 2, KVH, HD))
    O = [nc.dram_tensor(f"out_{i}", s, F32, kind="ExternalOutput").ap() for i, s in enumerate(shapes)]
    with ExitStack() as ctx:
        program(nc, ctx, A, O)
    r = run_bass_kernel_spmd(nc, [{f"in_{n}": x for n, x in lay.items()}], core_ids=[0])
    return tuple(r.results[0][f"out_{i}"] for i in range(len(shapes)))
```

```python
from contextlib import ExitStack

import numpy as np
import concourse.bass as bass
from concourse import mybir

F32 = mybir.dt.float32
I32 = mybir.dt.int32
ALU = mybir.AluOpType
ACT = mybir.ActivationFunctionType
AX = mybir.AxisListType
ds = bass.ds

P = 128
D = 1024
KD = D // P
NTILE = 5
LAT = NTILE - 1
NKEYT = 6
KEYS = NKEYT * P
LKEYS = 5 * P
EPS = 1e-6
HEADS = 16
NOPE, ROPE, VD = 64, 32, 64
QD = NOPE + ROPE
QL, KVL = 384, 256
KV = KVL + ROPE
KVH, HD = 4, 64
NG, EPG = 4, 4
NE = NG * EPG
NR = NG + NE
FF = 256
TOK = NTILE * P
PAIRS = 2 * TOK
SLOT_TILES = (PAIRS - NE) // P + NE
GRID_W = 64
BANK = 512
SLOT = 4096
NSLOT = 4
ADA_ITEMS = 12
ADA_SPLIT = (2, 6)
NQ, NK = HEADS * HD, KVH * HD
SCALE = (QD ** -0.5, HD ** -0.5)
ROUNDS = (SLOT_TILES - 2) // 2
LOOPED = 2 * ROUNDS
MASKED = -3.0e38

C_ID, C_ONE, C_TRI, C_CM = 0, P, 2 * P, 3 * P
C_SM = C_CM + LAT * ROPE
C_CG = C_SM + LAT * ROPE
C_SG = C_CG + LAT * HD
C_R4 = C_SG + LAT * HD
C_TI = C_R4 + NG
C_SEL = C_TI + SLOT_TILES
C_RND = C_SEL + 1
C_END = C_RND + ROUNDS

MODS = 2 * 6 * KD
VB_COND, VB_QN, VB_END = 0, 16, 19


def bmid(ap, n):
    return ap.unsqueeze(1).broadcast_to([ap.shape[0], n, ap.shape[1]])


def blast(ap, n):
    return ap.unsqueeze(2).broadcast_to([ap.shape[0], ap.shape[1], n])


def split(ap, a):
    return ap.rearrange("p (a b) -> p a b", a=a)


A_HEADS = HEADS * KEYS + NKEYT * D + 3 * TOK
ARENA = A_HEADS + 5632 + QL

R_SH = 0
R_EX = R_SH + NTILE * (NG + 1)
R_W = R_EX + NTILE * (NG + 1)
R_FREE = R_W + 2 * NTILE
R_M = R_FREE + NTILE * (NG + NE + NG + NE + 2 * EPG + 4 + NG + 2 * EPG + 2 * NE)

MATRICES = (("dq", "dkv", "uk", "uv", "uq0", "uq1", "wo0", "wo1"), ("qkv0", "qkv1", "qkv2", "gwo0", "gwo1"))


def program(nc, ctx, A, O):
    def sb(name, cols, dt=F32):
        return ctx.enter_context(nc.sbuf_tensor(name, [P, cols], dt))

    def split_rows(ap):
        return ap.rearrange("p (a b) -> p a b", b=P)

    sems = {}

    def S(name, layer=None):
        key = name if layer is None else f"{name}_{layer}"
        if key not in sems:
            sems[key] = ctx.enter_context(nc.semaphore(key))
        return sems[key]

    const = sb("const", C_END)
    X = sb("X", NTILE * D)
    vecb, colb = sb("vecb", P), sb("colb", VB_END)
    cond = sb("cond", 2 * KD)
    modc = sb("modc", 2 * 96)
    modt = sb("modt", P)
    mod_vec = sb("mod_vec", 4 * P)
    gate_rows = sb("gate_rows", 2 * D)
    zeros = sb("zeros", P)
    kvn_row, qkn_row = sb("kvn_row", KVL), sb("qkn_row", 2 * HD)
    rbias, rw = sb("rbias", 2 * NR), sb("rw", KD * NR)
    ring = sb("ring", NSLOT * SLOT)
    ssq, rstd, st = sb("ssq", NTILE), sb("rstd", NTILE), sb("st", 2 * NTILE)
    hst, hsum, hinv = sb("hst", HEADS), sb("hsum", HEADS), sb("hinv", HEADS)
    pst = sb("pst", 3 * (HEADS + KVH))
    arena = sb("arena", ARENA)
    expert, slot_i = sb("expert", SLOT_TILES, I32), sb("slot_i", 2 * NTILE, I32)
    rounds = sb("rounds", 2, I32)
    ps = ctx.enter_context(nc.psum_tensor("ps", [P, 8 * BANK], F32))

    slots = nc.dram_tensor("slot_rows", (SLOT_TILES * P, D), F32).ap()
    modraw = [nc.dram_tensor(f"mod_raw{l}", (2, 6 * D), F32).ap() for l in range(2)]
    modrow = [nc.dram_tensor(f"mod_rows{l}", (2, 6, D), F32).ap() for l in range(2)]

    ident, ones, tri = const[:, C_ID:C_ID + P], const[:, C_ONE:C_ONE + P], const[:, C_TRI:C_TRI + P]

    def bank(b, n=BANK, at=0):
        return ps[:, b * BANK + at:b * BANK + at + n]

    def ar(at, n):
        return arena[:, at:at + n]

    def xt(t):
        return X[:, ds(t * D, D)]

    m_kT, m_V, m_qlT = ar(0, HEADS * KEYS), ar(HEADS * KEYS, NKEYT * D), ar(A_HEADS - 3 * TOK, 3 * TOK)
    qT, Pb, PT = ar(A_HEADS, HEADS * P), ar(A_HEADS + 2048, 2 * LKEYS), ar(A_HEADS + 3328, 2 * LKEYS)
    oT, qls = ar(A_HEADS + 4608, D), ar(A_HEADS + 5632, QL)
    q_tok, q_cos, q_sin = ar(A_HEADS + 2048, HEADS * QD), ar(A_HEADS + 3584, 512), ar(A_HEADS + 4096, 512)
    m_ckvT, m_krT = ar(A_HEADS, 2 * KEYS), ar(A_HEADS + 2 * KEYS, KEYS)
    m_ql, m_key = ar(4 * D, 2 * QL), ar(5 * D, NKEYT * KV)
    m_junk, m_rope = ar(7 * D, D), ar(8 * D, 2 * ROPE)
    g_kT, g_V, g_qT = ar(0, KVH * KEYS), ar(3072, NKEYT * NK), ar(4608, 8 * TOK)
    g_qk, g_cache = ar(13824, 2 * (NQ + NK)), ar(18944, NK)
    g_a, g_b, g_junk = ar(16384, NQ + NK), ar(17664, NQ + NK), ar(19200, D)
    e_row, e_h, e_hT = ar(0, 4 * D), ar(4 * D, NTILE * D), ar(9 * D, 2 * D)
    e_junk, e_r = ar(11 * D, D), ar(12 * D, 1600)
    e_xs, e_xsT = ar(14000, 2 * D), ar(16048, 2 * D)
    e_sil, e_hid, e_hidT, e_y = ar(18096, 2 * FF), ar(18608, 2 * FF), ar(19120, 2 * FF), ar(19632, 2 * D)
    e_g = ar(4 * D, 4 * D)
    mod_raw = (ar(9 * D, 2 * BANK), ar(0, 2 * BANK))
    xn = [lambda t, o=o: ar(o + (t % 2) * D, D) for o in (0, 9728)]
    hT = [lambda t, o=o: ar(o + (2 + t % 2) * D, D) for o in (0, 9728)]

    def pbuf(h, n):
        return Pb[:, (h % 2) * LKEYS:(h % 2) * LKEYS + n]

    def ptbuf(h, n):
        return PT[:, (h % 2) * LKEYS:(h % 2) * LKEYS + n]

    def spair(h, n):
        return ps[:, (h % 2) * 2 * BANK:(h % 2) * 2 * BANK + n]

    def scores(h, keys):
        return split(spair(h, 2 * BANK), 2)[:, :, 0:keys // 2] if keys > P else split(spair(h, keys), 1)

    def oT_block(h):
        b = h // 2
        return ps[64 * (h % 2):64 * (h % 2) + 64, 6 * BANK + b * P:6 * BANK + (b + 1) * P]

    place, uses, order = {}, [0] * NSLOT, []

    def item(name):
        s = len(order) % NSLOT
        uses[s] += 1
        place[name] = (s, 32 * uses[s], len(order))
        order.append(name)

    def use_of(n):
        kind, l, t = order[n]
        if kind in ("gu", "dn"):
            return S("gu_done" if kind == "gu" else "y_done", l), t + 1
        if kind == "ada":
            return S("ada_made"), ADA_ITEMS * l + t + 1
        return S("ring_used"), sum(x[0] not in ("gu", "dn", "ada") for x in order[:n + 1])

    for l in range(2):
        for n in range(ADA_ITEMS) if l == 0 else range(ADA_SPLIT[1], ADA_ITEMS):
            item(("ada", l, n))
        for n in MATRICES[l]:
            item((n, l, 0))
        if l == 0:
            for n in range(ADA_SPLIT[1]):
                item(("ada", 1, n))
        for n in range(-len(order) % NSLOT):
            item(("pad", l, n))
        item(("gu", l, 0))
        for t in range(SLOT_TILES):
            if t + 1 < SLOT_TILES:
                item(("gu", l, t + 1))
            item(("dn", l, t))
        for n in range(-len(order) % NSLOT):
            item(("pad", 2 + l, n))

    def slot_of(name, cols):
        s = place[name][0]
        return ring[:, s * SLOT:s * SLOT + cols]

    def wait_landed(pe, name, more=0, less=0):
        s, v, _ = place[name]
        pe.wait_ge(S(f"ring_landed{s}"), more + (v - less))

    def rounds_needed(eng, l):
        eng.wait_ge(S("routed", l), 1)
        return eng.value_load(rounds[0:1, 0:1], min_val=1, max_val=ROUNDS)

    def tiles_before(l, it):
        return it + NTILE * l

    def meet(eng, n):
        eng.drain().then_inc(S("phase_over"), 1)
        eng.wait_ge(S("phase_over"), 4 * (n + 1))

    rows_of = {"dq": A["mla_w_dq"][0], "dkv": A["mla_w_dkv"][0], "uk": A["mla_w_uk"], "uv": A["mla_w_uv"],
               "uq": A["mla_w_uq"][0], "wo": A["mla_w_o"][0], "qkv": A["gqa_w_qkv"][0], "gwo": A["gqa_w_o"][0]}
    cols_of = {"dq": (QL, 0), "dkv": (KV, 0), "uk": (D, 0), "uv": (D, 0), "uq0": (768, 0), "uq1": (768, 768)}
    for n in (*MATRICES[0], *MATRICES[1]):
        cols_of.setdefault(n, (BANK, BANK * int(n[-1]) if n[-1].isdigit() else 0))

    inputs = [(const[:], A["const"]), (mod_vec[0:MODS, :], A["vec_m"]), (vecb[0:VB_END, :], A["vec_b"]),
              (X[:, 0:D], A["x_prompt"][0]), (split(X[:, D:], LAT), A["x_sample"][0].rearrange("(t p) n -> p t n", p=P)),
              (m_key[:, 0:KV], A["cache_mla"][0, 0]),
              (kvn_row[:], A["mla_kv_norm"][0:1, :].broadcast_to([P, KVL])),
              (qkn_row[:, 0:HD], A["gqa_q_norm"][0:1, :].broadcast_to([P, HD])),
              (qkn_row[:, HD:2 * HD], A["gqa_k_norm"][0:1, :].broadcast_to([P, HD]))]
    for l in range(2):
        inputs.append((rbias[:, l * NR:l * NR + NG], A["moe_b_group"][l:l + 1, :].broadcast_to([P, NG])))
        inputs.append((rbias[:, l * NR + NG:(l + 1) * NR], A["moe_b_expert"][l:l + 1, :].broadcast_to([P, NE])))

    block = ctx.enter_context(nc.Block())

    @block.sync
    def _(sp):
        def free(n):
            if n >= NSLOT and not (order[n - NSLOT][0] in ("gu", "dn") and order[n][0] not in ("gu", "dn")):
                sp.wait_ge(*use_of(n - NSLOT))

        def fill_slots(l, R):
            last = place[("dn", l, SLOT_TILES - 1)][2]
            for n in range(last - NSLOT + 1, last + 1):
                kind, _, t = order[n]
                sp.wait_ge(S("gu_done" if kind == "gu" else "y_done", l), R * 2 + (t - LOOPED + 1))
                sp.nop().then_inc(S("slots_used"), 1)
                with sp.Fori(0, ROUNDS) as i:
                    with sp.If(i >= R):
                        sp.nop().then_inc(S(f"ring_landed{n % NSLOT}"), 32)

        def load(name, src, cols, off):
            s, _, n = place[name]
            free(n)
            kk = src.shape[0] // P
            w = split(ring[:, s * SLOT:s * SLOT + kk * cols], kk)
            src = src.rearrange("(k p) n -> p k n", p=P)
            ha = (kk + 1) // 2
            sp.dma_start(w[:, 0:ha], src[:, 0:ha, off:off + cols]).then_inc(S(f"ring_landed{s}"), 16)
            sp.dma_start(w[:, ha:kk], src[:, ha:kk, off:off + cols]).then_inc(S(f"ring_landed{s}"), 16)

        def load_gu(l, t, e):
            s = place[("gu", l, t)][0]
            w = split(ring[:, s * SLOT:(s + 1) * SLOT], KD)
            for m, name in enumerate(("moe_w_gate", "moe_w_up")):
                src = A[name][l][ds(e, 1)].rearrange("e (k p) n -> p (e k) n", p=P)
                sp.dma_start(w[:, :, m * FF:(m + 1) * FF], src).then_inc(S(f"ring_landed{s}"), 16)

        def load_dn(l, t, e):
            s = place[("dn", l, t)][0]
            w = split(ring[:, s * SLOT:s * SLOT + 2 * D], 2)
            src = A["moe_w_down"][l][ds(e, 1)].rearrange("e (k p) n -> p (e k) n", p=P)
            for k in range(2):
                sp.dma_start(w[:, k:k + 1], src[:, k:k + 1]).then_inc(S(f"ring_landed{s}"), 16)

        def load_rows(l, t, u, used=None):
            if used is not None:
                sp.wait_ge(S("xs_used", l), used)
            sp.dma_start(e_xs[:, (u % 2) * D:(u % 2 + 1) * D], slots[ds(t * P, P), :]).then_inc(S(f"xs_landed{u % 2}", l), 16)

        def expert_of(t):
            return sp.value_load(expert[0:1, ds(t, 1)], min_val=0, max_val=NE - 1)

        def pads(l):
            for name in order:
                if name[0] == "pad" and name[1] == l:
                    s, _, n = place[name]
                    free(n)
                    sp.nop().then_inc(S(f"ring_landed{s}"), 32)

        for l in range(2):
            for n in range(ADA_ITEMS) if l == 0 else range(ADA_SPLIT[1], ADA_ITEMS):
                load(("ada", l, n), A["ada_w"][l], BANK, n * BANK)
            for n in MATRICES[l]:
                load((n, l, 0), rows_of[n.rstrip("012")], *cols_of[n])
            if l == 0:
                for n in range(ADA_SPLIT[1]):
                    load(("ada", 1, n), A["ada_w"][1], BANK, n * BANK)
            pads(l)
            R = rounds_needed(sp, l)
            sp.wait_ge(S("rows_scattered", l), 16 * 2 * NTILE)
            load_rows(l, 0, 0)
            load_rows(l, 1, 1)
            e = expert_of(0)
            if l == 0:
                sp.wait_ge(S("ada_made"), ADA_ITEMS + ADA_SPLIT[1])
            load_gu(l, 0, e)

            def turn(t, u, before=None):
                e, e_next = expert_of(t), expert_of(t + 1)
                if u:
                    sp.wait_ge(S("gu_done", l), t)
                load_gu(l, u + 1, e_next)
                if u + 2 < SLOT_TILES:
                    load_rows(l, t + 2, u, t + 1)
                if u >= 2:
                    sp.wait_ge(S("y_done", l), t - 1 if before is None else before)
                load_dn(l, u, e)

            for t in range(2):
                turn(t, t)
            with sp.Fori(1, ROUNDS) as i:
                with sp.If(i < R):
                    for u in range(2):
                        turn(i * 2 + u, u + 2)
            before = sp.value_load(rounds[0:1, 1:2], min_val=1, max_val=LOOPED - 1)
            for t in range(LOOPED, SLOT_TILES - 1):
                turn(R * 2 + (t - LOOPED), t, before if t == LOOPED else R * 2 + (t - LOOPED - 1))
            e = expert_of(R * 2 + (SLOT_TILES - 1 - LOOPED))
            sp.wait_ge(S("y_done", l), R * 2 + (SLOT_TILES - 2 - LOOPED))
            load_dn(l, SLOT_TILES - 1, e)
            fill_slots(l, R)
            pads(2 + l)
        for t in range(NTILE):
            sp.wait_ge(S("y_ready"), t + 1)
            dst = O[0][0] if t == 0 else O[1][0, (t - 1) * P:t * P, :]
            sp.dma_start(dst, e_h[:, t * D:(t + 1) * D]).then_inc(S("results_stored"), 16)
        sp.wait_ge(S("results_stored"), 16 * NTILE)

    @block.gpsimd
    def _(pool):
        pool.memset(zeros[:], 0.0).then_inc(S("zero_made"), 1)
        pool.wait_ge(S("zero_made"), 1)
        pool.wait_ge(S("ada_made"), ADA_ITEMS)
        for t in range(SLOT_TILES):
            pool.dma_start(split_rows(slots[t * P:(t + 1) * P, :]), bmid(zeros[:], KD)).then_inc(S("table_zeroed"), 16)
        pool.wait_ge(S("table_zeroed"), 16 * SLOT_TILES)
        pool.wait_ge(S("turned_out", 0), NKEYT)
        pool.wait_ge(S("state_stored", 0), 16)
        nc.gpsimd.tensor_copy(split(m_kT[64:96, :], HEADS), bmid(m_krT[64:96, :], HEADS)).then_inc(S("rope_keys"), 1)
        for l in range(2):
            meet(pool, 2 * l)
            pool.wait_ge(S("routed", l), 1)
            for t in range(NTILE):
                for c in range(2):
                    pool.indirect_dma_start(
                        slots, bass.IndirectOffsetOnAxis(ap=slot_i[:, 2 * t + c:2 * t + c + 1], axis=0),
                        e_h[:, t * D:(t + 1) * D], None).then_inc(S("rows_scattered", l), 16)
            pool.wait_ge(S("rows_scattered", l), 16 * 2 * NTILE)
            pool.wait_ge(S("last_stored"), 32 * (l + 1))
            for t in range(NTILE):
                if t >= 2:
                    pool.wait_ge(S("combined", l), t - 1)
                for c in range(2):
                    pool.indirect_dma_start(
                        e_g[:, (2 * (t % 2) + c) * D:(2 * (t % 2) + c + 1) * D], None, slots,
                        bass.IndirectOffsetOnAxis(ap=slot_i[:, 2 * t + c:2 * t + c + 1], axis=0))\
                        .then_inc(S(f"gathered{t % 2}", l), 16)
            meet(pool, 2 * l + 1)

    @block.scalar
    def _(act):
        for dst, src in inputs:
            act.dma_start(dst, src).then_inc(S("inputs"), 16)
        act.wait_ge(S("cols_ready"), 1)
        act.activation(cond[:], colb[:, VB_COND:VB_COND + 2 * KD], ACT.Silu).then_inc(S("cond_ready"), 1)

        def squares(name, junk):
            for t in range(NTILE):
                act.activation(junk, xt(t), ACT.Square, accum_out=ssq[:, t:t + 1]).then_inc(S(f"{name}_squared"), 1)
                act.drain()
            act.wait_ge(S(f"{name}_mean"), 1)
            act.activation(st[:, NTILE:], st[:, 0:NTILE], ACT.Sqrt).then_inc(S(f"{name}_root"), 1)

        def mod_out(l, a, b):
            for n in range(a, b):
                act.wait_ge(S("ada_made"), ADA_ITEMS * l + n + 1)
                if n >= 2 or l:
                    act.wait_ge(S(f"mod_raw_out{n % 2}"), 16 * ((ADA_ITEMS * l + n) // 2))
                raw = mod_raw[l][0:2, (n % 2) * BANK:(n % 2 + 1) * BANK]
                act.activation(raw, bank(4 + n % 2)[0:2, :], ACT.Copy).then_inc(S("ada_out"), 1)
                act.wait_ge(S("ada_out"), ADA_ITEMS * l + n + 1)
                act.dma_start(modraw[l][:, n * BANK:(n + 1) * BANK], raw).then_inc(S(f"mod_raw_out{n % 2}"), 16)

        def mod_rows(l):
            for b in range(2):
                act.wait_ge(S(f"mod_raw_out{b}"), 16 * ADA_ITEMS // 2 * (l + 1))
            act.dma_start(modt[0:MODS, :], modraw[l].rearrange("v (k p) -> (v k) p", p=P)).then_inc(S("mod_landed", l), 16)
            act.wait_ge(S("mod_ready", l), 1)
            act.dma_start(modrow[l].rearrange("v c (k p) -> (v c k) p", p=P), modt[0:MODS, :]).then_inc(S("mod_stored", l), 16)
            act.wait_ge(S("mod_stored", l), 16)
            for v in range(2):
                act.dma_start(gate_rows[:, v * D:(v + 1) * D], modrow[l][v, 2:3, :].broadcast_to([P, D]))\
                    .then_inc(S("gates_a", l), 16)

        def heads(l, it, keys, before_end=None):
            past = tiles_before(l, it)

            def out(half):
                act.wait_ge(S("pv_done"), past * HEADS + (half + 1) * 8)
                act.activation(oT[:, half * BANK:(half + 1) * BANK], bank(6 + half), ACT.Copy).then_inc(S("oT_ready"), 1)

            for h in range(HEADS):
                act.wait_ge(S("max_ready"), past * HEADS + h + 1)
                if h >= 2:
                    act.wait_ge(S("p_turned"), past * HEADS + h - 1)
                act.activation(split(pbuf(h, keys), 2 if keys > P else 1), scores(h, keys), ACT.Exp, bias=hst[:, h:h + 1],
                               accum_out=hsum[:, h:h + 1]).then_inc(S("exp_ready"), 1)
                if h == 12:
                    out(0)
                if h == 13 and before_end:
                    before_end()
            out(1)

        def experts(l):
            for v in range(2):
                act.dma_start(gate_rows[:, v * D:(v + 1) * D], modrow[l][v, 5:6, :].broadcast_to([P, D]))\
                    .then_inc(S("rows_e", l), 16)
                for n, c in ((0, 4), (1, 3)):
                    act.dma_start(e_row[:, (2 * v + n) * D:(2 * v + n + 1) * D], modrow[l][v, c:c + 1, :].broadcast_to([P, D]))\
                        .then_inc(S("rows_e", l), 16)
            act.dma_start(split(rw[:], KD)[:, :, 0:NG], A["moe_w_group"][l].rearrange("(k p) n -> p k n", p=P))\
                .then_inc(S("router_landed", l), 16)
            act.dma_start(split(rw[:], KD)[:, :, NG:NR], A["moe_w_expert"][l].rearrange("(k p) n -> p k n", p=P))\
                .then_inc(S("router_landed", l), 16)
            squares(f"ffn{l}", e_junk)
            for t in range(NTILE):
                act.wait_ge(S("h_turned", l), t + 1)
                if t >= 2:
                    act.wait_ge(S("logits", l), t - 1)
                act.activation(e_hT[:, (t % 2) * D:(t % 2 + 1) * D], ps[:, 0:D], ACT.Copy).then_inc(S("hT_out", l), 1)
            if l == 0:
                mod_out(1, 0, ADA_SPLIT[0])
            act.wait_ge(S("shifted", l), 1)
            act.activation(r_ex, r_sh, ACT.Exp).then_inc(S("r_exp", l), 1)
            if l == 0:
                mod_out(1, *ADA_SPLIT)

            def sil(t, u):
                act.wait_ge(S("gu_done", l), t + 1)
                act.activation(e_sil[:, (u % 2) * FF:(u % 2 + 1) * FF], bank(2 + u % 2, FF), ACT.Silu).then_inc(S("sil_ready", l), 1)

            def y_out(t, u, r, last=False):
                act.wait_ge(S("y_done", l), t + 1)
                act.wait_ge(S(f"y_stored{u % 2}", l), r * 16 + 16)
                y = e_y[:, (u % 2) * D:(u % 2 + 1) * D]
                act.activation(y, ps[:, 6 * BANK:8 * BANK], ACT.Copy).then_inc(S("y_out", l), 1)
                act.wait_ge(S("y_out", l), t + 2)
                stored = S("last_stored") if last else S(f"y_stored{u % 2}", l)
                act.dma_start(slots[ds(t * P, P), :], y).then_inc(stored, 16)

            act.drain().then_inc(S("y_out", l), 1)
            for b in range(2):
                act.drain().then_inc(S(f"y_stored{b}", l), 16)
            R = rounds_needed(act, l)
            sil(0, 0)
            with act.Fori(0, ROUNDS) as i:
                with act.If(i < R):
                    for u in range(2):
                        sil(i * 2 + (u + 1), u + 1)
                        y_out(i * 2 + u, u, i)
            for k in range(SLOT_TILES - LOOPED):
                if k + 1 < SLOT_TILES - LOOPED:
                    sil(R * 2 + (k + 1), k + 1)
                y_out(R * 2 + k, k, R + k // 2, k >= SLOT_TILES - LOOPED - 2)

        r_sh, r_ex = e_r[:, R_SH:R_SH + NTILE * (NG + 1)], e_r[:, R_EX:R_EX + NTILE * (NG + 1)]

        act.wait_ge(S("inputs"), 16 * len(inputs))
        squares("mix0", m_junk)

        def turned_m(t):
            j = t if t > 0 else 5 if t == 0 else 0
            act.wait_ge(S("turned", 0), t + 2)
            if t >= 0:
                for m in range(3):
                    act.activation(m_qlT[:, m * TOK + t * P:m * TOK + (t + 1) * P], bank(4, P, m * P), ACT.Identity,
                                   scale=colb[:, VB_QN + m:VB_QN + m + 1])
            act.activation(split(m_ckvT, 2)[:, :, j * P:(j + 1) * P], split(bank(5, 2 * P), 2), ACT.Copy)
            act.activation(m_krT[64:96, j * P:(j + 1) * P], ps[0:ROPE, 5 * BANK + 2 * P:5 * BANK + 3 * P], ACT.Copy)\
                .then_inc(S("turned_out", 0), 1)

        mod_out(0, 0, ADA_ITEMS)
        mod_rows(0)
        turned_m(-1)
        for t in range(NTILE):
            act.wait_ge(S("projected", 0), t + 1)
            act.activation(m_junk[:, 0:QL], bank(2, QL), ACT.Square, accum_out=pst[:, 0:1])
            act.activation(m_junk[:, QL:QL + KVL], bank(3, KVL), ACT.Square, accum_out=pst[:, 1:2]).then_inc(S("proj_squared", 0), 1)
            act.wait_ge(S("proj_mean", 0), t + 1)
            act.activation(pst[:, 4:6], pst[:, 2:4], ACT.Sqrt).then_inc(S("proj_root", 0), 1)
            if t == 0:
                act.wait_ge(S("proj_out", 0), 1)
                act.dma_start(O[2][0, 0], m_key[:, 5 * KV:6 * KV]).then_inc(S("state_stored", 0), 16)
            else:
                turned_m(t - 1)
        turned_m(NTILE - 1)
        act.wait_ge(S("state_stored", 0), 16)
        for m in range(HEADS // 2):
            act.wait_ge(S("k_made"), m + 1)
            act.activation(m_kT[0:64, 2 * m * KEYS:(2 * m + 1) * KEYS], spair(m, KEYS)[0:64], ACT.Copy).then_inc(S("k_even"), 1)
        for j in range(0, NKEYT, 2):
            act.wait_ge(S("v_made"), j + 1)
            act.activation(m_V[:, j * D:(j + 1) * D], ps[:, 4 * BANK:6 * BANK], ACT.Copy).then_inc(S("v_even"), 1)
        act.wait_ge(S("rope_keys"), 1)

        def ql(it):
            act.activation(split(qls, 3), split(m_qlT, 3)[:, :, ds(it * P, P)], ACT.Copy).then_inc(S("ql_ready"), 1)

        def q_stage(it):
            act.wait_ge(S("q_made"), it + 1)
            act.activation(split(q_tok, 4), split(ps[:, 0:4 * BANK], 4)[:, :, 0:4 * QD], ACT.Copy, scale=SCALE[0])\
                .then_inc(S("q_out"), 1)
            act.wait_ge(S("q_turned"), it + 1)
            act.activation(qT[0:QD, 0:D], ps[0:QD, 0:D], ACT.Copy).then_inc(S("q_ready", 0), 1)

        ql(0)
        q_stage(0)
        heads(0, 0, P, lambda: ql(1))
        q_stage(1)
        with act.Fori(0, LAT - 1) as i:
            heads(0, i + 1, LKEYS, lambda: ql(i + 2))
            q_stage(i + 2)
        heads(0, LAT, LKEYS)
        meet(act, 0)
        experts(0)
        mod_out(1, ADA_SPLIT[1], ADA_ITEMS)
        mod_rows(1)
        meet(act, 1)

        act.dma_start(g_V[:, 0:NK], A["cache_gqa"][0, 0, :, 1].rearrange("t h d -> t (h d)")).then_inc(S("cache_landed"), 16)
        act.dma_start(g_cache, A["cache_gqa"][0, 0, :, 0].rearrange("t h d -> t (h d)")).then_inc(S("cache_landed"), 16)
        squares("mix1", g_junk)

        def turned_g(t):
            j = t if t > 0 else 5 if t == 0 else 0
            act.wait_ge(S("turned", 1), t + 2)
            if t >= 0:
                act.activation(split(g_qT, 8)[:, :, t * P:(t + 1) * P], split(ps[:, 5 * BANK:7 * BANK], 8), ACT.Copy,
                               scale=SCALE[1])
            for half in range(2):
                last = act.activation(split(g_kT[half * HD:(half + 1) * HD, :], KVH)[:, :, j * P:(j + 1) * P],
                                      split(bank(7)[0:HD, :], KVH), ACT.Copy)
            last.then_inc(S("turned_out", 1), 1)

        turned_g(-1)
        for t in range(NTILE):
            act.wait_ge(S("projected", 1), t + 1)
            if t >= 2:
                act.wait_ge(S("turned", 1), t)
            act.activation(g_qk[:, (t % 2) * (NQ + NK):(t % 2 + 1) * (NQ + NK)], ps[:, 2 * BANK:2 * BANK + NQ + NK], ACT.Copy)
            j = t if t > 0 else 5
            act.activation(g_V[:, j * NK:(j + 1) * NK], bank(4, NK, NK), ACT.Copy).then_inc(S("proj_out", 1), 1)
            act.wait_ge(S("proj_mean", 1), t + 1)
            act.activation(pst[:, 40:60], pst[:, 20:40], ACT.Sqrt).then_inc(S("proj_root", 1), 1)
            if t == 0:
                act.wait_ge(S("qk_ready"), 1)
                act.dma_start(O[3][0, 0, :, 0].rearrange("t h d -> t (h d)"), g_qk[:, NQ:NQ + NK]).then_inc(S("state_stored", 1), 16)
                act.wait_ge(S("proj_out", 1), 1)
                act.dma_start(O[3][0, 0, :, 1].rearrange("t h d -> t (h d)"), g_V[:, 5 * NK:6 * NK]).then_inc(S("state_stored", 1), 16)
            else:
                turned_g(t - 1)
                if t == 1:
                    act.wait_ge(S("state_stored", 1), 32)
        turned_g(NTILE - 1)

        def q_stage_g(it):
            act.activation(split(qT[:, 0:D], 8), split(g_qT, 8)[:, :, ds(it * P, P)], ACT.Copy).then_inc(S("q_ready", 1), 1)

        act.wait_ge(S("turned_out", 1), NKEYT)
        q_stage_g(0)
        heads(1, 0, P)
        q_stage_g(1)
        with act.Fori(0, LAT - 1) as i:
            heads(1, i + 1, LKEYS)
            q_stage_g(i + 2)
        heads(1, LAT, LKEYS)
        meet(act, 2)
        experts(1)
        meet(act, 3)
        act.dma_start(e_row[:, 0:D], A["final_norm"].unsqueeze(0).broadcast_to([P, D])).then_inc(S("final_landed"), 16)
        squares("end", e_junk)

    @block.vector
    def _(dve):
        def settle():
            dve.drain()

        dve.wait_ge(S("cols_turned"), 1)
        nc.vector.tensor_copy(colb[:], bank(7, VB_END)).then_inc(S("cols_ready"), 1)

        def modulation(l):
            dve.wait_ge(S("mod_landed", l), 16)
            m = modt[0:MODS, :]
            nc.vector.tensor_tensor(m, m, mod_vec[0:MODS, l * P:(l + 1) * P], ALU.add)
            settle()
            nc.vector.scalar_tensor_tensor(m, m, const[0:MODS, C_SEL:C_SEL + 1], mod_vec[0:MODS, (2 + l) * P:(3 + l) * P],
                                           ALU.add, ALU.mult).then_inc(S("mod_ready", l), 1)
            dve.wait_ge(S("mod_turned", l), 1)
            nc.vector.tensor_copy(modc[:, 96 * l:96 * (l + 1)], bank(6, MODS)).then_inc(S("mod_cols", l), 1)
            settle()

        def row_stats(name):
            dve.wait_ge(S(f"{name}_squared"), NTILE)
            nc.vector.tensor_scalar(st[:, 0:NTILE], ssq[:], 1.0 / D, EPS, ALU.mult, ALU.add).then_inc(S(f"{name}_mean"), 1)
            dve.wait_ge(S(f"{name}_root"), 1)
            nc.vector.reciprocal(rstd[:], st[:, NTILE:])
            settle()

        def norm(l, t):
            if t >= 2:
                dve.wait_ge(S("n_turned", l), t - 1)
            nc.vector.tensor_scalar(xn[l](t), xt(t), rstd[:, t:t + 1], None, ALU.mult).then_inc(S("xn_ready", l), 1)

        def mod_cols(l, t):
            v = 0 if t == 0 else 1
            dve.wait_ge(S("n_turned", l), t + 1)
            if t >= 2:
                dve.wait_ge(S("projected", l), t - 1)
            for k in range(KD):
                at = 96 * l + 48 * v + k
                last = nc.vector.tensor_scalar(hT[l](t)[:, k * P:(k + 1) * P], ps[:, k * P:(k + 1) * P],
                                               modc[:, at + 8:at + 9], modc[:, at:at + 1], ALU.mult, ALU.add)
            last.then_inc(S("hT_ready", l), 1)

        def rope(out0, out1, cs, sn):
            nc.vector.tensor_tensor(out0, cs[..., 0], sn[..., 1], ALU.subtract)
            return nc.vector.tensor_tensor(out1, sn[..., 0], cs[..., 1], ALU.add)

        def residual(l, it, kind):
            dve.wait_ge(S("mixed"), tiles_before(l, it) + 1)
            mix = ps[:, 6 * BANK:8 * BANK]
            nc.vector.tensor_tensor(mix, mix, gate_rows[:, kind * D:(kind + 1) * D], ALU.mult)
            settle()
            nc.vector.tensor_tensor(xt(it), xt(it), mix, ALU.add).then_inc(S("mix_out"), 1)

        def heads(l, it, keys, last_mix=None):
            past = tiles_before(l, it)
            for h in range(HEADS + 2):
                if h == 2 and last_mix:
                    last_mix()
                if h < HEADS:
                    dve.wait_ge(S("scored"), past * HEADS + h + 1)
                    nc.vector.tensor_reduce(hst[:, h:h + 1], scores(h, keys), AX.XY, ALU.max, negate=True)\
                        .then_inc(S("max_ready"), 1)
                if 0 <= h - 1 < HEADS:
                    j = h - 1
                    dve.wait_ge(S("exp_ready"), past * HEADS + j + 1)
                    nc.vector.reciprocal(hinv[:, j:j + 1], hsum[:, j:j + 1])
                    settle()
                    nc.vector.tensor_scalar(pbuf(j, keys), pbuf(j, keys), hinv[:, j:j + 1], None, ALU.mult)\
                        .then_inc(S("p_ready"), 1)
                if h >= 2:
                    j = h - 2
                    dve.wait_ge(S("p_turned"), past * HEADS + j + 1)
                    if j >= 2:
                        dve.wait_ge(S("pv_done"), past * HEADS + j - 1)
                    nc.vector.tensor_copy(ptbuf(j, keys), ps[:, 4 * BANK:4 * BANK + keys]).then_inc(S("pt_ready"), 1)

        dve.wait_ge(S("inputs"), 16 * len(inputs))
        row_stats("mix0")
        modulation(0)

        def post_m(t):
            dve.wait_ge(S("proj_squared", 0), t + 1)
            nc.vector.tensor_scalar(pst[:, 2:3], pst[:, 0:1], 1.0 / QL, EPS, ALU.mult, ALU.add)
            nc.vector.tensor_scalar(pst[:, 3:4], pst[:, 1:2], 1.0 / KVL, EPS, ALU.mult, ALU.add).then_inc(S("proj_mean", 0), 1)
            dve.wait_ge(S("proj_root", 0), t + 1)
            nc.vector.reciprocal(pst[:, 6:8], pst[:, 4:6])
            settle()
            if t >= 2:
                dve.wait_ge(S("turned", 0), t)
            j = t if t > 0 else 5
            key = m_key[:, j * KV:(j + 1) * KV]
            nc.vector.tensor_scalar(m_ql[:, (t % 2) * QL:(t % 2 + 1) * QL], bank(2, QL), pst[:, 6:7], None, ALU.mult)
            nc.vector.scalar_tensor_tensor(key[:, 0:KVL], bank(3, KVL), pst[:, 7:8], kvn_row[:], ALU.mult, ALU.mult)
            pe_ = bank(3, ROPE, KVL)
            if t == 0:
                nc.vector.tensor_copy(key[:, KVL:KV], pe_).then_inc(S("proj_out", 0), 1)
            else:
                cs, sn = m_rope[:, 0:ROPE], m_rope[:, ROPE:2 * ROPE]
                at = (t - 1) * ROPE
                nc.vector.tensor_tensor(cs, pe_, const[:, C_CM + at:C_CM + at + ROPE], ALU.mult)
                nc.vector.tensor_tensor(sn, pe_, const[:, C_SM + at:C_SM + at + ROPE], ALU.mult)
                settle()
                out = split(key[:, KVL:KV], ROPE // 2)
                rope(out[..., 0], out[..., 1], split(cs, ROPE // 2), split(sn, ROPE // 2)).then_inc(S("proj_out", 0), 1)
            settle()

        def post_g(t):
            W = NQ + NK
            qk = g_qk[:, (t % 2) * W:(t % 2 + 1) * W]
            heads_ = HEADS + KVH
            dve.wait_ge(S("proj_out", 1), t + 1)
            nc.vector.tensor_tensor(g_a, qk, qk, ALU.mult)
            settle()
            nc.vector.tensor_reduce(pst[:, 0:20], split(g_a, heads_), AX.X, ALU.add)
            settle()
            nc.vector.tensor_scalar(pst[:, 20:40], pst[:, 0:20], 1.0 / HD, EPS, ALU.mult, ALU.add).then_inc(S("proj_mean", 1), 1)
            dve.wait_ge(S("proj_root", 1), t + 1)
            nc.vector.reciprocal(pst[:, 0:20], pst[:, 40:60])
            settle()
            nc.vector.tensor_tensor(split(qk, heads_), split(qk, heads_), blast(pst[:, 0:20], HD), ALU.mult)
            settle()
            nc.vector.tensor_tensor(split(qk[:, 0:NQ], HEADS), split(qk[:, 0:NQ], HEADS), bmid(qkn_row[:, 0:HD], HEADS), ALU.mult)
            last = nc.vector.tensor_tensor(split(qk[:, NQ:W], KVH), split(qk[:, NQ:W], KVH), bmid(qkn_row[:, HD:2 * HD], KVH),
                                           ALU.mult)
            if t > 0:
                at = (t - 1) * HD
                settle()
                nc.vector.tensor_tensor(split(g_a, heads_), split(qk, heads_), bmid(const[:, C_CG + at:C_CG + at + HD], heads_), ALU.mult)
                nc.vector.tensor_tensor(split(g_b, heads_), split(qk, heads_), bmid(const[:, C_SG + at:C_SG + at + HD], heads_), ALU.mult)
                settle()
                out = split(qk, W // 2)
                last = rope(out[..., 0], out[..., 1], split(g_a, W // 2), split(g_b, W // 2))
            last.then_inc(S("qk_ready"), 1)
            settle()

        def projection(l, post):
            norm(l, 0)
            norm(l, 1)
            mod_cols(l, 0)
            for t in range(NTILE):
                if t + 2 < NTILE:
                    norm(l, t + 2)
                if t + 1 < NTILE:
                    mod_cols(l, t + 1)
                post(t)

        projection(0, post_m)
        dve.wait_ge(S("state_stored", 0), 16)
        for m in range(HEADS // 2):
            dve.wait_ge(S("k_made"), m + 1)
            nc.vector.tensor_copy(m_kT[0:64, (2 * m + 1) * KEYS:(2 * m + 2) * KEYS], spair(m, KEYS)[64:128]).then_inc(S("k_odd"), 1)
        for j in range(1, NKEYT, 2):
            dve.wait_ge(S("v_made"), j + 1)
            nc.vector.tensor_copy(m_V[:, j * D:(j + 1) * D], ps[:, 6 * BANK:8 * BANK]).then_inc(S("v_odd"), 1)
        dve.wait_ge(S("gates_a", 0), 32)
        dve.wait_ge(S("rope_keys"), 1)

        def q_stage(it):
            if not isinstance(it, int) or it:
                dve.wait_ge(S("q_out"), it + 1)
                pe_ = split(q_tok, HEADS)[:, :, NOPE:QD]
                cos = const[:, ds(it * ROPE + (C_CM - ROPE), ROPE)]
                sin = const[:, ds(it * ROPE + (C_SM - ROPE), ROPE)]
                nc.vector.tensor_tensor(split(q_cos, HEADS), pe_, bmid(cos, HEADS), ALU.mult)
                nc.vector.tensor_tensor(split(q_sin, HEADS), pe_, bmid(sin, HEADS), ALU.mult)
                settle()
                out = pe_.rearrange("p h (r two) -> p h r two", two=2)
                cs = q_cos.rearrange("p (h r two) -> p h r two", h=HEADS, two=2)
                sn = q_sin.rearrange("p (h r two) -> p h r two", h=HEADS, two=2)
                rope(out[..., 0], out[..., 1], cs, sn).then_inc(S("q_roped"), 1)
            dve.wait_ge(S("q_turned"), it + 1)
            nc.vector.tensor_copy(qT[0:QD, D:2 * D], ps[0:QD, D:2 * D]).then_inc(S("q_ready", 0), 1)

        def attend(l, stage):
            stage(0)
            heads(l, 0, P)
            stage(1)
            heads(l, 1, LKEYS, lambda: residual(l, 0, 0))
            with dve.Fori(1, LAT) as i:
                stage(i + 1)
                heads(l, i + 1, LKEYS, lambda: residual(l, i, 1))
            residual(l, LAT, 1)

        attend(0, q_stage)
        meet(dve, 0)

        def routing(l):
            r4 = const[:, C_R4:C_R4 + NG]
            n = [R_FREE]

            def new(cols):
                n[0] += cols
                return e_r[:, n[0] - cols:n[0]]

            def op(ins):
                settle()
                return ins

            T5 = NTILE
            lg, le = new(T5 * NG), new(T5 * NE)
            sc4, t80, ein, e2 = new(T5 * NG), new(T5 * NE), new(T5 * EPG), new(T5 * EPG)
            gm, m1, m2, mx = new(T5), new(T5), new(T5), new(T5)
            og, o1, o2 = new(T5 * NG), new(T5 * EPG), new(T5 * EPG)
            M1, M2, M = new(T5 * NE), new(T5 * NE), new(T5 * NE)
            den, gw = new(T5), new(T5)
            cnt, nt, cs, c2 = new(NE), new(NE), new(NE), new(NE)
            te, te1 = new(SLOT_TILES * NE), new(SLOT_TILES)
            place_ = new(2 * T5)
            rank = new(T5 * NE)
            need, rnd = new(ROUNDS), new(1)
            assert n[0] <= 1600, n[0]
            sh, ex = e_r[:, R_SH:R_SH + T5 * (NG + 1)], e_r[:, R_EX:R_EX + T5 * (NG + 1)]
            dve.wait_ge(S("logits", l), T5)
            lo = split(bank(2, T5 * 32), T5)
            nc.vector.tensor_tensor(split(lg, T5), lo[:, :, 0:NG], bmid(rbias[:, l * NR:l * NR + NG], T5), ALU.add)
            op(nc.vector.tensor_tensor(split(le, T5), lo[:, :, NG:NR], bmid(rbias[:, l * NR + NG:(l + 1) * NR], T5), ALU.add))

            def first_max(oh, v, m):
                op(nc.vector.tensor_reduce(m, split(v, T5), AX.X, ALU.max))
                op(nc.vector.tensor_tensor(split(sc4, T5), split(v, T5), blast(m, NG), ALU.is_equal))
                op(nc.vector.tensor_tensor(split(sc4, T5), split(sc4, T5), bmid(r4, T5), ALU.mult))
                op(nc.vector.tensor_reduce(mx, split(sc4, T5), AX.X, ALU.max))
                op(nc.vector.tensor_tensor(split(oh, T5), split(sc4, T5), blast(mx, NG), ALU.is_equal))

            first_max(og, lg, gm)
            nc.vector.tensor_tensor(split(sh[:, 0:T5 * NG], T5), split(lg, T5), blast(gm, NG), ALU.subtract)
            op(nc.vector.tensor_tensor(t80.rearrange("p (x j) -> p x j", j=EPG), le.rearrange("p (x j) -> p x j", j=EPG),
                                       blast(og, EPG), ALU.mult))
            op(nc.vector.tensor_reduce(split(ein, T5), t80.rearrange("p (t g j) -> p t j g", t=T5, g=NG), AX.X, ALU.add))
            first_max(o1, ein, m1)
            op(nc.vector.scalar_tensor_tensor(e2, o1, MASKED, ein, ALU.mult, ALU.add))
            first_max(o2, e2, m2)
            nc.vector.tensor_tensor(sh[:, T5 * NG:], m2, m1, ALU.subtract).then_inc(S("shifted", l), 1)
            for oh, m in ((o1, M1), (o2, M2)):
                for g in range(NG):
                    nc.vector.tensor_tensor(m.rearrange("p (t g j) -> p t g j", t=T5, g=NG)[:, :, g], split(oh, T5),
                                            blast(split(og, T5)[:, :, g], EPG), ALU.mult)
            settle()
            nc.vector.tensor_tensor(M, M1, M2, ALU.add).then_inc(S("picked", l), 1)
            dve.wait_ge(S("ranked", l), 1)
            op(nc.vector.tensor_copy(rank, bank(3, T5 * NE)))
            nc.vector.tensor_copy(cnt, bank(3, NE, T5 * NE))
            for t in range(1, T5):
                settle()
                nc.vector.tensor_tensor(rank[:, t * NE:(t + 1) * NE], rank[:, t * NE:(t + 1) * NE], cnt, ALU.add)
                settle()
                nc.vector.tensor_tensor(cnt, cnt, bank(3, NE, (T5 + t) * NE), ALU.add)
            settle()
            op(nc.vector.tensor_scalar(nt, cnt, 0.0, None, ALU.is_gt))
            for k in range(1, NTILE):
                op(nc.vector.scalar_tensor_tensor(nt, cnt, float(k * P), nt, ALU.is_gt, ALU.add))
            src = nt
            for k, dst in ((1, cs), (2, c2), (4, cs), (8, c2)):
                nc.vector.tensor_copy(dst[:, 0:k], src[:, 0:k])
                op(nc.vector.tensor_tensor(dst[:, k:NE], src[:, k:NE], src[:, 0:NE - k], ALU.add))
                src = dst
            nc.vector.tensor_tensor(split(te, SLOT_TILES), blast(const[:, C_TI:C_TI + SLOT_TILES], NE), bmid(c2, SLOT_TILES),
                                    ALU.is_ge)
            op(nc.vector.tensor_tensor(cs, c2, nt, ALU.subtract))
            nc.vector.tensor_scalar(need, const[:, C_RND:C_RND + ROUNDS], c2[:, NE - 1:NE], None, ALU.is_lt)
            nc.vector.tensor_reduce(te1, split(te, SLOT_TILES), AX.X, ALU.add)
            op(nc.vector.tensor_scalar(cs, cs, float(P), None, ALU.mult))
            op(nc.vector.tensor_tensor(split(t80, T5), split(rank, T5), bmid(cs, T5), ALU.add))
            op(nc.vector.tensor_tensor(M1, M1, t80, ALU.mult))
            nc.vector.tensor_tensor(M2, M2, t80, ALU.mult)
            sl = place_.rearrange("p (t c) -> p c t", c=2)
            settle()
            nc.vector.tensor_reduce(sl[:, 0], split(M1, T5), AX.X, ALU.add)
            nc.vector.tensor_reduce(sl[:, 1], split(M2, T5), AX.X, ALU.add)
            nc.vector.tensor_reduce(rnd, need, AX.X, ALU.add)
            op(nc.vector.tensor_scalar(te1, te1, float(NE - 1), None, ALU.min))
            nc.vector.tensor_copy(slot_i[:], place_)
            nc.vector.tensor_copy(rounds[:, 0:1], rnd)
            nc.vector.tensor_scalar(rounds[:, 1:2], rnd, 2.0, -1.0, ALU.mult, ALU.add)
            nc.vector.tensor_copy(expert[:], te1).then_inc(S("routed", l), 1)
            dve.wait_ge(S("r_exp", l), 1)
            op(nc.vector.tensor_reduce(den, split(ex[:, 0:T5 * NG], T5), AX.X, ALU.add))
            op(nc.vector.scalar_tensor_tensor(den, ex[:, T5 * NG:], 1.0, den, ALU.add, ALU.mult))
            op(nc.vector.reciprocal(w_pair[:, 0:T5], den))
            op(nc.vector.tensor_tensor(w_pair[:, T5:], w_pair[:, 0:T5], ex[:, T5 * NG:], ALU.mult))

        w_pair = e_r[:, R_W:R_W + 2 * NTILE]

        def experts(l):
            row_stats(f"ffn{l}")
            dve.wait_ge(S("rows_e", l), 16 * 6)
            for t in range(NTILE):
                v = 0 if t == 0 else 1
                h = e_h[:, t * D:(t + 1) * D]
                nc.vector.scalar_tensor_tensor(h, xt(t), rstd[:, t:t + 1], e_row[:, 2 * v * D:(2 * v + 1) * D], ALU.mult, ALU.mult)
                settle()
                nc.vector.tensor_tensor(h, h, e_row[:, (2 * v + 1) * D:(2 * v + 2) * D], ALU.add).then_inc(S("h_ready", l), 1)
            routing(l)

            def xsT(t, u):
                dve.wait_ge(S("xs_used", l), t + 1)
                nc.vector.tensor_copy(e_xsT[:, (u % 2) * D:(u % 2 + 1) * D], ps[:, 0:D]).then_inc(S("xsT_ready", l), 1)

            def hid(t, u):
                dve.wait_ge(S("sil_ready", l), t + 1)
                c = slice((u % 2) * FF, (u % 2 + 1) * FF)
                nc.vector.tensor_tensor(e_hid[:, c], bank(2 + u % 2, FF, FF), e_sil[:, c], ALU.mult).then_inc(S("hid_ready", l), 1)

            def hidT(t, u):
                dve.wait_ge(S("hid_turned", l), t + 1)
                nc.vector.tensor_copy(e_hidT[:, (u % 2) * FF:(u % 2 + 1) * FF], bank(4, FF)).then_inc(S("hidT_ready", l), 1)

            xsT(0, 0)
            hid(0, 0)
            xsT(1, 1)
            R = rounds_needed(dve, l)
            with dve.Fori(0, ROUNDS) as i:
                with dve.If(i < R):
                    for u in range(2):
                        hidT(i * 2 + u, u)
                        xsT(i * 2 + (u + 2), u)
                        hid(i * 2 + (u + 1), u + 1)
            for k in range(SLOT_TILES - LOOPED):
                hidT(R * 2 + k, k)
                if k + 2 < SLOT_TILES - LOOPED:
                    xsT(R * 2 + (k + 2), k)
                if k + 1 < SLOT_TILES - LOOPED:
                    hid(R * 2 + (k + 1), k + 1)
            for t in range(NTILE):
                dve.wait_ge(S(f"gathered{t % 2}", l), 32 * (t // 2 + 1))
                a, b = (e_g[:, (2 * (t % 2) + c) * D:(2 * (t % 2) + c + 1) * D] for c in range(2))
                v = 0 if t == 0 else 1
                nc.vector.tensor_scalar(a, a, w_pair[:, t:t + 1], None, ALU.mult)
                settle()
                nc.vector.scalar_tensor_tensor(a, b, w_pair[:, NTILE + t:NTILE + t + 1], a, ALU.mult, ALU.add)
                settle()
                nc.vector.tensor_tensor(a, a, gate_rows[:, v * D:(v + 1) * D], ALU.mult)
                settle()
                nc.vector.tensor_tensor(xt(t), xt(t), a, ALU.add).then_inc(S("combined", l), 1)

        experts(0)
        modulation(1)
        meet(dve, 1)
        row_stats("mix1")
        projection(1, post_g)
        dve.wait_ge(S("gates_a", 1), 32)
        attend(1, lambda it: None)
        meet(dve, 2)
        experts(1)
        meet(dve, 3)
        row_stats("end")
        dve.wait_ge(S("final_landed"), 16)
        for t in range(NTILE):
            nc.vector.scalar_tensor_tensor(e_h[:, t * D:(t + 1) * D], xt(t), rstd[:, t:t + 1], e_row[:, 0:D], ALU.mult, ALU.mult)\
                .then_inc(S("y_ready"), 1)

    @block.tensor
    def _(pe):
        mm = nc.tensor.matmul

        def turn(out, in_, rows=P):
            return nc.tensor.transpose(out, in_, ident[0:rows, 0:rows])

        pe.wait_ge(S("inputs"), 16 * len(inputs))
        turn(bank(7, VB_END), vecb[0:VB_END, :], VB_END).then_inc(S("cols_turned"), 1)

        def ada(l, a, b):
            c = cond[:].rearrange("p (v k) -> p k v", v=2)
            for n in range(a, b):
                wait_landed(pe, ("ada", l, n))
                if ADA_ITEMS * l + n >= 2:
                    pe.wait_ge(S("ada_out"), ADA_ITEMS * l + n - 1)
                w = split(slot_of(("ada", l, n), SLOT), KD)
                for k in range(KD):
                    last = mm(bank(4 + n % 2)[0:2, :], c[:, k], w[:, k], start=k == 0, stop=k == KD - 1)
                last.then_inc(S("ada_made"), 1)

        def turn_mods(l):
            pe.wait_ge(S("mod_ready", l), 1)
            turn(bank(6, MODS), modt[0:MODS, :], MODS).then_inc(S("mod_turned", l), 1)

        def turn_tile(l, t):
            pe.wait_ge(S("xn_ready", l), t + 1)
            if t:
                pe.wait_ge(S("hT_ready", l), t)
            for k in range(KD):
                last = turn(ps[:, k * P:(k + 1) * P], xn[l](t)[:, k * P:(k + 1) * P])
            last.then_inc(S("n_turned", l), 1)

        def project(l, t, parts, out_sem):
            pe.wait_ge(S("hT_ready", l), t + 1)
            if t:
                pe.wait_ge(out_sem, t)
            for b, (name, cols) in enumerate(parts):
                if t == 0:
                    wait_landed(pe, (name, l, 0))
                w = split(slot_of((name, l, 0), KD * cols), KD)
                for k in range(KD):
                    last = mm(bank(2 + b, cols), hT[l](t)[:, k * P:(k + 1) * P], w[:, k], start=k == 0, stop=k == KD - 1)
            last.then_inc(S("projected", l), 1)

        def mix(l, it, half):
            name = (MATRICES[l][-2 + half], l, 0)
            w = split(slot_of(name, SLOT), KD)
            for k in range(KD):
                last = mm(bank(6 + half), oT[:, k * P:(k + 1) * P], w[:, k], start=k == 0, stop=k == KD - 1)
            if half:
                last.then_inc(S("mixed"), 1)

        def heads(l, it, keys, score_of, v_of, last_mix=None):
            past = tiles_before(l, it)
            g = past * HEADS
            first = 5 if keys == P else 0
            w = keys // 2 if keys > P else keys
            for n in range(HEADS + 3):
                if n == 2 and last_mix:
                    last_mix()
                if n < HEADS:
                    if n >= 2:
                        pe.wait_ge(S("exp_ready"), g + n - 1)
                    q, k = score_of(n)
                    for c in range(keys // w):
                        at = first * P + c * w
                        last = mm(scores(n, keys)[:, c], q, k[:, at:at + w], start=True, stop=True)
                    last.then_inc(S("scored"), 1)
                if 0 <= n - 2 < HEADS:
                    h = n - 2
                    pe.wait_ge(S("p_ready"), g + h + 1)
                    if h:
                        pe.wait_ge(S("pt_ready"), g + h)
                    for j in range(keys // P):
                        last = turn(ps[:, 4 * BANK + j * P:4 * BANK + (j + 1) * P], pbuf(h, keys)[:, j * P:(j + 1) * P])
                    last.then_inc(S("p_turned"), 1)
                if n >= 3:
                    h = n - 3
                    pe.wait_ge(S("pt_ready"), g + h + 1)
                    if h == 0 and not (isinstance(past, int) and past == 0):
                        pe.wait_ge(S("mix_out"), past)
                    for j in range(keys // P):
                        last = mm(oT_block(h), v_of(h, first + j), ptbuf(h, keys)[:, j * P:(j + 1) * P],
                                  start=j == 0, stop=j == keys // P - 1)
                    last.then_inc(S("pv_done"), 1)

        def attend(l, make_q, turn_q, score_of, v_of):
            def tile(it, keys, last, more):
                heads(l, it, keys, score_of, v_of, last)
                if more:
                    make_q(it + 1)
                pe.wait_ge(S("oT_ready"), tiles_before(l, it) * 2 + 2)
                mix(l, it, 0)
                if more:
                    turn_q(it + 1)

            for half in range(2):
                wait_landed(pe, (MATRICES[l][-2 + half], l, 0))
            make_q(0)
            turn_q(0)
            tile(0, P, None, True)
            tile(1, LKEYS, lambda: mix(l, 0, 1), True)
            with pe.Fori(1, LAT - 1) as i:
                tile(i + 1, LKEYS, lambda: mix(l, i, 1), True)
            tile(LAT, LKEYS, lambda: mix(l, LAT - 1, 1), False)
            mix(l, LAT, 1)

        def used(n):
            pe.drain().then_inc(S("ring_used"), n)

        pe.wait_ge(S("cond_ready"), 1)
        ada(0, 0, ADA_ITEMS)
        turn_mods(0)

        def turn_keys_m(t):
            j = t if t > 0 else 5 if t == 0 else 0
            if t >= 0:
                pe.wait_ge(S("proj_out", 0), t + 1)
                pe.wait_ge(S("turned_out", 0), t + 1)
                for m in range(3):
                    turn(bank(4, P, m * P), m_ql[:, (t % 2) * QL + m * P:(t % 2) * QL + (m + 1) * P])
            key = m_key[:, j * KV:(j + 1) * KV]
            for m in range(2):
                turn(bank(5, P, m * P), key[:, m * P:(m + 1) * P])
            turn(ps[0:ROPE, 5 * BANK + 2 * P:5 * BANK + 3 * P], key[:, KVL:KV]).then_inc(S("turned", 0), 1)

        def turn_keys_g(t):
            W = NQ + NK
            if t >= 0:
                pe.wait_ge(S("qk_ready"), t + 1)
                pe.wait_ge(S("turned_out", 1), t + 1)
                for m in range(8):
                    turn(ps[:, 5 * BANK + m * P:5 * BANK + (m + 1) * P], g_qk[:, (t % 2) * W + m * P:(t % 2) * W + (m + 1) * P])
                k = g_qk[:, (t % 2) * W + NQ:(t % 2 + 1) * W]
            else:
                pe.wait_ge(S("cache_landed"), 32)
                k = g_cache
            for h in range(KVH):
                last = turn(ps[0:HD, 7 * BANK + h * P:7 * BANK + (h + 1) * P], k[:, h * HD:(h + 1) * HD])
            last.then_inc(S("turned", 1), 1)

        def projection(l, parts, turn_keys, out_sem):
            turn_tile(l, 0)
            turn_keys(-1)
            for t in range(NTILE):
                if t + 1 < NTILE:
                    turn_tile(l, t + 1)
                project(l, t, parts, out_sem)
                if t == NTILE - 1:
                    used(len(parts))
                if t:
                    turn_keys(t - 1)
            turn_keys(NTILE - 1)

        projection(0, (("dq", QL), ("dkv", KV)), turn_keys_m, S("proj_out", 0))
        wait_landed(pe, ("uk", 0, 0))
        pe.wait_ge(S("turned_out", 0), NKEYT)
        w = split(slot_of(("uk", 0, 0), 2 * D), 2)
        for m in range(HEADS // 2):
            if m >= 2:
                pe.wait_ge(S("k_even"), m - 1)
                pe.wait_ge(S("k_odd"), m - 1)
            for c, n in ((0, BANK), (BANK, KEYS - BANK)):
                for k in range(2):
                    last = mm(spair(m, KEYS)[:, c:c + n], w[:, k, m * P:(m + 1) * P], m_ckvT[:, k * KEYS + c:k * KEYS + c + n],
                              start=k == 0, stop=k == 1)
            last.then_inc(S("k_made"), 1)
        used(1)
        wait_landed(pe, ("uv", 0, 0))
        pe.wait_ge(S("mod_cols", 0), 1)
        w = split(slot_of(("uv", 0, 0), 2 * D), 2)
        for j in range(NKEYT):
            if j >= 2:
                pe.wait_ge(S("v_odd" if j % 2 else "v_even"), j // 2)
            for n in range(2):
                for k in range(2):
                    last = mm(bank(4 + 2 * (j % 2) + n), m_ckvT[:, k * KEYS + j * P:k * KEYS + (j + 1) * P],
                              w[:, k, n * BANK:(n + 1) * BANK], start=k == 0, stop=k == 1)
            last.then_inc(S("v_made"), 1)
        used(1)
        pe.wait_ge(S("k_even"), HEADS // 2)
        pe.wait_ge(S("k_odd"), HEADS // 2)
        pe.wait_ge(S("v_even"), NKEYT // 2)
        pe.wait_ge(S("v_odd"), NKEYT // 2)
        pe.wait_ge(S("rope_keys"), 1)
        for n in range(2):
            wait_landed(pe, (f"uq{n}", 0, 0))

        def make_q(it):
            pe.wait_ge(S("ql_ready"), it + 1)
            for b in range(4):
                w = split(slot_of((f"uq{b // 2}", 0, 0), 3 * 768), 3)
                for k in range(3):
                    last = mm(bank(b, 4 * QD), qls[:, k * P:(k + 1) * P], w[:, k, (b % 2) * 4 * QD:(b % 2 + 1) * 4 * QD],
                              start=k == 0, stop=k == 2)
            last.then_inc(S("q_made"), 1)

        def turn_q(it):
            pe.wait_ge(S("q_out"), it + 1)
            if not isinstance(it, int) or it:
                pe.wait_ge(S("q_roped"), it)
            for h in range(HEADS):
                last = turn(ps[0:QD, h * P:(h + 1) * P], q_tok[:, h * QD:(h + 1) * QD])
            last.then_inc(S("q_turned"), 1)
            pe.wait_ge(S("q_ready", 0), it * 2 + 2)

        attend(0, make_q, turn_q, lambda h: (qT[0:QD, h * P:(h + 1) * P], m_kT[0:QD, h * KEYS:(h + 1) * KEYS]),
               lambda h, j: m_V[:, j * D + h * VD:j * D + (h + 1) * VD])
        used(4)
        meet(pe, 0)

        def pads(l):
            n = sum(x[0] == "pad" and x[1] == l for x in order)
            if n:
                used(n)

        def experts(l):
            def turn_h(t):
                pe.wait_ge(S("h_ready", l), t + 1)
                if t:
                    pe.wait_ge(S("hT_out", l), t)
                for k in range(KD):
                    last = turn(ps[:, k * P:(k + 1) * P], e_h[:, t * D + k * P:t * D + (k + 1) * P])
                last.then_inc(S("h_turned", l), 1)

            turn_h(0)
            pe.wait_ge(S("router_landed", l), 32)
            for t in range(NTILE):
                if t + 1 < NTILE:
                    turn_h(t + 1)
                pe.wait_ge(S("hT_out", l), t + 1)
                for k in range(KD):
                    last = mm(bank(2, NR, t * 32), e_hT[:, (t % 2) * D + k * P:(t % 2) * D + (k + 1) * P], rw[:, k * NR:(k + 1) * NR],
                              start=k == 0, stop=k == KD - 1)
                last.then_inc(S("logits", l), 1)
            if l == 0:
                ada(1, 0, ADA_SPLIT[0])
            pe.wait_ge(S("picked", l), 1)
            M = e_r[:, R_M:R_M + NTILE * NE]
            mm(bank(3, NTILE * NE), tri, M, start=True, stop=True)
            mm(bank(3, NTILE * NE, NTILE * NE), ones, M, start=True, stop=True).then_inc(S("ranked", l), 1)
            if l == 0:
                ada(1, *ADA_SPLIT)
                pads(0)
            R = rounds_needed(pe, l)

            def turn_rows(t, u, r):
                pe.wait_ge(S(f"xs_landed{u % 2}", l), r * 16 + 16)
                for k in range(KD):
                    last = turn(ps[:, k * P:(k + 1) * P], e_xs[:, (u % 2) * D + k * P:(u % 2) * D + (k + 1) * P])
                last.then_inc(S("xs_used", l), 1)

            def gate_up(t, u, more=0, less=0):
                pe.wait_ge(S("xsT_ready", l), t + 1)
                wait_landed(pe, ("gu", l, u), more, less)
                w = split(slot_of(("gu", l, u), SLOT), KD)
                for k in range(KD):
                    last = mm(bank(2 + u % 2), e_xsT[:, (u % 2) * D + k * P:(u % 2) * D + (k + 1) * P], w[:, k],
                              start=k == 0, stop=k == KD - 1)
                last.then_inc(S("gu_done", l), 1)

            def turn_hid(t, u):
                pe.wait_ge(S("hid_ready", l), t + 1)
                for k in range(2):
                    last = turn(bank(4, P, k * P), e_hid[:, (u % 2) * FF + k * P:(u % 2) * FF + (k + 1) * P])
                last.then_inc(S("hid_turned", l), 1)

            def down(t, u, more=0, less=0):
                pe.wait_ge(S("hidT_ready", l), t + 1)
                pe.wait_ge(S("y_out", l), t + 1)
                wait_landed(pe, ("dn", l, u), more, less)
                w = split(slot_of(("dn", l, u), 2 * D), 2)
                for n in range(2):
                    for k in range(2):
                        last = mm(bank(6 + n), e_hidT[:, (u % 2) * FF + k * P:(u % 2) * FF + (k + 1) * P],
                                  w[:, k, n * BANK:(n + 1) * BANK], start=k == 0, stop=k == 1)
                last.then_inc(S("y_done", l), 1)

            turn_rows(0, 0, 0)
            gate_up(0, 0)
            turn_rows(1, 1, 0)
            with pe.Fori(0, ROUNDS) as i:
                with pe.If(i < R):
                    for u in range(2):
                        turn_hid(i * 2 + u, u)
                        gate_up(i * 2 + (u + 1), u + 1, i * 32)
                        turn_rows(i * 2 + (u + 2), u, i + 1)
                        down(i * 2 + u, u, i * 32)
            for u in range(LOOPED, SLOT_TILES):
                k = u - LOOPED
                turn_hid(R * 2 + k, u)
                if u + 1 < SLOT_TILES:
                    gate_up(R * 2 + (k + 1), u + 1, R * 32, ROUNDS * 32)
                if u + 2 < SLOT_TILES:
                    turn_rows(R * 2 + (k + 2), u, R + (k // 2 + 1))
                down(R * 2 + k, u, R * 32, ROUNDS * 32)

        experts(0)
        pads(2)
        ada(1, ADA_SPLIT[1], ADA_ITEMS)
        turn_mods(1)
        meet(pe, 1)
        projection(1, (("qkv0", BANK), ("qkv1", BANK), ("qkv2", BANK)), turn_keys_g, S("qk_ready"))
        pe.wait_ge(S("turned_out", 1), NKEYT)

        def score_g(h):
            half = slice(64 * (h % 2), 64 * (h % 2) + 64)
            return qT[half, (h // 2) * P:(h // 2 + 1) * P], g_kT[half, (h // 4) * KEYS:(h // 4 + 1) * KEYS]

        attend(1, lambda it: None, lambda it: pe.wait_ge(S("q_ready", 1), it + 1), score_g,
               lambda h, j: g_V[:, j * NK + (h // 4) * HD:j * NK + (h // 4 + 1) * HD])
        used(2)
        meet(pe, 2)
        pads(1)
        experts(1)
        pads(3)
        meet(pe, 3)


def constants():
    c = np.zeros((P, C_END), np.float32)
    c[:, C_ID:C_ID + P] = np.eye(P)
    c[:, C_ONE:C_ONE + P] = 1.0
    c[:, C_TRI:C_TRI + P] = np.triu(np.ones((P, P)), 1)
    t = np.arange(LAT * P)
    row, col = (t // GRID_W).astype(np.float32), (t % GRID_W).astype(np.float32)
    for dim, at_c, at_s in ((ROPE, C_CM, C_SM), (HD, C_CG, C_SG)):
        axis = dim // 2
        inv = np.power(np.float32(10000.0), -np.arange(0, axis, 2, dtype=np.float32) / np.float32(axis)).astype(np.float32)
        ang = np.concatenate([row[:, None] * inv, col[:, None] * inv], axis=1)
        for f, at in ((np.cos, at_c), (np.sin, at_s)):
            v = np.repeat(f(ang).astype(np.float32), 2, axis=1).reshape(LAT, P, dim)
            c[:, at:at + LAT * dim] = v.transpose(1, 0, 2).reshape(P, LAT * dim)
    c[:, C_R4:C_R4 + NG] = NG - np.arange(NG)
    c[:, C_TI:C_TI + SLOT_TILES] = np.arange(SLOT_TILES)
    c[:, C_RND:C_RND + ROUNDS] = SLOT_TILES - LOOPED + 2 * np.arange(ROUNDS)
    c[0:MODS, C_SEL] = [(r // KD) % 6 in (1, 4) for r in range(MODS)]
    return c


def kernel(**inputs):
    import concourse.bacc as bacc
    from concourse.bass_utils import run_bass_kernel_spmd

    a = {n: np.ascontiguousarray(np.asarray(x)) for n, x in inputs.items()}
    small = ("c", "c_ctx", "ada_b", "norm_mix", "norm_ffn", "mla_q_norm")
    lay = {n: x for n, x in a.items() if n not in small}
    one = np.ones((KD, P), np.float32)
    bias = [np.concatenate([a["ada_b"][l].reshape(-1, P)] * 2) for l in range(2)]
    gain = [np.concatenate([one, a["norm_mix"][l].reshape(KD, P), one, one, a["norm_ffn"][l].reshape(KD, P), one] * 2)
            for l in range(2)]
    lay["vec_m"] = np.ascontiguousarray(np.concatenate(bias + gain, axis=1))
    lay["vec_b"] = np.concatenate([a["c_ctx"].reshape(-1, P), a["c"].reshape(-1, P), a["mla_q_norm"].reshape(-1, P)])
    lay["mla_w_uk"] = a["mla_w_uk"].reshape(KVL, HEADS * NOPE)
    lay["mla_w_uv"] = a["mla_w_uv"].reshape(KVL, HEADS * VD)
    lay["const"] = constants()
    nc = bacc.Bacc("TRN2", target_bir_lowering=False, num_devices=1)
    A = {n: nc.dram_tensor(f"in_{n}", x.shape, mybir.dt.from_np(x.dtype), kind="ExternalInput").ap() for n, x in lay.items()}
    shapes = ((1, P, D), (1, LAT * P, D), (1, 1, P, KV), (1, 1, P, 2, KVH, HD))
    O = [nc.dram_tensor(f"out_{i}", s, F32, kind="ExternalOutput").ap() for i, s in enumerate(shapes)]
    with ExitStack() as ctx:
        program(nc, ctx, A, O)
    r = run_bass_kernel_spmd(nc, [{f"in_{n}": x for n, x in lay.items()}], core_ids=[0])
    return tuple(r.results[0][f"out_{i}"] for i in range(len(shapes)))
```

```python
from contextlib import ExitStack

import numpy as np
import concourse.bass as bass
from concourse import mybir

F32 = mybir.dt.float32
I32 = mybir.dt.int32
ALU = mybir.AluOpType
ACT = mybir.ActivationFunctionType
AX = mybir.AxisListType
ds = bass.ds

P = 128
D = 1024
KD = D // P
NTILE = 5
LAT = NTILE - 1
NKEYT = 6
KEYS = NKEYT * P
LKEYS = 5 * P
EPS = 1e-6
HEADS = 16
NOPE, ROPE, VD = 64, 32, 64
QD = NOPE + ROPE
QL, KVL = 384, 256
KV = KVL + ROPE
KVH, HD = 4, 64
NG, EPG = 4, 4
NE = NG * EPG
NR = NG + NE
FF = 256
TOK = NTILE * P
PAIRS = 2 * TOK
SLOT_TILES = (PAIRS - NE) // P + NE
GRID_W = 64
BANK = 512
SLOT = 4096
NSLOT = 4
ADA_ITEMS = 12
PARTS = ((0, 2), (2, 5), (5, 6))
PART_ENDS = (4, 10, 12)
NQ, NK = HEADS * HD, KVH * HD
SCALE = (QD ** -0.5, HD ** -0.5)
ROUNDS = (SLOT_TILES - 2) // 2
LOOPED = 2 * ROUNDS
MASKED = -3.0e38

C_ID, C_ONE, C_TRI, C_CM = 0, P, 2 * P, 3 * P
C_SM = C_CM + LAT * ROPE
C_CG = C_SM + LAT * ROPE
C_SG = C_CG + LAT * HD
C_R4 = C_SG + LAT * HD
C_TI = C_R4 + NG
C_RND = C_TI + SLOT_TILES
C_OV = C_RND + ROUNDS
C_END = C_OV + NTILE

MODV = 2 * KD
STATS = {"mix0": (0, 0), "ffn0": (1, 1), "mix1": (2, 3), "ffn1": (3, 4), "end": (4, 6)}
VB_COND, VB_QN, VB_END = 0, 16, 19


def bmid(ap, n):
    return ap.unsqueeze(1).broadcast_to([ap.shape[0], n, ap.shape[1]])


def blast(ap, n):
    return ap.unsqueeze(2).broadcast_to([ap.shape[0], ap.shape[1], n])


def split(ap, a):
    return ap.rearrange("p (a b) -> p a b", a=a)


A_HEADS = HEADS * KEYS + NKEYT * D + 3 * TOK
ARENA = A_HEADS + 5632 + QL

R_SH = 0
R_EX = R_SH + NTILE * (NG + 1)
R_W = R_EX + NTILE * (NG + 1)
R_FREE = R_W + 2 * NTILE
R_M = R_FREE + NTILE * (NG + NE + NG + NE + 2 * EPG + 4 + NG + 2 * EPG + 2 * NE)

MATRICES = (("dq", "dkv", "uk", "uv", "uq0", "uq1", "wo0", "wo1"), ("qkv0", "qkv1", "qkv2", "gwo0", "gwo1"))


def program(nc, ctx, A, O):
    def sb(name, cols, dt=F32):
        return ctx.enter_context(nc.sbuf_tensor(name, [P, cols], dt))

    def split_rows(ap):
        return ap.rearrange("p (a b) -> p a b", b=P)

    sems = {}

    def S(name, layer=None):
        key = name if layer is None else f"{name}_{layer}"
        if key not in sems:
            sems[key] = ctx.enter_context(nc.semaphore(key))
        return sems[key]

    const = sb("const", C_END)
    X = sb("X", NTILE * D)
    vecb, colb = sb("vecb", P), sb("colb", VB_END)
    cond = sb("cond", 2 * KD)
    modc = sb("modc", 2 * 2 * MODV)
    modt = sb("modt", P)
    mod_vec = sb("mod_vec", 2 * P + 1)
    gate_rows = sb("gate_rows", 2 * D)
    zeros = sb("zeros", P)
    kvn_row, qkn_row = sb("kvn_row", KVL), sb("qkn_row", 2 * HD)
    rbias, rw = sb("rbias", 2 * NR), sb("rw", KD * NR)
    ring = sb("ring", NSLOT * SLOT)
    ssq, rstd, st = sb("ssq", NTILE), sb("rstd", NTILE), sb("st", 2 * NTILE)
    hst, hsum, hinv = sb("hst", HEADS), sb("hsum", HEADS), sb("hinv", HEADS)
    pst = sb("pst", 3 * (HEADS + KVH))
    arena = sb("arena", ARENA)
    expert, slot_i = sb("expert", SLOT_TILES, I32), sb("slot_i", 2 * NTILE, I32)
    rounds = sb("rounds", 2, I32)
    ps = ctx.enter_context(nc.psum_tensor("ps", [P, 8 * BANK], F32))

    slots = nc.dram_tensor("slot_rows", (SLOT_TILES * P, D), F32).ap()
    modraw = [nc.dram_tensor(f"mod_raw{l}", (6, 2, D), F32).ap() for l in range(2)]
    modrow = [nc.dram_tensor(f"mod_rows{l}", (6, 2, D), F32).ap() for l in range(2)]

    ident, ones, tri = const[:, C_ID:C_ID + P], const[:, C_ONE:C_ONE + P], const[:, C_TRI:C_TRI + P]

    def bank(b, n=BANK, at=0):
        return ps[:, b * BANK + at:b * BANK + at + n]

    def ar(at, n):
        return arena[:, at:at + n]

    def xt(t):
        return X[:, ds(t * D, D)]

    m_kT, m_V, m_qlT = ar(0, HEADS * KEYS), ar(HEADS * KEYS, NKEYT * D), ar(A_HEADS - 3 * TOK, 3 * TOK)
    qT, Pb, PT = ar(A_HEADS, HEADS * P), ar(A_HEADS + 2048, 2 * LKEYS), ar(A_HEADS + 3328, 2 * LKEYS)
    oT, qls = ar(A_HEADS + 4608, D), ar(A_HEADS + 5632, QL)
    q_tok, q_cos, q_sin = ar(A_HEADS + 2048, HEADS * QD), ar(A_HEADS + 3584, 512), ar(A_HEADS + 4096, 512)
    m_ckvT, m_krT = ar(A_HEADS, 2 * KEYS), ar(A_HEADS + 2 * KEYS, KEYS)
    m_ql, m_key = ar(4 * D, 2 * QL), ar(5 * D, NKEYT * KV)
    m_junk, m_rope = ar(7 * D, D), ar(8 * D, 2 * ROPE)
    g_kT, g_V, g_qT = ar(0, KVH * KEYS), ar(3072, NKEYT * NK), ar(4608, 8 * TOK)
    g_qk, g_cache = ar(13824, 2 * (NQ + NK)), ar(18944, NK)
    g_a, g_b = ar(16384, NQ + NK), ar(17664, NQ + NK)
    e_row, e_h, e_hT = ar(0, 4 * D), ar(4 * D, NTILE * D), ar(9 * D, 2 * D)
    e_junk, e_r = ar(11 * D, D), ar(12 * D, 1600)
    e_xs, e_xsT = ar(14000, 2 * D), ar(16048, 2 * D)
    e_sil, e_hid, e_hidT, e_y = ar(18096, 2 * FF), ar(18608, 2 * FF), ar(19120, 2 * FF), ar(19632, 2 * D)
    e_g = [ar(at, 2 * D) for at in (21696, 21696 + 2 * D, 14000, 14000 + 2 * D)]
    w_pair = e_r[:, R_W:R_W + 2 * NTILE]
    ffn_junk = ar(18432, D)
    mod_raw = (ar(9 * D, 2 * BANK), ar(19632, 2 * BANK))
    xn = [lambda t, o=o: ar(o + (t % 2) * D, D) for o in (0, 9728)]
    hT = [lambda t, o=o: ar(o + (2 + t % 2) * D, D) for o in (0, 9728)]

    def pbuf(h, n):
        return Pb[:, (h % 2) * LKEYS:(h % 2) * LKEYS + n]

    def ptbuf(h, n):
        return PT[:, (h % 2) * LKEYS:(h % 2) * LKEYS + n]

    def spair(h, n):
        return ps[:, (h % 2) * 2 * BANK:(h % 2) * 2 * BANK + n]

    def scores(h, keys):
        return split(spair(h, 2 * BANK), 2)[:, :, 0:keys // 2] if keys > P else split(spair(h, keys), 1)

    def oT_block(h):
        b = h // 2
        return ps[64 * (h % 2):64 * (h % 2) + 64, 6 * BANK + b * P:6 * BANK + (b + 1) * P]

    place, uses, order = {}, [0] * NSLOT, []

    def item(name):
        s = len(order) % NSLOT
        uses[s] += 1
        place[name] = (s, 32 * uses[s], len(order))
        order.append(name)

    def use_of(n):
        kind, l, t = order[n]
        if kind in ("gu", "dn"):
            return S("gu_done" if kind == "gu" else "y_done", l), t + 1
        if kind == "ada":
            return S("ada_made"), ADA_ITEMS * l + t + 1
        return S("ring_used"), sum(x[0] not in ("gu", "dn", "ada") for x in order[:n + 1])

    ada_first = ([(0, n) for n in range(PART_ENDS[1])], [(1, n) for n in range(PART_ENDS[0], PART_ENDS[1])])
    ada_ranks = [[(l, n) for n in range(PART_ENDS[1], PART_ENDS[2])] for l in range(2)]
    ada_routing = ([(1, n) for n in range(PART_ENDS[0])], [])

    for l in range(2):
        for a in ada_first[l]:
            item(("ada", *a))
        for n in MATRICES[l]:
            item((n, l, 0))
        for a in ada_ranks[l] + ada_routing[l]:
            item(("ada", *a))
        item(("gu", l, 0))
        for t in range(SLOT_TILES):
            if t + 1 < SLOT_TILES:
                item(("gu", l, t + 1))
            item(("dn", l, t))

    def slot_of(name, cols):
        s = place[name][0]
        return ring[:, s * SLOT:s * SLOT + cols]

    def wait_landed(pe, name, more=0, less=0):
        s, v, _ = place[name]
        pe.wait_ge(S(f"ring_landed{s}"), more + (v - less))

    def rounds_needed(eng, l):
        eng.wait_ge(S("routed", l), 1)
        return eng.value_load(rounds[0:1, 0:1], min_val=1, max_val=ROUNDS)

    def tiles_before(l, it):
        return it + NTILE * l

    rows_of = {"dq": A["mla_w_dq"][0], "dkv": A["mla_w_dkv"][0], "uk": A["mla_w_uk"], "uv": A["mla_w_uv"],
               "uq": A["mla_w_uq"][0], "wo": A["mla_w_o"][0], "qkv": A["gqa_w_qkv"][0], "gwo": A["gqa_w_o"][0]}
    cols_of = {"dq": (QL, 0), "dkv": (KV, 0), "uk": (D, 0), "uv": (D, 0), "uq0": (768, 0), "uq1": (768, 768)}
    for n in (*MATRICES[0], *MATRICES[1]):
        cols_of.setdefault(n, (BANK, BANK * int(n[-1]) if n[-1].isdigit() else 0))

    first_inputs = [(vecb[0:VB_END, :], A["vec_b"]), (const[:], A["const"])]
    inputs = [(X[:, 0:D], A["x_prompt"][0]), (split(X[:, D:], LAT), A["x_sample"][0].rearrange("(t p) n -> p t n", p=P)),
              (m_key[:, 0:KV], A["cache_mla"][0, 0]),
              (kvn_row[:], A["mla_kv_norm"][0:1, :].broadcast_to([P, KVL])),
              (qkn_row[:, 0:HD], A["gqa_q_norm"][0:1, :].broadcast_to([P, HD])),
              (qkn_row[:, HD:2 * HD], A["gqa_k_norm"][0:1, :].broadcast_to([P, HD]))]
    for l in range(2):
        inputs.append((rbias[:, l * NR:l * NR + NG], A["moe_b_group"][l:l + 1, :].broadcast_to([P, NG])))
        inputs.append((rbias[:, l * NR + NG:(l + 1) * NR], A["moe_b_expert"][l:l + 1, :].broadcast_to([P, NE])))

    block = ctx.enter_context(nc.Block())

    @block.sync
    def _(sp):
        def free(n, R=None):
            if n < NSLOT:
                return
            kind, l, t = order[n - NSLOT]
            if kind not in ("gu", "dn"):
                sp.wait_ge(*use_of(n - NSLOT))
                return
            sp.wait_ge(S("gu_done" if kind == "gu" else "y_done", l), R * 2 + (t - LOOPED + 1))
            sp.nop().then_inc(S("slots_used"), 1)
            with sp.Fori(0, ROUNDS) as i:
                with sp.If(i >= R):
                    sp.nop().then_inc(S(f"ring_landed{n % NSLOT}"), 32)

        def load(name, src, cols, off, R=None):
            s, _, n = place[name]
            free(n, R)
            kk = src.shape[0] // P
            w = split(ring[:, s * SLOT:s * SLOT + kk * cols], kk)
            src = src.rearrange("(k p) n -> p k n", p=P)
            ha = (kk + 1) // 2
            sp.dma_start(w[:, 0:ha], src[:, 0:ha, off:off + cols]).then_inc(S(f"ring_landed{s}"), 16)
            sp.dma_start(w[:, ha:kk], src[:, ha:kk, off:off + cols]).then_inc(S(f"ring_landed{s}"), 16)

        def load_gu(l, t, e):
            s = place[("gu", l, t)][0]
            w = split(ring[:, s * SLOT:(s + 1) * SLOT], KD)
            for m, name in enumerate(("moe_w_gate", "moe_w_up")):
                src = A[name][l][ds(e, 1)].rearrange("e (k p) n -> p (e k) n", p=P)
                sp.dma_start(w[:, :, m * FF:(m + 1) * FF], src).then_inc(S(f"ring_landed{s}"), 16)

        def load_dn(l, t, e):
            s = place[("dn", l, t)][0]
            w = split(ring[:, s * SLOT:s * SLOT + 2 * D], 2)
            src = A["moe_w_down"][l][ds(e, 1)].rearrange("e (k p) n -> p (e k) n", p=P)
            for k in range(2):
                sp.dma_start(w[:, k:k + 1], src[:, k:k + 1]).then_inc(S(f"ring_landed{s}"), 16)

        def load_rows(l, t, u, used=None):
            if used is not None:
                sp.wait_ge(S("xs_used", l), used)
            sp.dma_start(e_xs[:, (u % 2) * D:(u % 2 + 1) * D], slots[ds(t * P, P), :]).then_inc(S(f"xs_landed{u % 2}", l), 16)

        def expert_of(t):
            return sp.value_load(expert[0:1, ds(t, 1)], min_val=0, max_val=NE - 1)

        def load_ada(items, R=None):
            for l, n in items:
                load(("ada", l, n), A["ada_w"][l], BANK, n * BANK, R)

        R = None
        for l in range(2):
            load_ada(ada_first[l], R)
            for n in MATRICES[l]:
                load((n, l, 0), rows_of[n.rstrip("012")], *cols_of[n])
            load_ada(ada_ranks[l] + ada_routing[l])
            R = rounds_needed(sp, l)
            sp.wait_ge(S("rows_scattered", l), 16 * 2 * NTILE)
            load_rows(l, 0, 0)
            load_rows(l, 1, 1)
            e = expert_of(0)
            sp.wait_ge(S("ada_made"), 2 * ADA_ITEMS if l else ADA_ITEMS + PART_ENDS[0])
            load_gu(l, 0, e)

            def turn(t, u, before=None):
                e, e_next = expert_of(t), expert_of(t + 1)
                if u:
                    sp.wait_ge(S("gu_done", l), t)
                load_gu(l, u + 1, e_next)
                if u + 2 < SLOT_TILES:
                    load_rows(l, t + 2, u, t + 1)
                if u >= 2:
                    sp.wait_ge(S("y_done", l), t - 1 if before is None else before)
                load_dn(l, u, e)

            for t in range(2):
                turn(t, t)
            with sp.Fori(1, ROUNDS) as i:
                with sp.If(i < R):
                    for u in range(2):
                        turn(i * 2 + u, u + 2)
            before = sp.value_load(rounds[0:1, 1:2], min_val=1, max_val=LOOPED - 1)
            for t in range(LOOPED, SLOT_TILES - 1):
                turn(R * 2 + (t - LOOPED), t, before if t == LOOPED else R * 2 + (t - LOOPED - 1))
            e = expert_of(R * 2 + (SLOT_TILES - 1 - LOOPED))
            sp.wait_ge(S("y_done", l), R * 2 + (SLOT_TILES - 2 - LOOPED))
            load_dn(l, SLOT_TILES - 1, e)
        for t in range(NTILE):
            sp.wait_ge(S("y_ready"), t + 1)
            dst = O[0][0] if t == 0 else O[1][0, (t - 1) * P:t * P, :]
            sp.dma_start(dst, e_h[:, t * D:(t + 1) * D]).then_inc(S("results_stored"), 16)
        sp.wait_ge(S("results_stored"), 16 * NTILE)

    @block.gpsimd
    def _(pool):
        pool.memset(zeros[:], 0.0).then_inc(S("zero_made"), 1)
        pool.wait_ge(S("zero_made"), 1)
        pool.wait_ge(S("ada_made"), PART_ENDS[1])
        for t in range(SLOT_TILES):
            pool.dma_start(split_rows(slots[t * P:(t + 1) * P, :]), bmid(zeros[:], KD)).then_inc(S("table_zeroed"), 16)
        pool.wait_ge(S("table_zeroed"), 16 * SLOT_TILES)
        pool.wait_ge(S("turned_out", 0), NKEYT)
        pool.wait_ge(S("state_stored", 0), 16)
        nc.gpsimd.tensor_copy(split(m_kT[64:96, :], HEADS), bmid(m_krT[64:96, :], HEADS)).then_inc(S("rope_keys"), 1)
        for l in range(2):
            pool.wait_ge(S("routed", l), 1)
            for t in range(NTILE):
                for c in range(2):
                    pool.indirect_dma_start(
                        slots, bass.IndirectOffsetOnAxis(ap=slot_i[:, 2 * t + c:2 * t + c + 1], axis=0),
                        e_h[:, t * D:(t + 1) * D], None).then_inc(S("rows_scattered", l), 16)
            pool.wait_ge(S("rows_scattered", l), 16 * 2 * NTILE)
            pool.wait_ge(S("last_stored"), 32 * (l + 1))
            for t in range(NTILE):
                if t >= 4:
                    pool.wait_ge(S("combined", l), t - 3)
                for c in range(2):
                    pool.indirect_dma_start(
                        e_g[t % 4][:, c * D:(c + 1) * D], None, slots,
                        bass.IndirectOffsetOnAxis(ap=slot_i[:, 2 * t + c:2 * t + c + 1], axis=0))\
                        .then_inc(S(f"gathered{t % 4}"), 16)

    @block.scalar
    def _(act):
        for dst, src in first_inputs:
            act.dma_start(dst, src).then_inc(S("first_inputs"), 16)
        for dst, src in inputs:
            act.dma_start(dst, src).then_inc(S("inputs"), 16)
        act.wait_ge(S("cols_ready"), 1)
        act.activation(cond[:], colb[:, VB_COND:VB_COND + 2 * KD], ACT.Silu).then_inc(S("cond_ready"), 1)

        def square(t, junk):
            act.activation(junk, xt(t), ACT.Square, accum_out=ssq[:, t:t + 1]).then_inc(S("squared"), 1)
            act.drain()

        def root(name, a, b, batch=0):
            n = STATS[name][1] + batch + 1
            act.wait_ge(S("mean"), n)
            act.activation(st[:, NTILE + a:NTILE + b], st[:, a:b], ACT.Sqrt).then_inc(S("root"), 1)

        def mod_out(items):
            for l, n in items:
                g = ADA_ITEMS * l + n
                act.wait_ge(S("ada_made"), g + 1)
                if g >= 2:
                    act.wait_ge(S(f"mod_raw_out{n % 2}"), 16 * (g // 2))
                raw = mod_raw[g >= PART_ENDS[1]][0:2, (n % 2) * BANK:(n % 2 + 1) * BANK]
                act.activation(raw, bank(4 + n % 2)[0:2, :], ACT.Copy).then_inc(S("ada_out"), 1)
                act.wait_ge(S("ada_out"), g + 1)
                half = slice((n % 2) * BANK, (n % 2 + 1) * BANK)
                act.dma_start(modraw[l][n // 2, :, half], raw).then_inc(S(f"mod_raw_out{n % 2}"), 16)

        def mod_part(l, part):
            a, b = PARTS[part]
            for half in range(2):
                act.wait_ge(S(f"mod_raw_out{half}"), 16 * (ADA_ITEMS // 2 * l + b))
            if part == 1:
                act.wait_ge(S("mod_cols"), l + 1)
            rows = MODV * (b - a)
            act.dma_start(modt[0:rows, :], modraw[l][a:b].rearrange("c v (k p) -> (c v k) p", p=P)).then_inc(S("mod_landed"), 16)
            at = (6 * l + a) * MODV
            act.dma_start(mod_vec[0:rows, :], A["vec_m"][at:at + rows]).then_inc(S("mod_landed"), 16)
            if part:
                act.wait_ge(S("mod_ready"), 3 * l + part + 1)
                act.dma_start(modrow[l][a:b].rearrange("c v (k p) -> (c v k) p", p=P), modt[0:rows, :]).then_inc(S("mod_stored"), 16)
                act.wait_ge(S("mod_stored"), 16 * (2 * l + part))

        def rows_in(dst, l, c, v, sem):
            act.dma_start(dst, modrow[l][c, v:v + 1, :].broadcast_to([P, D])).then_inc(sem, 16)

        def scale(l, t):
            if t == 0:
                act.wait_ge(S("weighted"), l + 1)
            act.wait_ge(S(f"gathered{t % 4}"), 32 * (2 * l + t // 4 + 1 if t % 4 == 0 else l + 1))
            a = e_g[t % 4][:, 0:D]
            act.activation(a, a, ACT.Copy, scale=w_pair[:, t:t + 1]).then_inc(S("scaled"), 1)

        def heads(l, it, keys, before_end=None):
            past = tiles_before(l, it)

            def out(half):
                act.wait_ge(S("pv_done"), past * HEADS + (half + 1) * 8)
                act.activation(oT[:, half * BANK:(half + 1) * BANK], bank(6 + half), ACT.Copy).then_inc(S("oT_ready"), 1)

            for h in range(HEADS + 2):
                if h >= 2:
                    j = h - 2
                    act.wait_ge(S("p_turned"), past * HEADS + j + 1)
                    if j >= 2:
                        act.wait_ge(S("pv_done"), past * HEADS + j - 1)
                    act.activation(ptbuf(j, keys), ps[:, 4 * BANK:4 * BANK + keys], ACT.Copy).then_inc(S("pt_ready"), 1)
                if h < HEADS:
                    act.wait_ge(S("max_ready"), past * HEADS + h + 1)
                    act.activation(split(pbuf(h, keys), 2 if keys > P else 1), scores(h, keys), ACT.Exp, bias=hst[:, h:h + 1],
                                   accum_out=hsum[:, h:h + 1]).then_inc(S("exp_ready"), 1)
                if h == 12:
                    out(0)
                if h == 13 and before_end:
                    before_end()
            out(1)

        def early_squares(l):
            act.wait_ge(S("mix_out"), tiles_before(l, LAT))
            for t in range(LAT):
                square(t, ffn_junk)

        def experts(l):
            for v in range(2):
                for n, c in ((0, 4), (1, 3)):
                    rows_in(e_row[:, (2 * v + n) * D:(2 * v + n + 1) * D], l, c, v, S("rows_e", l))
            act.dma_start(split(rw[:], KD)[:, :, 0:NG], A["moe_w_group"][l].rearrange("(k p) n -> p k n", p=P))\
                .then_inc(S("router_landed", l), 16)
            act.dma_start(split(rw[:], KD)[:, :, NG:NR], A["moe_w_expert"][l].rearrange("(k p) n -> p k n", p=P))\
                .then_inc(S("router_landed", l), 16)
            root(f"ffn{l}", 0, LAT)

            def hT_out(t):
                act.wait_ge(S("h_turned", l), t + 1)
                if t >= 2:
                    act.wait_ge(S("logits", l), t - 1)
                act.activation(e_hT[:, (t % 2) * D:(t % 2 + 1) * D], ps[:, 0:D], ACT.Copy).then_inc(S("hT_out", l), 1)

            hT_out(0)
            act.wait_ge(S("mix_out"), tiles_before(l, NTILE))
            square(LAT, ffn_junk)
            root(f"ffn{l}", LAT, NTILE, 1)
            for t in range(1, NTILE):
                hT_out(t)
            mod_out(ada_ranks[l])
            act.wait_ge(S("shifted", l), 1)
            act.activation(r_ex, r_sh, ACT.Exp).then_inc(S("r_exp", l), 1)
            mod_out(ada_routing[l])
            mod_part(l, 2)
            for v in range(2):
                rows_in(gate_rows[:, v * D:(v + 1) * D], l, 5, v, S("gates_m", l))
            if l == 0:
                mod_part(1, 0)

            def sil(t, u):
                act.wait_ge(S("gu_done", l), t + 1)
                act.activation(e_sil[:, (u % 2) * FF:(u % 2 + 1) * FF], bank(2 + u % 2, FF), ACT.Silu).then_inc(S("sil_ready", l), 1)

            def y_out(t, u, r, last=False):
                act.wait_ge(S("y_done", l), t + 1)
                act.wait_ge(S(f"y_stored{u % 2}", l), r * 16 + 16)
                y = e_y[:, (u % 2) * D:(u % 2 + 1) * D]
                act.activation(y, ps[:, 6 * BANK:8 * BANK], ACT.Copy).then_inc(S("y_out", l), 1)
                act.wait_ge(S("y_out", l), t + 2)
                stored = S("last_stored") if last else S(f"y_stored{u % 2}", l)
                act.dma_start(slots[ds(t * P, P), :], y).then_inc(stored, 16)

            act.drain().then_inc(S("y_out", l), 1)
            for b in range(2):
                act.drain().then_inc(S(f"y_stored{b}", l), 16)
            R = rounds_needed(act, l)
            sil(0, 0)
            with act.Fori(0, ROUNDS) as i:
                with act.If(i < R):
                    for u in range(2):
                        sil(i * 2 + (u + 1), u + 1)
                        y_out(i * 2 + u, u, i)
            for k in range(SLOT_TILES - LOOPED):
                if k + 1 < SLOT_TILES - LOOPED:
                    sil(R * 2 + (k + 1), k + 1)
                y_out(R * 2 + k, k, R + k // 2, k >= SLOT_TILES - LOOPED - 2)

        r_sh, r_ex = e_r[:, R_SH:R_SH + NTILE * (NG + 1)], e_r[:, R_EX:R_EX + NTILE * (NG + 1)]

        mod_out(ada_first[0][:2])
        act.wait_ge(S("inputs"), 16 * len(inputs))
        for t in range(NTILE):
            square(t, m_junk)
            if t == 2:
                mod_out(ada_first[0][2:3])
        root("mix0", 0, NTILE)

        def turned_m(t):
            j = t if t > 0 else 5 if t == 0 else 0
            act.wait_ge(S("turned", 0), t + 2)
            if t >= 0:
                for m in range(3):
                    act.activation(m_qlT[:, m * TOK + t * P:m * TOK + (t + 1) * P], bank(4, P, m * P), ACT.Identity,
                                   scale=colb[:, VB_QN + m:VB_QN + m + 1])
            act.activation(split(m_ckvT, 2)[:, :, j * P:(j + 1) * P], split(bank(5, 2 * P), 2), ACT.Copy)
            act.activation(m_krT[64:96, j * P:(j + 1) * P], ps[0:ROPE, 5 * BANK + 2 * P:5 * BANK + 3 * P], ACT.Copy)\
                .then_inc(S("turned_out", 0), 1)

        mod_out(ada_first[0][3:PART_ENDS[0]])
        mod_part(0, 0)
        mod_out(ada_first[0][PART_ENDS[0]:])
        mod_part(0, 1)
        for v in range(2):
            rows_in(gate_rows[:, v * D:(v + 1) * D], 0, 2, v, S("gates_a", 0))
        turned_m(-1)
        for t in range(NTILE):
            act.wait_ge(S("projected", 0), t + 1)
            act.activation(m_junk[:, 0:QL], bank(2, QL), ACT.Square, accum_out=pst[:, 0:1])
            act.activation(m_junk[:, QL:QL + KVL], bank(3, KVL), ACT.Square, accum_out=pst[:, 1:2]).then_inc(S("proj_squared", 0), 1)
            act.wait_ge(S("proj_mean", 0), t + 1)
            act.activation(pst[:, 4:6], pst[:, 2:4], ACT.Sqrt).then_inc(S("proj_root", 0), 1)
            if t == 0:
                act.wait_ge(S("proj_out", 0), 1)
                act.dma_start(O[2][0, 0], m_key[:, 5 * KV:6 * KV]).then_inc(S("state_stored", 0), 16)
            else:
                turned_m(t - 1)
        turned_m(NTILE - 1)
        act.wait_ge(S("state_stored", 0), 16)
        for m in range(HEADS // 2):
            act.wait_ge(S("k_made"), m + 1)
            act.activation(m_kT[0:64, 2 * m * KEYS:(2 * m + 1) * KEYS], spair(m, KEYS)[0:64], ACT.Copy).then_inc(S("k_even"), 1)
        for j in range(0, NKEYT, 2):
            act.wait_ge(S("v_made"), j + 1)
            act.activation(m_V[:, j * D:(j + 1) * D], ps[:, 4 * BANK:6 * BANK], ACT.Copy).then_inc(S("v_even"), 1)
        act.wait_ge(S("rope_keys"), 1)

        def ql(it):
            act.activation(split(qls, 3), split(m_qlT, 3)[:, :, ds(it * P, P)], ACT.Copy).then_inc(S("ql_ready"), 1)

        def q_stage(it):
            act.wait_ge(S("q_made"), it + 1)
            act.activation(split(q_tok, 4), split(ps[:, 0:4 * BANK], 4)[:, :, 0:4 * QD], ACT.Copy, scale=SCALE[0])\
                .then_inc(S("q_out"), 1)
            act.wait_ge(S("q_turned"), it + 1)
            act.activation(qT[0:QD, 0:D], ps[0:QD, 0:D], ACT.Copy).then_inc(S("q_ready", 0), 1)

        ql(0)
        q_stage(0)
        heads(0, 0, P, lambda: ql(1))
        q_stage(1)
        with act.Fori(0, LAT - 1) as i:
            heads(0, i + 1, LKEYS, lambda: ql(i + 2))
            q_stage(i + 2)
        heads(0, LAT, LKEYS, lambda: early_squares(0))
        experts(0)
        act.wait_ge(S("last_stored"), 32)
        mod_out(ada_first[1][:1])
        scale(0, 0)
        mod_out(ada_first[1][1:2])
        scale(0, 1)
        for t in range(NTILE):
            if t + 2 < NTILE:
                scale(0, t + 2)
            act.wait_ge(S("combined", 0), t + 1)
            square(t, ar(0, D))
            if t in (0, 2):
                mod_out(ada_first[1][2 + t // 2:3 + t // 2])
        root("mix1", 0, NTILE)
        mod_out(ada_first[1][4:])

        act.dma_start(g_V[:, 0:NK], A["cache_gqa"][0, 0, :, 1].rearrange("t h d -> t (h d)")).then_inc(S("cache_landed"), 16)
        act.dma_start(g_cache, A["cache_gqa"][0, 0, :, 0].rearrange("t h d -> t (h d)")).then_inc(S("cache_landed"), 16)
        mod_part(1, 1)
        for v in range(2):
            rows_in(gate_rows[:, v * D:(v + 1) * D], 1, 2, v, S("gates_a", 1))

        def turned_g(t):
            j = t if t > 0 else 5 if t == 0 else 0
            act.wait_ge(S("turned", 1), t + 2)
            if t >= 0:
                act.activation(split(g_qT, 8)[:, :, t * P:(t + 1) * P], split(ps[:, 5 * BANK:7 * BANK], 8), ACT.Copy,
                               scale=SCALE[1])
            for half in range(2):
                last = act.activation(split(g_kT[half * HD:(half + 1) * HD, :], KVH)[:, :, j * P:(j + 1) * P],
                                      split(bank(7)[0:HD, :], KVH), ACT.Copy)
            last.then_inc(S("turned_out", 1), 1)

        turned_g(-1)
        for t in range(NTILE):
            act.wait_ge(S("projected", 1), t + 1)
            if t >= 2:
                act.wait_ge(S("turned", 1), t)
            act.activation(g_qk[:, (t % 2) * (NQ + NK):(t % 2 + 1) * (NQ + NK)], ps[:, 2 * BANK:2 * BANK + NQ + NK], ACT.Copy)
            j = t if t > 0 else 5
            act.activation(g_V[:, j * NK:(j + 1) * NK], bank(4, NK, NK), ACT.Copy).then_inc(S("proj_out", 1), 1)
            act.wait_ge(S("proj_mean", 1), t + 1)
            act.activation(pst[:, 40:60], pst[:, 20:40], ACT.Sqrt).then_inc(S("proj_root", 1), 1)
            if t == 0:
                act.wait_ge(S("qk_ready"), 1)
                act.dma_start(O[3][0, 0, :, 0].rearrange("t h d -> t (h d)"), g_qk[:, NQ:NQ + NK]).then_inc(S("state_stored", 1), 16)
                act.wait_ge(S("proj_out", 1), 1)
                act.dma_start(O[3][0, 0, :, 1].rearrange("t h d -> t (h d)"), g_V[:, 5 * NK:6 * NK]).then_inc(S("state_stored", 1), 16)
            else:
                turned_g(t - 1)
                if t == 1:
                    act.wait_ge(S("state_stored", 1), 32)
        turned_g(NTILE - 1)

        def q_stage_g(it):
            act.activation(split(qT[:, 0:D], 8), split(g_qT, 8)[:, :, ds(it * P, P)], ACT.Copy).then_inc(S("q_ready", 1), 1)

        act.wait_ge(S("turned_out", 1), NKEYT)
        q_stage_g(0)
        heads(1, 0, P)
        q_stage_g(1)
        with act.Fori(0, LAT - 1) as i:
            heads(1, i + 1, LKEYS)
            q_stage_g(i + 2)
        heads(1, LAT, LKEYS, lambda: early_squares(1))
        experts(1)
        act.dma_start(e_row[:, 0:D], A["final_norm"].unsqueeze(0).broadcast_to([P, D])).then_inc(S("final_landed"), 16)
        scale(1, 0)
        scale(1, 1)
        for t in range(NTILE):
            act.wait_ge(S("combined", 1), t + 1)
            square(t, e_junk)
            if t + 2 < NTILE:
                scale(1, t + 2)
            root("end", t, t + 1, t)

    @block.vector
    def _(dve):
        def settle():
            dve.drain()

        dve.wait_ge(S("cols_turned"), 1)
        nc.vector.tensor_copy(colb[:], bank(7, VB_END)).then_inc(S("cols_ready"), 1)

        def modulation(l, part):
            n = 3 * l + part + 1
            rows = MODV * (PARTS[part][1] - PARTS[part][0])
            dve.wait_ge(S("mod_landed"), 32 * n)
            m = modt[0:rows, :]
            nc.vector.tensor_tensor(m, m, mod_vec[0:rows, 0:P], ALU.add)
            settle()
            nc.vector.scalar_tensor_tensor(m, m, mod_vec[0:rows, 2 * P:2 * P + 1], mod_vec[0:rows, P:2 * P],
                                           ALU.add, ALU.mult).then_inc(S("mod_ready"), 1)
            if part == 0:
                dve.wait_ge(S("mod_turned"), l + 1)
                nc.vector.tensor_copy(modc[:, 2 * MODV * l:2 * MODV * (l + 1)], bank(6, 2 * MODV)).then_inc(S("mod_cols"), 1)
                settle()

        def row_stats(name, a, b, batch=0):
            phase, first = STATS[name]
            dve.wait_ge(S("squared"), NTILE * phase + b)
            nc.vector.tensor_scalar(st[:, a:b], ssq[:, a:b], 1.0 / D, EPS, ALU.mult, ALU.add).then_inc(S("mean"), 1)
            dve.wait_ge(S("root"), first + batch + 1)
            nc.vector.reciprocal(rstd[:, a:b], st[:, NTILE + a:NTILE + b])
            settle()

        def norm(l, t):
            if t >= 2:
                dve.wait_ge(S("n_turned", l), t - 1)
            nc.vector.tensor_scalar(xn[l](t), xt(t), rstd[:, t:t + 1], None, ALU.mult).then_inc(S("xn_ready", l), 1)

        def mod_cols(l, t):
            v = 0 if t == 0 else 1
            dve.wait_ge(S("n_turned", l), t + 1)
            if t >= 2:
                dve.wait_ge(S("projected", l), t - 1)
            for k in range(KD):
                at = 2 * MODV * l + KD * v + k
                last = nc.vector.tensor_scalar(hT[l](t)[:, k * P:(k + 1) * P], ps[:, k * P:(k + 1) * P],
                                               modc[:, at + MODV:at + MODV + 1], modc[:, at:at + 1], ALU.mult, ALU.add)
            last.then_inc(S("hT_ready", l), 1)

        def rope(out0, out1, cs, sn):
            nc.vector.tensor_tensor(out0, cs[..., 0], sn[..., 1], ALU.subtract)
            return nc.vector.tensor_tensor(out1, sn[..., 0], cs[..., 1], ALU.add)

        def residual(l, it, kind):
            dve.wait_ge(S("mixed"), tiles_before(l, it) + 1)
            mix = ps[:, 6 * BANK:8 * BANK]
            nc.vector.tensor_tensor(mix, mix, gate_rows[:, kind * D:(kind + 1) * D], ALU.mult)
            settle()
            nc.vector.tensor_tensor(xt(it), xt(it), mix, ALU.add).then_inc(S("mix_out"), 1)

        def heads(l, it, keys, last_mix=None):
            past = tiles_before(l, it)
            for h in range(HEADS + 1):
                if h == 2 and last_mix:
                    last_mix()
                if h < HEADS:
                    dve.wait_ge(S("scored"), past * HEADS + h + 1)
                    nc.vector.tensor_reduce(hst[:, h:h + 1], scores(h, keys), AX.XY, ALU.max, negate=True)\
                        .then_inc(S("max_ready"), 1)
                if 0 <= h - 1 < HEADS:
                    j = h - 1
                    dve.wait_ge(S("exp_ready"), past * HEADS + j + 1)
                    nc.vector.reciprocal(hinv[:, j:j + 1], hsum[:, j:j + 1])
                    settle()
                    nc.vector.tensor_scalar(pbuf(j, keys), pbuf(j, keys), hinv[:, j:j + 1], None, ALU.mult)\
                        .then_inc(S("p_ready"), 1)

        dve.wait_ge(S("inputs"), 16 * len(inputs))
        row_stats("mix0", 0, NTILE)

        def post_m(t):
            dve.wait_ge(S("proj_squared", 0), t + 1)
            nc.vector.tensor_scalar(pst[:, 2:3], pst[:, 0:1], 1.0 / QL, EPS, ALU.mult, ALU.add)
            nc.vector.tensor_scalar(pst[:, 3:4], pst[:, 1:2], 1.0 / KVL, EPS, ALU.mult, ALU.add).then_inc(S("proj_mean", 0), 1)
            dve.wait_ge(S("proj_root", 0), t + 1)
            nc.vector.reciprocal(pst[:, 6:8], pst[:, 4:6])
            settle()
            if t >= 2:
                dve.wait_ge(S("turned", 0), t)
            j = t if t > 0 else 5
            key = m_key[:, j * KV:(j + 1) * KV]
            nc.vector.tensor_scalar(m_ql[:, (t % 2) * QL:(t % 2 + 1) * QL], bank(2, QL), pst[:, 6:7], None, ALU.mult)
            nc.vector.scalar_tensor_tensor(key[:, 0:KVL], bank(3, KVL), pst[:, 7:8], kvn_row[:], ALU.mult, ALU.mult)
            pe_ = bank(3, ROPE, KVL)
            if t == 0:
                nc.vector.tensor_copy(key[:, KVL:KV], pe_).then_inc(S("proj_out", 0), 1)
            else:
                cs, sn = m_rope[:, 0:ROPE], m_rope[:, ROPE:2 * ROPE]
                at = (t - 1) * ROPE
                nc.vector.tensor_tensor(cs, pe_, const[:, C_CM + at:C_CM + at + ROPE], ALU.mult)
                nc.vector.tensor_tensor(sn, pe_, const[:, C_SM + at:C_SM + at + ROPE], ALU.mult)
                settle()
                out = split(key[:, KVL:KV], ROPE // 2)
                rope(out[..., 0], out[..., 1], split(cs, ROPE // 2), split(sn, ROPE // 2)).then_inc(S("proj_out", 0), 1)
            settle()

        def post_g(t):
            W = NQ + NK
            qk = g_qk[:, (t % 2) * W:(t % 2 + 1) * W]
            heads_ = HEADS + KVH
            dve.wait_ge(S("proj_out", 1), t + 1)
            nc.vector.tensor_tensor(g_a, qk, qk, ALU.mult)
            settle()
            nc.vector.tensor_reduce(pst[:, 0:20], split(g_a, heads_), AX.X, ALU.add)
            settle()
            nc.vector.tensor_scalar(pst[:, 20:40], pst[:, 0:20], 1.0 / HD, EPS, ALU.mult, ALU.add).then_inc(S("proj_mean", 1), 1)
            dve.wait_ge(S("proj_root", 1), t + 1)
            nc.vector.reciprocal(pst[:, 0:20], pst[:, 40:60])
            settle()
            nc.vector.tensor_tensor(split(qk, heads_), split(qk, heads_), blast(pst[:, 0:20], HD), ALU.mult)
            settle()
            nc.vector.tensor_tensor(split(qk[:, 0:NQ], HEADS), split(qk[:, 0:NQ], HEADS), bmid(qkn_row[:, 0:HD], HEADS), ALU.mult)
            last = nc.vector.tensor_tensor(split(qk[:, NQ:W], KVH), split(qk[:, NQ:W], KVH), bmid(qkn_row[:, HD:2 * HD], KVH),
                                           ALU.mult)
            if t > 0:
                at = (t - 1) * HD
                settle()
                nc.vector.tensor_tensor(split(g_a, heads_), split(qk, heads_), bmid(const[:, C_CG + at:C_CG + at + HD], heads_), ALU.mult)
                nc.vector.tensor_tensor(split(g_b, heads_), split(qk, heads_), bmid(const[:, C_SG + at:C_SG + at + HD], heads_), ALU.mult)
                settle()
                out = split(qk, W // 2)
                last = rope(out[..., 0], out[..., 1], split(g_a, W // 2), split(g_b, W // 2))
            last.then_inc(S("qk_ready"), 1)
            settle()

        def projection(l, post):
            norm(l, 0)
            norm(l, 1)
            if l == 0:
                modulation(0, 0)
            mod_cols(l, 0)
            modulation(l, 1)
            for t in range(NTILE):
                if t + 2 < NTILE:
                    norm(l, t + 2)
                if t + 1 < NTILE:
                    mod_cols(l, t + 1)
                post(t)

        projection(0, post_m)
        dve.wait_ge(S("state_stored", 0), 16)
        for m in range(HEADS // 2):
            dve.wait_ge(S("k_made"), m + 1)
            nc.vector.tensor_copy(m_kT[0:64, (2 * m + 1) * KEYS:(2 * m + 2) * KEYS], spair(m, KEYS)[64:128]).then_inc(S("k_odd"), 1)
        for j in range(1, NKEYT, 2):
            dve.wait_ge(S("v_made"), j + 1)
            nc.vector.tensor_copy(m_V[:, j * D:(j + 1) * D], ps[:, 6 * BANK:8 * BANK]).then_inc(S("v_odd"), 1)
        dve.wait_ge(S("gates_a", 0), 32)
        dve.wait_ge(S("rope_keys"), 1)

        def q_stage(it):
            if not isinstance(it, int) or it:
                dve.wait_ge(S("q_out"), it + 1)
                pe_ = split(q_tok, HEADS)[:, :, NOPE:QD]
                cos = const[:, ds(it * ROPE + (C_CM - ROPE), ROPE)]
                sin = const[:, ds(it * ROPE + (C_SM - ROPE), ROPE)]
                nc.vector.tensor_tensor(split(q_cos, HEADS), pe_, bmid(cos, HEADS), ALU.mult)
                nc.vector.tensor_tensor(split(q_sin, HEADS), pe_, bmid(sin, HEADS), ALU.mult)
                settle()
                out = pe_.rearrange("p h (r two) -> p h r two", two=2)
                cs = q_cos.rearrange("p (h r two) -> p h r two", h=HEADS, two=2)
                sn = q_sin.rearrange("p (h r two) -> p h r two", h=HEADS, two=2)
                rope(out[..., 0], out[..., 1], cs, sn).then_inc(S("q_roped"), 1)
            dve.wait_ge(S("q_turned"), it + 1)
            nc.vector.tensor_copy(qT[0:QD, D:2 * D], ps[0:QD, D:2 * D]).then_inc(S("q_ready", 0), 1)

        def attend(l, stage):
            stage(0)
            heads(l, 0, P)
            stage(1)
            heads(l, 1, LKEYS, lambda: residual(l, 0, 0))
            with dve.Fori(1, LAT) as i:
                stage(i + 1)
                heads(l, i + 1, LKEYS, lambda: residual(l, i, 1))

        attend(0, q_stage)

        def routing(l):
            r4 = const[:, C_R4:C_R4 + NG]
            n = [R_FREE]

            def new(cols):
                n[0] += cols
                return e_r[:, n[0] - cols:n[0]]

            def op(ins):
                settle()
                return ins

            T5 = NTILE
            lg, le = new(T5 * NG), new(T5 * NE)
            sc4, t80, ein, e2 = new(T5 * NG), new(T5 * NE), new(T5 * EPG), new(T5 * EPG)
            gm, m1, m2, mx = new(T5), new(T5), new(T5), new(T5)
            og, o1, o2 = new(T5 * NG), new(T5 * EPG), new(T5 * EPG)
            M1, M2, M, before = new(T5 * NE), new(T5 * NE), new(T5 * NE), new(T5 * NE)
            den, gw = new(T5), new(T5)
            nt, cs, c2 = new(NE), new(NE), new(NE)
            te, te1 = new(SLOT_TILES * NE), new(SLOT_TILES)
            place_ = new(2 * T5)
            over = new(T5 * NE)
            need, rnd = new(ROUNDS), new(1)
            assert n[0] <= 1600, n[0]
            sh, ex = e_r[:, R_SH:R_SH + T5 * (NG + 1)], e_r[:, R_EX:R_EX + T5 * (NG + 1)]
            dve.wait_ge(S("logits", l), T5)
            lo = split(bank(2, T5 * 32), T5)
            nc.vector.tensor_tensor(split(lg, T5), lo[:, :, 0:NG], bmid(rbias[:, l * NR:l * NR + NG], T5), ALU.add)
            op(nc.vector.tensor_tensor(split(le, T5), lo[:, :, NG:NR], bmid(rbias[:, l * NR + NG:(l + 1) * NR], T5), ALU.add))

            def first_max(oh, v, m):
                op(nc.vector.tensor_reduce(m, split(v, T5), AX.X, ALU.max))
                op(nc.vector.tensor_tensor(split(sc4, T5), split(v, T5), blast(m, NG), ALU.is_equal))
                op(nc.vector.tensor_tensor(split(sc4, T5), split(sc4, T5), bmid(r4, T5), ALU.mult))
                op(nc.vector.tensor_reduce(mx, split(sc4, T5), AX.X, ALU.max))
                op(nc.vector.tensor_tensor(split(oh, T5), split(sc4, T5), blast(mx, NG), ALU.is_equal))

            first_max(og, lg, gm)
            nc.vector.tensor_tensor(split(sh[:, 0:T5 * NG], T5), split(lg, T5), blast(gm, NG), ALU.subtract)
            op(nc.vector.tensor_tensor(t80.rearrange("p (x j) -> p x j", j=EPG), le.rearrange("p (x j) -> p x j", j=EPG),
                                       blast(og, EPG), ALU.mult))
            op(nc.vector.tensor_reduce(split(ein, T5), t80.rearrange("p (t g j) -> p t j g", t=T5, g=NG), AX.X, ALU.add))
            first_max(o1, ein, m1)
            op(nc.vector.scalar_tensor_tensor(e2, o1, MASKED, ein, ALU.mult, ALU.add))
            first_max(o2, e2, m2)
            nc.vector.tensor_tensor(sh[:, T5 * NG:], m2, m1, ALU.subtract).then_inc(S("shifted", l), 1)
            for oh, m in ((o1, M1), (o2, M2)):
                for g in range(NG):
                    nc.vector.tensor_tensor(m.rearrange("p (t g j) -> p t g j", t=T5, g=NG)[:, :, g], split(oh, T5),
                                            blast(split(og, T5)[:, :, g], EPG), ALU.mult)
            settle()
            nc.vector.tensor_tensor(M, M1, M2, ALU.add)
            nc.vector.tensor_tensor(before[:, 0:NE], M1[:, 0:NE], M2[:, 0:NE], ALU.add)
            for t in range(1, T5):
                settle()
                last = nc.vector.tensor_tensor(before[:, t * NE:(t + 1) * NE], before[:, (t - 1) * NE:t * NE],
                                               M[:, t * NE:(t + 1) * NE], ALU.add)
            last.then_inc(S("picked", l), 1)
            dve.wait_ge(S("ranked", l), 1)
            op(nc.vector.tensor_tensor(split(over, NE), blast(bank(3, NE, T5 * NE), T5), bmid(const[:, C_OV:C_OV + T5], NE), ALU.is_gt))
            op(nc.vector.tensor_reduce(nt, split(over, NE), AX.X, ALU.add))
            src = nt
            for k, dst in ((1, cs), (2, c2), (4, cs), (8, c2)):
                nc.vector.tensor_copy(dst[:, 0:k], src[:, 0:k])
                op(nc.vector.tensor_tensor(dst[:, k:NE], src[:, k:NE], src[:, 0:NE - k], ALU.add))
                src = dst
            nc.vector.tensor_tensor(split(te, SLOT_TILES), blast(const[:, C_TI:C_TI + SLOT_TILES], NE), bmid(c2, SLOT_TILES),
                                    ALU.is_ge)
            op(nc.vector.tensor_tensor(cs, c2, nt, ALU.subtract))
            nc.vector.tensor_scalar(need, const[:, C_RND:C_RND + ROUNDS], c2[:, NE - 1:NE], None, ALU.is_lt)
            nc.vector.tensor_reduce(te1, split(te, SLOT_TILES), AX.X, ALU.add)
            op(nc.vector.tensor_scalar(cs, cs, float(P), None, ALU.mult))
            op(nc.vector.tensor_tensor(split(t80, T5), split(bank(3, T5 * NE), T5), bmid(cs, T5), ALU.add))
            op(nc.vector.tensor_tensor(M1, M1, t80, ALU.mult))
            nc.vector.tensor_tensor(M2, M2, t80, ALU.mult)
            sl = place_.rearrange("p (t c) -> p c t", c=2)
            settle()
            nc.vector.tensor_reduce(sl[:, 0], split(M1, T5), AX.X, ALU.add)
            nc.vector.tensor_reduce(sl[:, 1], split(M2, T5), AX.X, ALU.add)
            nc.vector.tensor_reduce(rnd, need, AX.X, ALU.add)
            op(nc.vector.tensor_scalar(te1, te1, float(NE - 1), None, ALU.min))
            nc.vector.tensor_copy(slot_i[:], place_)
            nc.vector.tensor_copy(rounds[:, 0:1], rnd)
            nc.vector.tensor_scalar(rounds[:, 1:2], rnd, 2.0, -1.0, ALU.mult, ALU.add)
            nc.vector.tensor_copy(expert[:], te1).then_inc(S("routed", l), 1)
            dve.wait_ge(S("r_exp", l), 1)
            op(nc.vector.tensor_reduce(den, split(ex[:, 0:T5 * NG], T5), AX.X, ALU.add))
            op(nc.vector.scalar_tensor_tensor(den, ex[:, T5 * NG:], 1.0, den, ALU.add, ALU.mult))
            op(nc.vector.reciprocal(w_pair[:, 0:T5], den))
            op(nc.vector.tensor_tensor(w_pair[:, T5:], w_pair[:, 0:T5], ex[:, T5 * NG:], ALU.mult)).then_inc(S("weighted"), 1)
            settle()

        def experts(l):
            row_stats(f"ffn{l}", 0, LAT)
            dve.wait_ge(S("rows_e", l), 16 * 4)
            dve.wait_ge(S("pv_done"), tiles_before(l, NTILE) * HEADS)
            for t in range(NTILE):
                if t == LAT:
                    residual(l, LAT, 1)
                    row_stats(f"ffn{l}", LAT, NTILE, 1)
                v = 0 if t == 0 else 1
                h = e_h[:, t * D:(t + 1) * D]
                nc.vector.scalar_tensor_tensor(h, xt(t), rstd[:, t:t + 1], e_row[:, 2 * v * D:(2 * v + 1) * D], ALU.mult, ALU.mult)
                settle()
                nc.vector.tensor_tensor(h, h, e_row[:, (2 * v + 1) * D:(2 * v + 2) * D], ALU.add).then_inc(S("h_ready", l), 1)
            routing(l)
            modulation(l, 2)
            if l == 0:
                modulation(1, 0)

            def xsT(t, u):
                dve.wait_ge(S("xs_used", l), t + 1)
                nc.vector.tensor_copy(e_xsT[:, (u % 2) * D:(u % 2 + 1) * D], ps[:, 0:D]).then_inc(S("xsT_ready", l), 1)

            def hid(t, u):
                dve.wait_ge(S("sil_ready", l), t + 1)
                c = slice((u % 2) * FF, (u % 2 + 1) * FF)
                nc.vector.tensor_tensor(e_hid[:, c], bank(2 + u % 2, FF, FF), e_sil[:, c], ALU.mult).then_inc(S("hid_ready", l), 1)

            def hidT(t, u):
                dve.wait_ge(S("hid_turned", l), t + 1)
                nc.vector.tensor_copy(e_hidT[:, (u % 2) * FF:(u % 2 + 1) * FF], bank(4, FF)).then_inc(S("hidT_ready", l), 1)

            xsT(0, 0)
            hid(0, 0)
            xsT(1, 1)
            R = rounds_needed(dve, l)
            with dve.Fori(0, ROUNDS) as i:
                with dve.If(i < R):
                    for u in range(2):
                        hidT(i * 2 + u, u)
                        xsT(i * 2 + (u + 2), u)
                        hid(i * 2 + (u + 1), u + 1)
            for k in range(SLOT_TILES - LOOPED):
                hidT(R * 2 + k, k)
                if k + 2 < SLOT_TILES - LOOPED:
                    xsT(R * 2 + (k + 2), k)
                if k + 1 < SLOT_TILES - LOOPED:
                    hid(R * 2 + (k + 1), k + 1)
        def combine(l, t):
            if t == 0:
                dve.wait_ge(S("gates_m", l), 32)
            dve.wait_ge(S("scaled"), NTILE * l + t + 1)
            a, b = e_g[t % 4][:, 0:D], e_g[t % 4][:, D:2 * D]
            v = 0 if t == 0 else 1
            nc.vector.scalar_tensor_tensor(a, b, w_pair[:, NTILE + t:NTILE + t + 1], a, ALU.mult, ALU.add)
            settle()
            nc.vector.tensor_tensor(a, a, gate_rows[:, v * D:(v + 1) * D], ALU.mult)
            settle()
            nc.vector.tensor_tensor(xt(t), xt(t), a, ALU.add).then_inc(S("combined", l), 1)

        def final(t):
            row_stats("end", t, t + 1, t)
            nc.vector.scalar_tensor_tensor(e_h[:, t * D:(t + 1) * D], xt(t), rstd[:, t:t + 1], e_row[:, 0:D], ALU.mult, ALU.mult)\
                .then_inc(S("y_ready"), 1)

        experts(0)
        for t in range(NTILE):
            combine(0, t)
        row_stats("mix1", 0, NTILE)
        projection(1, post_g)
        dve.wait_ge(S("gates_a", 1), 32)
        attend(1, lambda it: None)
        experts(1)
        dve.wait_ge(S("final_landed"), 16)
        combine(1, 0)
        for t in range(NTILE):
            if t + 1 < NTILE:
                combine(1, t + 1)
            final(t)

    @block.tensor
    def _(pe):
        mm = nc.tensor.matmul

        def turn(out, in_, rows=P):
            return nc.tensor.transpose(out, in_, ident[0:rows, 0:rows])

        pe.wait_ge(S("first_inputs"), 16 * len(first_inputs))
        turn(bank(7, VB_END), vecb[0:VB_END, :], VB_END).then_inc(S("cols_turned"), 1)

        def ada(items):
            c = cond[:].rearrange("p (v k) -> p k v", v=2)
            for l, n in items:
                wait_landed(pe, ("ada", l, n))
                if ADA_ITEMS * l + n >= 2:
                    pe.wait_ge(S("ada_out"), ADA_ITEMS * l + n - 1)
                w = split(slot_of(("ada", l, n), SLOT), KD)
                for k in range(KD):
                    last = mm(bank(4 + n % 2)[0:2, :], c[:, k], w[:, k], start=k == 0, stop=k == KD - 1)
                last.then_inc(S("ada_made"), 1)

        def turn_mods(l):
            pe.wait_ge(S("mod_ready"), 3 * l + 1)
            turn(bank(6, 2 * MODV), modt[0:2 * MODV, :], 2 * MODV).then_inc(S("mod_turned"), 1)

        def turn_tile(l, t):
            pe.wait_ge(S("xn_ready", l), t + 1)
            if t:
                pe.wait_ge(S("hT_ready", l), t)
            for k in range(KD):
                last = turn(ps[:, k * P:(k + 1) * P], xn[l](t)[:, k * P:(k + 1) * P])
            last.then_inc(S("n_turned", l), 1)

        def project(l, t, parts, out_sem):
            pe.wait_ge(S("hT_ready", l), t + 1)
            if t:
                pe.wait_ge(out_sem, t)
            for b, (name, cols) in enumerate(parts):
                if t == 0:
                    wait_landed(pe, (name, l, 0))
                w = split(slot_of((name, l, 0), KD * cols), KD)
                for k in range(KD):
                    last = mm(bank(2 + b, cols), hT[l](t)[:, k * P:(k + 1) * P], w[:, k], start=k == 0, stop=k == KD - 1)
            last.then_inc(S("projected", l), 1)

        def mix(l, it, half):
            name = (MATRICES[l][-2 + half], l, 0)
            w = split(slot_of(name, SLOT), KD)
            for k in range(KD):
                last = mm(bank(6 + half), oT[:, k * P:(k + 1) * P], w[:, k], start=k == 0, stop=k == KD - 1)
            if half:
                last.then_inc(S("mixed"), 1)

        def heads(l, it, keys, score_of, v_of, last_mix=None):
            past = tiles_before(l, it)
            g = past * HEADS
            first = 5 if keys == P else 0
            w = keys // 2 if keys > P else keys
            for n in range(HEADS + 3):
                if n == 2 and last_mix:
                    last_mix()
                if n < HEADS:
                    if n >= 2:
                        pe.wait_ge(S("exp_ready"), g + n - 1)
                    q, k = score_of(n)
                    for c in range(keys // w):
                        at = first * P + c * w
                        last = mm(scores(n, keys)[:, c], q, k[:, at:at + w], start=True, stop=True)
                    last.then_inc(S("scored"), 1)
                if 0 <= n - 2 < HEADS:
                    h = n - 2
                    pe.wait_ge(S("p_ready"), g + h + 1)
                    if h:
                        pe.wait_ge(S("pt_ready"), g + h)
                    for j in range(keys // P):
                        last = turn(ps[:, 4 * BANK + j * P:4 * BANK + (j + 1) * P], pbuf(h, keys)[:, j * P:(j + 1) * P])
                    last.then_inc(S("p_turned"), 1)
                if n >= 3:
                    h = n - 3
                    pe.wait_ge(S("pt_ready"), g + h + 1)
                    if h == 0 and not (isinstance(past, int) and past == 0):
                        pe.wait_ge(S("mix_out"), past)
                    for j in range(keys // P):
                        last = mm(oT_block(h), v_of(h, first + j), ptbuf(h, keys)[:, j * P:(j + 1) * P],
                                  start=j == 0, stop=j == keys // P - 1)
                    last.then_inc(S("pv_done"), 1)

        def attend(l, make_q, turn_q, score_of, v_of):
            def tile(it, keys, last, more):
                heads(l, it, keys, score_of, v_of, last)
                if more:
                    make_q(it + 1)
                pe.wait_ge(S("oT_ready"), tiles_before(l, it) * 2 + 2)
                mix(l, it, 0)
                if more:
                    turn_q(it + 1)

            for half in range(2):
                wait_landed(pe, (MATRICES[l][-2 + half], l, 0))
            make_q(0)
            turn_q(0)
            tile(0, P, None, True)
            tile(1, LKEYS, lambda: mix(l, 0, 1), True)
            with pe.Fori(1, LAT - 1) as i:
                tile(i + 1, LKEYS, lambda: mix(l, i, 1), True)
            if l == 0:
                used(2)
            tile(LAT, LKEYS, lambda: mix(l, LAT - 1, 1), False)
            mix(l, LAT, 1)

        def used(n):
            pe.drain().then_inc(S("ring_used"), n)

        pe.wait_ge(S("cond_ready"), 1)
        ada(ada_first[0][:7])
        turn_mods(0)
        ada(ada_first[0][7:])

        def turn_keys_m(t):
            j = t if t > 0 else 5 if t == 0 else 0
            if t >= 0:
                pe.wait_ge(S("proj_out", 0), t + 1)
                pe.wait_ge(S("turned_out", 0), t + 1)
                for m in range(3):
                    turn(bank(4, P, m * P), m_ql[:, (t % 2) * QL + m * P:(t % 2) * QL + (m + 1) * P])
            key = m_key[:, j * KV:(j + 1) * KV]
            for m in range(2):
                turn(bank(5, P, m * P), key[:, m * P:(m + 1) * P])
            turn(ps[0:ROPE, 5 * BANK + 2 * P:5 * BANK + 3 * P], key[:, KVL:KV]).then_inc(S("turned", 0), 1)

        def turn_keys_g(t):
            W = NQ + NK
            if t >= 0:
                pe.wait_ge(S("qk_ready"), t + 1)
                pe.wait_ge(S("turned_out", 1), t + 1)
                for m in range(8):
                    turn(ps[:, 5 * BANK + m * P:5 * BANK + (m + 1) * P], g_qk[:, (t % 2) * W + m * P:(t % 2) * W + (m + 1) * P])
                k = g_qk[:, (t % 2) * W + NQ:(t % 2 + 1) * W]
            else:
                pe.wait_ge(S("cache_landed"), 32)
                k = g_cache
            for h in range(KVH):
                last = turn(ps[0:HD, 7 * BANK + h * P:7 * BANK + (h + 1) * P], k[:, h * HD:(h + 1) * HD])
            last.then_inc(S("turned", 1), 1)

        def projection(l, parts, turn_keys, out_sem):
            turn_tile(l, 0)
            pe.wait_ge(S("ada_out"), ADA_ITEMS * l + PART_ENDS[1])
            turn_keys(-1)
            for t in range(NTILE):
                if t + 1 < NTILE:
                    turn_tile(l, t + 1)
                project(l, t, parts, out_sem)
                if t == NTILE - 1:
                    used(len(parts))
                if t:
                    turn_keys(t - 1)
            turn_keys(NTILE - 1)

        projection(0, (("dq", QL), ("dkv", KV)), turn_keys_m, S("proj_out", 0))
        wait_landed(pe, ("uk", 0, 0))
        pe.wait_ge(S("turned_out", 0), NKEYT)
        w = split(slot_of(("uk", 0, 0), 2 * D), 2)
        for m in range(HEADS // 2):
            if m >= 2:
                pe.wait_ge(S("k_even"), m - 1)
                pe.wait_ge(S("k_odd"), m - 1)
            for c, n in ((0, BANK), (BANK, KEYS - BANK)):
                for k in range(2):
                    last = mm(spair(m, KEYS)[:, c:c + n], w[:, k, m * P:(m + 1) * P], m_ckvT[:, k * KEYS + c:k * KEYS + c + n],
                              start=k == 0, stop=k == 1)
            last.then_inc(S("k_made"), 1)
        used(1)
        wait_landed(pe, ("uv", 0, 0))
        pe.wait_ge(S("mod_cols"), 1)
        w = split(slot_of(("uv", 0, 0), 2 * D), 2)
        for j in range(NKEYT):
            if j >= 2:
                pe.wait_ge(S("v_odd" if j % 2 else "v_even"), j // 2)
            for n in range(2):
                for k in range(2):
                    last = mm(bank(4 + 2 * (j % 2) + n), m_ckvT[:, k * KEYS + j * P:k * KEYS + (j + 1) * P],
                              w[:, k, n * BANK:(n + 1) * BANK], start=k == 0, stop=k == 1)
            last.then_inc(S("v_made"), 1)
        used(1)
        pe.wait_ge(S("k_even"), HEADS // 2)
        pe.wait_ge(S("k_odd"), HEADS // 2)
        pe.wait_ge(S("v_even"), NKEYT // 2)
        pe.wait_ge(S("v_odd"), NKEYT // 2)
        pe.wait_ge(S("rope_keys"), 1)
        for n in range(2):
            wait_landed(pe, (f"uq{n}", 0, 0))

        def make_q(it):
            pe.wait_ge(S("ql_ready"), it + 1)
            for b in range(4):
                w = split(slot_of((f"uq{b // 2}", 0, 0), 3 * 768), 3)
                for k in range(3):
                    last = mm(bank(b, 4 * QD), qls[:, k * P:(k + 1) * P], w[:, k, (b % 2) * 4 * QD:(b % 2 + 1) * 4 * QD],
                              start=k == 0, stop=k == 2)
            last.then_inc(S("q_made"), 1)

        def turn_q(it):
            pe.wait_ge(S("q_out"), it + 1)
            if not isinstance(it, int) or it:
                pe.wait_ge(S("q_roped"), it)
            for h in range(HEADS):
                last = turn(ps[0:QD, h * P:(h + 1) * P], q_tok[:, h * QD:(h + 1) * QD])
            last.then_inc(S("q_turned"), 1)
            pe.wait_ge(S("q_ready", 0), it * 2 + 2)

        attend(0, make_q, turn_q, lambda h: (qT[0:QD, h * P:(h + 1) * P], m_kT[0:QD, h * KEYS:(h + 1) * KEYS]),
               lambda h, j: m_V[:, j * D + h * VD:j * D + (h + 1) * VD])
        used(2)

        def experts(l):
            def turn_h(t):
                pe.wait_ge(S("h_ready", l), t + 1)
                if t:
                    pe.wait_ge(S("hT_out", l), t)
                for k in range(KD):
                    last = turn(ps[:, k * P:(k + 1) * P], e_h[:, t * D + k * P:t * D + (k + 1) * P])
                last.then_inc(S("h_turned", l), 1)

            turn_h(0)
            pe.wait_ge(S("router_landed", l), 32)
            for t in range(NTILE):
                if t + 1 < NTILE:
                    turn_h(t + 1)
                pe.wait_ge(S("hT_out", l), t + 1)
                for k in range(KD):
                    last = mm(bank(2, NR, t * 32), e_hT[:, (t % 2) * D + k * P:(t % 2) * D + (k + 1) * P], rw[:, k * NR:(k + 1) * NR],
                              start=k == 0, stop=k == KD - 1)
                last.then_inc(S("logits", l), 1)
            ada(ada_ranks[l])
            pe.wait_ge(S("picked", l), 1)
            M = e_r[:, R_M:R_M + NTILE * NE]
            before = e_r[:, R_M + NTILE * NE:R_M + 2 * NTILE * NE]
            mm(bank(3, NTILE * NE), tri, M, start=True, stop=False)
            mm(bank(3, LAT * NE, NE), ones, before[:, 0:LAT * NE], start=False, stop=True)
            mm(bank(3, NE, NTILE * NE), ones, before[:, LAT * NE:], start=True, stop=True).then_inc(S("ranked", l), 1)
            ada(ada_routing[l])
            if l == 0:
                turn_mods(1)
            R = rounds_needed(pe, l)

            def turn_rows(t, u, r):
                pe.wait_ge(S(f"xs_landed{u % 2}", l), r * 16 + 16)
                for k in range(KD):
                    last = turn(ps[:, k * P:(k + 1) * P], e_xs[:, (u % 2) * D + k * P:(u % 2) * D + (k + 1) * P])
                last.then_inc(S("xs_used", l), 1)

            def gate_up(t, u, more=0, less=0):
                pe.wait_ge(S("xsT_ready", l), t + 1)
                wait_landed(pe, ("gu", l, u), more, less)
                w = split(slot_of(("gu", l, u), SLOT), KD)
                for k in range(KD):
                    last = mm(bank(2 + u % 2), e_xsT[:, (u % 2) * D + k * P:(u % 2) * D + (k + 1) * P], w[:, k],
                              start=k == 0, stop=k == KD - 1)
                last.then_inc(S("gu_done", l), 1)

            def turn_hid(t, u):
                pe.wait_ge(S("hid_ready", l), t + 1)
                for k in range(2):
                    last = turn(bank(4, P, k * P), e_hid[:, (u % 2) * FF + k * P:(u % 2) * FF + (k + 1) * P])
                last.then_inc(S("hid_turned", l), 1)

            def down(t, u, more=0, less=0):
                pe.wait_ge(S("hidT_ready", l), t + 1)
                pe.wait_ge(S("y_out", l), t + 1)
                wait_landed(pe, ("dn", l, u), more, less)
                w = split(slot_of(("dn", l, u), 2 * D), 2)
                for n in range(2):
                    for k in range(2):
                        last = mm(bank(6 + n), e_hidT[:, (u % 2) * FF + k * P:(u % 2) * FF + (k + 1) * P],
                                  w[:, k, n * BANK:(n + 1) * BANK], start=k == 0, stop=k == 1)
                last.then_inc(S("y_done", l), 1)

            turn_rows(0, 0, 0)
            gate_up(0, 0)
            turn_rows(1, 1, 0)
            with pe.Fori(0, ROUNDS) as i:
                with pe.If(i < R):
                    for u in range(2):
                        turn_hid(i * 2 + u, u)
                        gate_up(i * 2 + (u + 1), u + 1, i * 32)
                        turn_rows(i * 2 + (u + 2), u, i + 1)
                        down(i * 2 + u, u, i * 32)
            for u in range(LOOPED, SLOT_TILES):
                k = u - LOOPED
                turn_hid(R * 2 + k, u)
                if u + 1 < SLOT_TILES:
                    gate_up(R * 2 + (k + 1), u + 1, R * 32, ROUNDS * 32)
                if u + 2 < SLOT_TILES:
                    turn_rows(R * 2 + (k + 2), u, R + (k // 2 + 1))
                down(R * 2 + k, u, R * 32, ROUNDS * 32)

        experts(0)
        ada(ada_first[1])
        projection(1, (("qkv0", BANK), ("qkv1", BANK), ("qkv2", BANK)), turn_keys_g, S("proj_out", 1))
        pe.wait_ge(S("turned_out", 1), NKEYT)

        def score_g(h):
            half = slice(64 * (h % 2), 64 * (h % 2) + 64)
            return qT[half, (h // 2) * P:(h // 2 + 1) * P], g_kT[half, (h // 4) * KEYS:(h // 4 + 1) * KEYS]

        attend(1, lambda it: None, lambda it: pe.wait_ge(S("q_ready", 1), it + 1), score_g,
               lambda h, j: g_V[:, j * NK + (h // 4) * HD:j * NK + (h // 4 + 1) * HD])
        used(2)
        experts(1)


def constants():
    c = np.zeros((P, C_END), np.float32)
    c[:, C_ID:C_ID + P] = np.eye(P)
    c[:, C_ONE:C_ONE + P] = 1.0
    c[:, C_TRI:C_TRI + P] = np.triu(np.ones((P, P)), 1)
    t = np.arange(LAT * P)
    row, col = (t // GRID_W).astype(np.float32), (t % GRID_W).astype(np.float32)
    for dim, at_c, at_s in ((ROPE, C_CM, C_SM), (HD, C_CG, C_SG)):
        axis = dim // 2
        inv = np.power(np.float32(10000.0), -np.arange(0, axis, 2, dtype=np.float32) / np.float32(axis)).astype(np.float32)
        ang = np.concatenate([row[:, None] * inv, col[:, None] * inv], axis=1)
        for f, at in ((np.cos, at_c), (np.sin, at_s)):
            v = np.repeat(f(ang).astype(np.float32), 2, axis=1).reshape(LAT, P, dim)
            c[:, at:at + LAT * dim] = v.transpose(1, 0, 2).reshape(P, LAT * dim)
    c[:, C_R4:C_R4 + NG] = NG - np.arange(NG)
    c[:, C_TI:C_TI + SLOT_TILES] = np.arange(SLOT_TILES)
    c[:, C_RND:C_RND + ROUNDS] = SLOT_TILES - LOOPED + 2 * np.arange(ROUNDS)
    c[:, C_OV:C_OV + NTILE] = P * np.arange(NTILE)
    return c


def kernel(**inputs):
    import concourse.bacc as bacc
    from concourse.bass_utils import run_bass_kernel_spmd

    a = {n: np.ascontiguousarray(np.asarray(x)) for n, x in inputs.items()}
    small = ("c", "c_ctx", "ada_b", "norm_mix", "norm_ffn", "mla_q_norm")
    lay = {n: x for n, x in a.items() if n not in small}
    one, no = np.ones((KD, P), np.float32), np.zeros((KD, 1), np.float32)
    rows = []
    for l in range(2):
        gain = {1: a["norm_mix"][l].reshape(KD, P), 4: a["norm_ffn"][l].reshape(KD, P)}
        for c in range(6):
            bias = a["ada_b"][l].reshape(6, KD, P)[c]
            rows += [np.concatenate([bias, gain.get(c, one), no + (c in gain)], axis=1)] * 2
    lay["vec_m"] = np.ascontiguousarray(np.concatenate(rows))
    lay["vec_b"] = np.concatenate([a["c_ctx"].reshape(-1, P), a["c"].reshape(-1, P), a["mla_q_norm"].reshape(-1, P)])
    lay["mla_w_uk"] = a["mla_w_uk"].reshape(KVL, HEADS * NOPE)
    lay["mla_w_uv"] = a["mla_w_uv"].reshape(KVL, HEADS * VD)
    lay["const"] = constants()
    nc = bacc.Bacc("TRN2", target_bir_lowering=False, num_devices=1)
    A = {n: nc.dram_tensor(f"in_{n}", x.shape, mybir.dt.from_np(x.dtype), kind="ExternalInput").ap() for n, x in lay.items()}
    shapes = ((1, P, D), (1, LAT * P, D), (1, 1, P, KV), (1, 1, P, 2, KVH, HD))
    O = [nc.dram_tensor(f"out_{i}", s, F32, kind="ExternalOutput").ap() for i, s in enumerate(shapes)]
    with ExitStack() as ctx:
        program(nc, ctx, A, O)
    r = run_bass_kernel_spmd(nc, [{f"in_{n}": x for n, x in lay.items()}], core_ids=[0])
    return tuple(r.results[0][f"out_{i}"] for i in range(len(shapes)))
```
